# Optimizing a Trainium2 kernel written in Bass

```python
import math
import jax
import jax.numpy as jnp
from jax import lax
import numpy as np

D_MODEL = 1024
BATCH = 1
SEQ = 256
DEPTH = 2

CHUNK = 64
Q_BLOCK = 128
RMS_EPS = 1e-6
SUBLN_EPS = 1e-5
D_MIX = D_MODEL
D_FF = 4 * D_MODEL
DA_WIDTH = D_MIX // 4
DA_V = 64
DA_HEADS = DA_WIDTH // DA_V
DA_QK = DA_V // 2
MLA_WIDTH = D_MIX // 4
MLA_V = 64
MLA_HEADS = MLA_WIDTH // MLA_V
MLA_NOPE = 64
MLA_ROPE = 32
MLA_Q_LORA = D_MODEL // 4
MLA_KV_LORA = D_MODEL // 8
ROPE_THETA = 10000.0
SSM_WIDTH = D_MIX - DA_WIDTH - MLA_WIDTH
SSM_HEAD_DIM = 64
SSM_HEADS = SSM_WIDTH // SSM_HEAD_DIM
SSM_GROUPS = 2
SSM_STATE = 64
CONV_WIDTH = 4
CONV_CH = SSM_WIDTH + 2 * SSM_GROUPS * SSM_STATE
IN_SIZES = (DA_WIDTH, DA_WIDTH, DA_WIDTH, MLA_Q_LORA, MLA_KV_LORA, MLA_ROPE, SSM_WIDTH, CONV_CH, SSM_HEADS)
D_IN = sum(IN_SIZES)


def _rmsnorm(t, g, eps=RMS_EPS):
    tf = t.astype(jnp.float32)
    tf = tf * lax.rsqrt(jnp.mean(tf * tf, axis=-1, keepdims=True) + eps)
    return (tf * g.astype(jnp.float32)).astype(t.dtype)

def _rope_tables(positions):
    inv_freq = 1.0 / (ROPE_THETA ** (jnp.arange(0, MLA_ROPE, 2, dtype=jnp.float32) / MLA_ROPE))
    ang = positions.astype(jnp.float32)[..., None] * inv_freq
    return jnp.cos(ang), jnp.sin(ang)

def _apply_rope(t, cos, sin):
    tf = t.astype(jnp.float32)
    t1, t2 = jnp.split(tf, 2, axis=-1)
    return jnp.concatenate([t1 * cos - t2 * sin, t1 * sin + t2 * cos], axis=-1).astype(t.dtype)

def _to_blocks(t):
    b, s = t.shape[0], t.shape[1]
    return jnp.moveaxis(t.reshape((b, s // Q_BLOCK, Q_BLOCK) + t.shape[2:]), 1, 0)

def _from_blocks(o):
    nb, b, qb = o.shape[0], o.shape[1], o.shape[2]
    return jnp.moveaxis(o, 0, 1).reshape((b, nb * qb) + o.shape[3:])

def _chunk_mask(q_start, seq):
    q_chunk = (q_start + jnp.arange(Q_BLOCK)) // CHUNK
    k_chunk = jnp.arange(seq) // CHUNK
    return k_chunk[None, :] <= q_chunk[:, None]

def _masked_softmax(s, mask):
    return jax.nn.softmax(jnp.where(mask, s, -jnp.inf), axis=-1)

def _diff_attention(q, k, v, lam, subln_g, lambda_init):
    b, s, _ = q.shape
    q = q.reshape(b, s, DA_HEADS, 2, DA_QK)
    k = k.reshape(b, s, DA_HEADS, 2, DA_QK)
    v = v.reshape(b, s, DA_HEADS, DA_V)
    k1, k2 = k[..., 0, :], k[..., 1, :]
    scale = DA_QK ** -0.5

    def block(args):
        start, q1b, q2b = args
        mask = _chunk_mask(start, s)
        s1 = jnp.einsum('bqhd,bkhd->bhqk', q1b, k1).astype(jnp.float32) * scale
        s2 = jnp.einsum('bqhd,bkhd->bhqk', q2b, k2).astype(jnp.float32) * scale
        p = _masked_softmax(s1, mask) - lam * _masked_softmax(s2, mask)
        return jnp.einsum('bhqk,bkhe->bqhe', p.astype(v.dtype), v)

    starts = jnp.arange(s // Q_BLOCK) * Q_BLOCK
    o = _from_blocks(lax.map(block, (starts, _to_blocks(q[..., 0, :]), _to_blocks(q[..., 1, :]))))
    o = _rmsnorm(o, subln_g, SUBLN_EPS) * (1.0 - lambda_init)
    return o.reshape(b, s, DA_WIDTH)

def _mla(cq, ckv, kr, cos, sin, q_norm_g, w_uq, kv_norm_g, w_ukv):
    b, s, _ = cq.shape
    q = (_rmsnorm(cq, q_norm_g) @ w_uq).reshape(b, s, MLA_HEADS, MLA_NOPE + MLA_ROPE)
    qn = q[..., :MLA_NOPE]
    qr = _apply_rope(q[..., MLA_NOPE:], cos[:, :, None, :], sin[:, :, None, :])
    kv = (_rmsnorm(ckv, kv_norm_g) @ w_ukv).reshape(b, s, MLA_HEADS, MLA_NOPE + MLA_V)
    kn, v = kv[..., :MLA_NOPE], kv[..., MLA_NOPE:]
    kr = _apply_rope(kr, cos, sin)
    scale = (MLA_NOPE + MLA_ROPE) ** -0.5

    def block(args):
        start, qnb, qrb = args
        sc = (jnp.einsum('bqhd,bkhd->bhqk', qnb, kn)
              + jnp.einsum('bqhr,bkr->bhqk', qrb, kr)).astype(jnp.float32) * scale
        p = _masked_softmax(sc, _chunk_mask(start, s))
        return jnp.einsum('bhqk,bkhe->bqhe', p.astype(v.dtype), v)

    starts = jnp.arange(s // Q_BLOCK) * Q_BLOCK
    o = _from_blocks(lax.map(block, (starts, _to_blocks(qn), _to_blocks(qr))))
    return o.reshape(b, s, MLA_WIDTH)

def _ssd_scan(xs, dt, a, bm, cm):
    b, l, h, p = xs.shape
    n = bm.shape[-1]
    nc = l // CHUNK
    xd = (xs * dt[..., None]).reshape(b, nc, CHUNK, h, p)
    bc = bm.reshape(b, nc, CHUNK, h, n)
    cc = cm.reshape(b, nc, CHUNK, h, n)
    a_cs = jnp.cumsum(jnp.moveaxis((dt * a).reshape(b, nc, CHUNK, h), 3, 1), axis=-1)
    seg = a_cs[..., :, None] - a_cs[..., None, :]
    causal = jnp.tril(jnp.ones((CHUNK, CHUNK), dtype=bool))
    decay_in = jnp.exp(jnp.where(causal, seg, -jnp.inf))
    scores = jnp.einsum('bclhn,bcshn->bhcls', cc, bc) * decay_in
    y_diag = jnp.einsum('bhcls,bcshp->bclhp', scores, xd)
    decay_to_end = jnp.exp(a_cs[..., -1:] - a_cs)
    chunk_states = jnp.einsum('bclhn,bhcl,bclhp->bchpn', bc, decay_to_end, xd)
    chunk_decay = jnp.exp(a_cs[..., -1])

    def step(state, inp):
        st, dec = inp
        return state * dec[..., None, None] + st, state

    init = jnp.zeros((b, h, p, n), jnp.float32)
    _, prev = lax.scan(step, init, (jnp.moveaxis(chunk_states, 1, 0), jnp.moveaxis(chunk_decay, 2, 0)))
    prev = jnp.moveaxis(prev, 0, 1)
    y_off = jnp.einsum('bclhn,bchpn,bhcl->bclhp', cc, prev, jnp.exp(a_cs))
    return (y_diag + y_off).reshape(b, l, h, p)

def _mamba2(z, xbc, dt_raw, conv_w, conv_b, dt_bias, a_log, d_skip, norm_g):
    b, s, _ = z.shape
    xbc = lax.conv_general_dilated(xbc, conv_w[:, None, :].astype(xbc.dtype), (1,), [(CONV_WIDTH - 1, 0)],
                                   dimension_numbers=('NWC', 'WIO', 'NWC'), feature_group_count=CONV_CH)
    xbc = jax.nn.silu(xbc + conv_b)
    xs, bm, cm = jnp.split(xbc.astype(jnp.float32), [SSM_WIDTH, SSM_WIDTH + SSM_GROUPS * SSM_STATE], axis=-1)
    xs = xs.reshape(b, s, SSM_HEADS, SSM_HEAD_DIM)
    rep = SSM_HEADS // SSM_GROUPS
    bm = jnp.repeat(bm.reshape(b, s, SSM_GROUPS, SSM_STATE), rep, axis=2)
    cm = jnp.repeat(cm.reshape(b, s, SSM_GROUPS, SSM_STATE), rep, axis=2)
    dt = jax.nn.softplus(dt_raw.astype(jnp.float32) + dt_bias.astype(jnp.float32))
    a = -jnp.exp(a_log.astype(jnp.float32))
    y = _ssd_scan(xs, dt, a, bm, cm) + xs * d_skip.astype(jnp.float32)[:, None]
    y = y.reshape(b, s, SSM_WIDTH) * jax.nn.silu(z.astype(jnp.float32))
    y = _rmsnorm(y.reshape(b, s, SSM_GROUPS, SSM_WIDTH // SSM_GROUPS), norm_g.reshape(SSM_GROUPS, -1))
    return y.reshape(b, s, SSM_WIDTH).astype(z.dtype)

def _hybrid_mixer(h, cos, sin, layer, w_in, lam_p, subln_g, q_norm_g, w_uq, kv_norm_g, w_ukv,
                  conv_w, conv_b, dt_bias, a_log, d_skip, ssm_norm_g, w_out):
    proj = h @ w_in
    splits = np.cumsum(IN_SIZES)[:-1].tolist()
    a_q, a_k, a_v, b_cq, b_ckv, b_kr, c_z, c_xbc, c_dt = jnp.split(proj, splits, axis=-1)
    lambda_init = 0.8 - 0.6 * math.exp(-0.3 * layer)
    lp = lam_p.astype(jnp.float32)
    lam = jnp.exp(jnp.sum(lp[0] * lp[1])) - jnp.exp(jnp.sum(lp[2] * lp[3])) + lambda_init
    y_a = _diff_attention(a_q, a_k, a_v, lam, subln_g, lambda_init)
    y_b = _mla(b_cq, b_ckv, b_kr, cos, sin, q_norm_g, w_uq, kv_norm_g, w_ukv)
    y_c = _mamba2(c_z, c_xbc, c_dt, conv_w, conv_b, dt_bias, a_log, d_skip, ssm_norm_g)
    return jnp.concatenate([y_a, y_b, y_c], axis=-1) @ w_out

def _sq_relu_mlp(h, w_up, w_down):
    return jnp.square(jax.nn.relu(h @ w_up)) @ w_down

def first_inputs(seed: int = 0) -> dict:
    key = jax.random.key(seed)
    ks = jax.random.split(key, 24)

    def nrm(k, shape, scale):
        return jax.random.normal(k, shape, jnp.float32) * scale

    x = nrm(ks[0], (BATCH, SEQ, D_MODEL), 1.0)
    c = nrm(ks[1], (BATCH, D_MODEL), 1.0)
    offset = jax.random.randint(ks[2], (BATCH, 1), 0, 4096, dtype=jnp.int32)
    positions = offset + jnp.arange(SEQ, dtype=jnp.int32)[None, :]
    w_ada = nrm(ks[3], (DEPTH, D_MODEL, 6 * D_MODEL), 0.5 * D_MODEL ** -0.5)
    b_ada = nrm(ks[4], (DEPTH, 6 * D_MODEL), 0.02)
    norm_g = 1.0 + nrm(ks[5], (DEPTH, 4, D_MODEL), 0.02)
    w_in = nrm(ks[6], (DEPTH, D_MODEL, D_IN), D_MODEL ** -0.5)
    diff_lambda = nrm(ks[7], (DEPTH, 4, DA_QK), 0.1)
    diff_subln_g = 1.0 + nrm(ks[8], (DEPTH, DA_V), 0.02)
    mla_q_norm_g = 1.0 + nrm(ks[9], (DEPTH, MLA_Q_LORA), 0.02)
    w_uq = nrm(ks[10], (DEPTH, MLA_Q_LORA, MLA_HEADS * (MLA_NOPE + MLA_ROPE)), MLA_Q_LORA ** -0.5)
    mla_kv_norm_g = 1.0 + nrm(ks[11], (DEPTH, MLA_KV_LORA), 0.02)
    w_ukv = nrm(ks[12], (DEPTH, MLA_KV_LORA, MLA_HEADS * (MLA_NOPE + MLA_V)), MLA_KV_LORA ** -0.5)
    conv_w = nrm(ks[13], (DEPTH, CONV_WIDTH, CONV_CH), CONV_WIDTH ** -0.5)
    conv_b = nrm(ks[14], (DEPTH, CONV_CH), 0.02)
    dt0 = jnp.exp(jax.random.uniform(ks[15], (DEPTH, SSM_HEADS), jnp.float32,
                                     math.log(1e-3), math.log(1e-1)))
    dt_bias = dt0 + jnp.log(-jnp.expm1(-dt0))
    a_log = jnp.log(jax.random.uniform(ks[16], (DEPTH, SSM_HEADS), jnp.float32, 1.0, 16.0))
    d_skip = 1.0 + nrm(ks[17], (DEPTH, SSM_HEADS), 0.1)
    ssm_norm_g = 1.0 + nrm(ks[18], (DEPTH, SSM_WIDTH), 0.02)
    w_out = nrm(ks[19], (DEPTH, D_MIX, D_MODEL), D_MIX ** -0.5)
    w_up = nrm(ks[20], (DEPTH, D_MODEL, D_FF), D_MODEL ** -0.5)
    w_down = nrm(ks[21], (DEPTH, D_FF, D_MODEL), D_FF ** -0.5)
    return {'x': x, 'c': c, 'positions': positions, 'w_ada': w_ada, 'b_ada': b_ada, 'norm_g': norm_g,
            'w_in': w_in, 'diff_lambda': diff_lambda, 'diff_subln_g': diff_subln_g,
            'mla_q_norm_g': mla_q_norm_g, 'w_uq': w_uq, 'mla_kv_norm_g': mla_kv_norm_g, 'w_ukv': w_ukv,
            'conv_w': conv_w, 'conv_b': conv_b, 'dt_bias': dt_bias, 'a_log': a_log, 'd_skip': d_skip,
            'ssm_norm_g': ssm_norm_g, 'w_out': w_out, 'w_up': w_up, 'w_down': w_down}

def first_block(x, c, positions, w_ada, b_ada, norm_g, w_in, diff_lambda, diff_subln_g,
              mla_q_norm_g, w_uq, mla_kv_norm_g, w_ukv, conv_w, conv_b, dt_bias, a_log, d_skip,
              ssm_norm_g, w_out, w_up, w_down):
    cos, sin = _rope_tables(positions)
    cond = jax.nn.silu(c)
    for l in range(DEPTH):
        mod = (cond @ w_ada[l] + b_ada[l])[:, None, :]
        sh_m, sc_m, g_m, sh_f, sc_f, g_f = jnp.split(mod, 6, axis=-1)
        h = _rmsnorm(x, norm_g[l, 0]) * (1.0 + sc_m) + sh_m
        y = _hybrid_mixer(h, cos, sin, l, w_in[l], diff_lambda[l], diff_subln_g[l],
                          mla_q_norm_g[l], w_uq[l], mla_kv_norm_g[l], w_ukv[l],
                          conv_w[l], conv_b[l], dt_bias[l], a_log[l], d_skip[l], ssm_norm_g[l], w_out[l])
        x = x + g_m * _rmsnorm(y, norm_g[l, 1])
        h = _rmsnorm(x, norm_g[l, 2]) * (1.0 + sc_f) + sh_f
        y = _sq_relu_mlp(h, w_up[l], w_down[l])
        x = x + g_f * _rmsnorm(y, norm_g[l, 3])
    return x


DEPTH_2 = 1

HEAD_DIM = 64
D_RWKV = D_MODEL // 2
RWKV_HEADS = D_RWKV // HEAD_DIM
DECAY_LORA = 64
ICL_LORA = 64
GATE_LORA = 128
RWKV_GN_EPS = 64e-5
D_MOBA = D_MODEL // 2
MOBA_HEADS = D_MOBA // HEAD_DIM
MOBA_BLOCK = 256
MOBA_TOPK = 3
MOBA_Q_CHUNK = 32
D_SSM = D_MODEL // 2
SSM_GROUP = 16
SSM_GROUPS_2 = D_SSM // SSM_GROUP
N_BRANCHES = 3
N_EXPERT_GROUPS = 4
EXPERTS_PER_GROUP = 8
N_EXPERTS = N_EXPERT_GROUPS * EXPERTS_PER_GROUP
EXPERT_TOPK = 2
D_EXPERT = D_MODEL // 4
MOE_BLOCK = 512
LN_EPS = 1e-5
DEEPNORM_ALPHA = (2 * DEPTH_2) ** 0.25
DEEPNORM_BETA = (8 * DEPTH_2) ** -0.25
NEG_INF = -1e30
RWKV_COLS = 3 * D_RWKV + DECAY_LORA + ICL_LORA + GATE_LORA
MOBA_COLS = 3 * D_MOBA
OFF_MOBA = RWKV_COLS
OFF_SSM = OFF_MOBA + MOBA_COLS
OFF_GATE = OFF_SSM + D_SSM
D_IN_PROJ = OFF_GATE + N_BRANCHES * D_MODEL


def layer_norm(x, w, b):
    xf = x.astype(jnp.float32)
    mu = jnp.mean(xf, -1, keepdims=True)
    var = jnp.mean(jnp.square(xf - mu), -1, keepdims=True)
    y = (xf - mu) * lax.rsqrt(var + LN_EPS) * w.astype(jnp.float32) + b.astype(jnp.float32)
    return y.astype(x.dtype)

def wkv7_scan(r, w, k, v, a, b):
    Bsz, L, H, N = r.shape

    def step(S, inp):
        r_t, w_t, k_t, v_t, a_t, b_t = inp
        sa = jnp.einsum('bhij,bhj->bhi', S, a_t)
        S = S * w_t[:, :, None, :] + sa[..., None] * b_t[:, :, None, :] + v_t[..., None] * k_t[:, :, None, :]
        return S, jnp.einsum('bhij,bhj->bhi', S, r_t)

    xs = tuple(jnp.moveaxis(t, 1, 0) for t in (r, w, k, v, a, b))
    S0 = jnp.zeros((Bsz, H, N, N), jnp.float32)
    _, y = lax.scan(step, S0, xs)
    return jnp.moveaxis(y, 0, 1)

def rwkv7_mixer(z, mu, w0, w2, a0, a2, g2, k_k, k_a, r_k, ln_w, ln_b):
    f32 = jnp.float32
    Bsz, L, _ = z.shape
    z = z.astype(f32)
    z_prev = jnp.pad(z, ((0, 0), (1, 0), (0, 0)))[:, :-1]
    z = z + (z_prev - z) * mu.astype(f32)
    cuts = np.cumsum([D_RWKV, D_RWKV, D_RWKV, DECAY_LORA, ICL_LORA]).tolist()
    r, k, v, xw, xa, xg = jnp.split(z, cuts, axis=-1)
    w_log = -jax.nn.softplus(-(w0.astype(f32) + jnp.tanh(xw) @ w2.astype(f32))) - 0.5
    decay = jnp.exp(-jnp.exp(w_log))
    a = jax.nn.sigmoid(a0.astype(f32) + xa @ a2.astype(f32))
    g = jax.nn.sigmoid(xg) @ g2.astype(f32)

    def heads(t):
        return t.reshape(Bsz, L, RWKV_HEADS, HEAD_DIM)

    kk = heads(k * k_k.astype(f32))
    kk = kk * lax.rsqrt(jnp.maximum(jnp.sum(kk * kk, -1, keepdims=True), 1e-24))
    k = k * (1.0 + (a - 1.0) * k_a.astype(f32))
    rh, kh, vh, ah = heads(r), heads(k), heads(v), heads(a)
    y = wkv7_scan(rh, heads(decay), kh, vh, -kk, kk * ah)
    mean = jnp.mean(y, -1, keepdims=True)
    var = jnp.mean(jnp.square(y - mean), -1, keepdims=True)
    y = ((y - mean) * lax.rsqrt(var + RWKV_GN_EPS)).reshape(Bsz, L, D_RWKV)
    y = y * ln_w.astype(f32) + ln_b.astype(f32)
    bonus = jnp.sum(rh * kh * r_k.astype(f32), -1, keepdims=True) * vh
    return (y + bonus.reshape(Bsz, L, D_RWKV)) * g

def alibi_slopes(n_heads):
    return 2.0 ** (-8.0 * jnp.arange(1, n_heads + 1, dtype=jnp.float32) / n_heads)

def moba_attention(q, k, v):
    f32 = jnp.float32
    Bsz, L, H, Dh = q.shape
    n_blk = -(-L // MOBA_BLOCK)
    Lp = n_blk * MOBA_BLOCK
    k_sel = min(MOBA_TOPK, n_blk)
    pad = ((0, 0), (0, Lp - L), (0, 0), (0, 0))
    q = jnp.pad(q, pad) * (Dh ** -0.5)
    kbt = jnp.pad(k, pad).reshape(Bsz, n_blk, MOBA_BLOCK, H, Dh).transpose(0, 3, 1, 2, 4)
    vbt = jnp.pad(v, pad).reshape(Bsz, n_blk, MOBA_BLOCK, H, Dh).transpose(0, 3, 1, 2, 4)
    kmean = jnp.mean(kbt.astype(f32), axis=3)
    n_chunk = Lp // MOBA_Q_CHUNK
    qc = q.reshape(Bsz, n_chunk, MOBA_Q_CHUNK, H, Dh).transpose(1, 0, 3, 2, 4)
    slopes = alibi_slopes(H)
    bi = jnp.arange(Bsz)[:, None, None, None]
    hi = jnp.arange(H)[None, :, None, None]
    blk_ids = jnp.arange(n_blk)
    offs = jnp.arange(MOBA_BLOCK)

    def one_chunk(args):
        c, qb = args
        q0 = c * MOBA_Q_CHUNK
        blk = q0 // MOBA_BLOCK
        tpos = q0 + jnp.arange(MOBA_Q_CHUNK)
        gate = jnp.einsum('bhqd,bhnd->bhqn', qb.astype(f32), kmean)
        gate = jnp.where(blk_ids < blk, gate, -jnp.inf)
        _, idx = lax.top_k(gate, k_sel)
        valid = idx < blk
        kg = kbt[bi, hi, idx]
        vg = vbt[bi, hi, idx]
        s_sel = jnp.einsum('bhqd,bhqknd->bhqkn', qb, kg, preferred_element_type=f32)
        spos = idx[..., None] * MOBA_BLOCK + offs
        s_sel = s_sel - slopes[:, None, None, None] * (tpos[:, None, None] - spos).astype(f32)
        s_sel = jnp.where(valid[..., None], s_sel, NEG_INF)
        k_own = lax.dynamic_index_in_dim(kbt, blk, axis=2, keepdims=False)
        v_own = lax.dynamic_index_in_dim(vbt, blk, axis=2, keepdims=False)
        s_own = jnp.einsum('bhqd,bhnd->bhqn', qb, k_own, preferred_element_type=f32)
        dist = tpos[:, None] - (blk * MOBA_BLOCK + offs)[None, :]
        s_own = jnp.where(dist >= 0, s_own - slopes[:, None, None] * dist.astype(f32), NEG_INF)
        s = jnp.concatenate([s_sel.reshape(Bsz, H, MOBA_Q_CHUNK, k_sel * MOBA_BLOCK), s_own], -1)
        p = jax.nn.softmax(s, axis=-1)
        p_sel = p[..., :k_sel * MOBA_BLOCK].reshape(Bsz, H, MOBA_Q_CHUNK, k_sel, MOBA_BLOCK).astype(vg.dtype)
        p_own = p[..., k_sel * MOBA_BLOCK:].astype(v_own.dtype)
        return (jnp.einsum('bhqkn,bhqknd->bhqd', p_sel, vg)
                + jnp.einsum('bhqn,bhnd->bhqd', p_own, v_own))

    out = lax.map(one_chunk, (jnp.arange(n_chunk), qc))
    return out.transpose(1, 0, 3, 2, 4).reshape(Bsz, Lp, H * Dh)[:, :L]

def _complex_affine_combine(e1, e2):
    ar1, ai1, br1, bi1 = e1
    ar2, ai2, br2, bi2 = e2
    return (ar2 * ar1 - ai2 * ai1, ar2 * ai1 + ai2 * ar1,
            ar2 * br1 - ai2 * bi1 + br2, ar2 * bi1 + ai2 * br1 + bi2)

def s5_mixer(u, a_re, a_im, b_re, b_im, c_re, c_im, d, log_dt, glu_w, glu_b):
    f32 = jnp.float32
    Bsz, L, _ = u.shape
    u = u.astype(f32)
    a_re = a_re.astype(f32)
    a_im = a_im.astype(f32)
    dt = jnp.exp(log_dt.astype(f32))[:, None]
    mag = jnp.exp(a_re * dt)
    lam_re = mag * jnp.cos(a_im * dt)
    lam_im = mag * jnp.sin(a_im * dt)
    den = a_re * a_re + a_im * a_im
    nr = lam_re - 1.0
    coef_re = (nr * a_re + lam_im * a_im) / den
    coef_im = (lam_im * a_re - nr * a_im) / den
    b_re = b_re.astype(f32)
    b_im = b_im.astype(f32)
    bb_re = coef_re[..., None] * b_re - coef_im[..., None] * b_im
    bb_im = coef_re[..., None] * b_im + coef_im[..., None] * b_re
    ug = u.reshape(Bsz, L, SSM_GROUPS_2, SSM_GROUP)
    bu_re = jnp.einsum('blgh,gph->blgp', ug, bb_re)
    bu_im = jnp.einsum('blgh,gph->blgp', ug, bb_im)
    lr = jnp.broadcast_to(lam_re, bu_re.shape)
    li = jnp.broadcast_to(lam_im, bu_re.shape)
    _, _, h_re, h_im = lax.associative_scan(_complex_affine_combine, (lr, li, bu_re, bu_im), axis=1)
    y = (jnp.einsum('blgp,ghp->blgh', h_re, c_re.astype(f32))
         - jnp.einsum('blgp,ghp->blgh', h_im, c_im.astype(f32)))
    y = y.reshape(Bsz, L, D_SSM) + d.astype(f32) * u
    y = jax.nn.gelu(y)
    zg = y @ glu_w.astype(f32) + glu_b.astype(f32)
    return zg[..., :D_SSM] * jax.nn.sigmoid(zg[..., D_SSM:])

def hybrid_mixer(x, w_in, rwkv_mu, rwkv_w0, rwkv_w2, rwkv_a0, rwkv_a2, rwkv_g2, rwkv_k_k, rwkv_k_a,
                 rwkv_r_k, rwkv_ln_w, rwkv_ln_b, ssm_a_re, ssm_a_im, ssm_b_re, ssm_b_im, ssm_c_re,
                 ssm_c_im, ssm_d, ssm_log_dt, ssm_glu_w, ssm_glu_b, w_up_rwkv, w_up_moba, w_up_ssm,
                 gate_b, w_out):
    Bsz, L, _ = x.shape
    proj = x @ w_in
    y_a = rwkv7_mixer(proj[..., :OFF_MOBA], rwkv_mu, rwkv_w0, rwkv_w2, rwkv_a0, rwkv_a2, rwkv_g2,
                      rwkv_k_k, rwkv_k_a, rwkv_r_k, rwkv_ln_w, rwkv_ln_b).astype(x.dtype)
    q, k, v = jnp.split(proj[..., OFF_MOBA:OFF_SSM], 3, axis=-1)

    def heads(t):
        return t.reshape(Bsz, L, MOBA_HEADS, HEAD_DIM)

    y_b = moba_attention(heads(q), heads(k), heads(v))
    y_c = s5_mixer(proj[..., OFF_SSM:OFF_GATE], ssm_a_re, ssm_a_im, ssm_b_re, ssm_b_im, ssm_c_re,
                   ssm_c_im, ssm_d, ssm_log_dt, ssm_glu_w, ssm_glu_b).astype(x.dtype)
    gates = jax.nn.sigmoid(proj[..., OFF_GATE:] + gate_b).reshape(Bsz, L, N_BRANCHES, D_MODEL)
    merged = (gates[..., 0, :] * (y_a @ w_up_rwkv)
              + gates[..., 1, :] * (y_b @ w_up_moba)
              + gates[..., 2, :] * (y_c @ w_up_ssm))
    return merged @ w_out

def hier_moe(x, router_group_w, router_group_b, router_expert_w, router_expert_b,
             expert_w_gate, expert_w_up, expert_w_down):
    f32 = jnp.float32
    Bsz, L, D = x.shape
    T = Bsz * L
    TK = T * EXPERT_TOPK
    xt = x.reshape(T, D)
    xf = xt.astype(f32)
    g_logits = xf @ router_group_w.astype(f32) + router_group_b.astype(f32)
    g_sel = jnp.argmax(g_logits, axis=-1)
    p_group = jnp.take_along_axis(jax.nn.softmax(g_logits, -1), g_sel[:, None], axis=-1)
    e_logits = (xf @ router_expert_w.astype(f32) + router_expert_b.astype(f32)).reshape(
        T, N_EXPERT_GROUPS, EXPERTS_PER_GROUP)
    e_logits = jnp.take_along_axis(e_logits, g_sel[:, None, None], axis=1)[:, 0]
    top_logit, top_local = lax.top_k(e_logits, EXPERT_TOPK)
    weight = p_group * jax.nn.softmax(top_logit, axis=-1)
    expert = g_sel[:, None] * EXPERTS_PER_GROUP + top_local
    flat_e = expert.reshape(TK)
    order = jnp.argsort(flat_e)
    e_sorted = flat_e[order]
    tok_sorted = order // EXPERT_TOPK
    counts = jnp.bincount(flat_e, length=N_EXPERTS)
    starts = jnp.cumsum(counts) - counts
    padded = (counts + MOE_BLOCK - 1) // MOE_BLOCK * MOE_BLOCK
    p_ends = jnp.cumsum(padded)
    p_starts = p_ends - padded
    dest = p_starts[e_sorted] + jnp.arange(TK) - starts[e_sorted]
    n_blocks = -(-TK // MOE_BLOCK) + N_EXPERTS
    buf = jnp.zeros((n_blocks * MOE_BLOCK, D), x.dtype).at[dest].set(xt[tok_sorted])
    blk_e = jnp.minimum(jnp.searchsorted(p_ends, jnp.arange(n_blocks) * MOE_BLOCK, side='right'),
                        N_EXPERTS - 1)
    xb = buf.reshape(n_blocks, MOE_BLOCK, D)
    hid = (jax.nn.silu(jnp.einsum('nbd,ndf->nbf', xb, expert_w_gate[blk_e]))
           * jnp.einsum('nbd,ndf->nbf', xb, expert_w_up[blk_e]))
    yb = jnp.einsum('nbf,nfd->nbd', hid, expert_w_down[blk_e]).reshape(n_blocks * MOE_BLOCK, D)
    w_sorted = weight.reshape(TK)[order].astype(x.dtype)
    y = jnp.zeros((T, D), x.dtype).at[tok_sorted].add(yb[dest] * w_sorted[:, None])
    return y.reshape(Bsz, L, D)

def second_inputs(seed: int = 0) -> dict:
    key = jax.random.key(seed)
    keys = iter(jax.random.split(key, 48))
    f32 = jnp.float32

    def nrm(shape, scale):
        return scale * jax.random.normal(next(keys), shape, f32)

    def near(shape, center, spread):
        return center + spread * jax.random.normal(next(keys), shape, f32)

    Ld = DEPTH_2
    ratio = jnp.arange(D_RWKV, dtype=f32) / (D_RWKV - 1)
    w0_base = -7.0 + 5.0 * ratio ** 0.85 + 0.5
    a_im_base = jnp.pi * jnp.arange(SSM_STATE, dtype=f32)
    return {
        'x': nrm((BATCH, SEQ, D_MODEL), 1.0),
        'w_in': nrm((Ld, D_MODEL, D_IN_PROJ), D_MODEL ** -0.5),
        'rwkv_mu': jax.random.uniform(next(keys), (Ld, RWKV_COLS), f32),
        'rwkv_w0': w0_base + nrm((Ld, D_RWKV), 0.1),
        'rwkv_w2': nrm((Ld, DECAY_LORA, D_RWKV), 0.5 * DECAY_LORA ** -0.5),
        'rwkv_a0': nrm((Ld, D_RWKV), 0.1),
        'rwkv_a2': nrm((Ld, ICL_LORA, D_RWKV), ICL_LORA ** -0.5),
        'rwkv_g2': nrm((Ld, GATE_LORA, D_RWKV), GATE_LORA ** -0.5),
        'rwkv_k_k': near((Ld, D_RWKV), 0.85, 0.05),
        'rwkv_k_a': near((Ld, D_RWKV), 1.0, 0.05),
        'rwkv_r_k': nrm((Ld, RWKV_HEADS, HEAD_DIM), 0.1),
        'rwkv_ln_w': near((Ld, D_RWKV), 1.0, 0.05),
        'rwkv_ln_b': nrm((Ld, D_RWKV), 0.02),
        'ssm_a_re': near((Ld, SSM_GROUPS_2, SSM_STATE), -0.5, 0.01),
        'ssm_a_im': jnp.broadcast_to(a_im_base, (Ld, SSM_GROUPS_2, SSM_STATE)) + nrm((Ld, SSM_GROUPS_2, SSM_STATE), 0.01),
        'ssm_b_re': nrm((Ld, SSM_GROUPS_2, SSM_STATE, SSM_GROUP), (2 * SSM_GROUP) ** -0.5),
        'ssm_b_im': nrm((Ld, SSM_GROUPS_2, SSM_STATE, SSM_GROUP), (2 * SSM_GROUP) ** -0.5),
        'ssm_c_re': nrm((Ld, SSM_GROUPS_2, SSM_GROUP, SSM_STATE), 0.5),
        'ssm_c_im': nrm((Ld, SSM_GROUPS_2, SSM_GROUP, SSM_STATE), 0.5),
        'ssm_d': nrm((Ld, D_SSM), 1.0),
        'ssm_log_dt': jax.random.uniform(next(keys), (Ld, SSM_GROUPS_2), f32,
                                         minval=float(np.log(1e-3)), maxval=float(np.log(1e-1))),
        'ssm_glu_w': nrm((Ld, D_SSM, 2 * D_SSM), D_SSM ** -0.5),
        'ssm_glu_b': nrm((Ld, 2 * D_SSM), 0.02),
        'w_up_rwkv': nrm((Ld, D_RWKV, D_MODEL), D_RWKV ** -0.5),
        'w_up_moba': nrm((Ld, D_MOBA, D_MODEL), D_MOBA ** -0.5),
        'w_up_ssm': nrm((Ld, D_SSM, D_MODEL), D_SSM ** -0.5),
        'gate_b': nrm((Ld, N_BRANCHES * D_MODEL), 0.1),
        'w_out': nrm((Ld, D_MODEL, D_MODEL), DEEPNORM_BETA * D_MODEL ** -0.5),
        'ln1_w': near((Ld, D_MODEL), 1.0, 0.05),
        'ln1_b': nrm((Ld, D_MODEL), 0.02),
        'router_group_w': nrm((Ld, D_MODEL, N_EXPERT_GROUPS), D_MODEL ** -0.5),
        'router_group_b': nrm((Ld, N_EXPERT_GROUPS), 0.01),
        'router_expert_w': nrm((Ld, D_MODEL, N_EXPERTS), D_MODEL ** -0.5),
        'router_expert_b': nrm((Ld, N_EXPERTS), 0.01),
        'expert_w_gate': nrm((Ld, N_EXPERTS, D_MODEL, D_EXPERT), D_MODEL ** -0.5),
        'expert_w_up': nrm((Ld, N_EXPERTS, D_MODEL, D_EXPERT), D_MODEL ** -0.5),
        'expert_w_down': nrm((Ld, N_EXPERTS, D_EXPERT, D_MODEL), DEEPNORM_BETA * D_EXPERT ** -0.5),
        'ln2_w': near((Ld, D_MODEL), 1.0, 0.05),
        'ln2_b': nrm((Ld, D_MODEL), 0.02),
    }

def second_block(x, w_in, rwkv_mu, rwkv_w0, rwkv_w2, rwkv_a0, rwkv_a2, rwkv_g2, rwkv_k_k, rwkv_k_a,
              rwkv_r_k, rwkv_ln_w, rwkv_ln_b, ssm_a_re, ssm_a_im, ssm_b_re, ssm_b_im, ssm_c_re,
              ssm_c_im, ssm_d, ssm_log_dt, ssm_glu_w, ssm_glu_b, w_up_rwkv, w_up_moba, w_up_ssm,
              gate_b, w_out, ln1_w, ln1_b, router_group_w, router_group_b, router_expert_w,
              router_expert_b, expert_w_gate, expert_w_up, expert_w_down, ln2_w, ln2_b):
    for l in range(DEPTH_2):
        h = hybrid_mixer(x, w_in[l], rwkv_mu[l], rwkv_w0[l], rwkv_w2[l], rwkv_a0[l], rwkv_a2[l],
                         rwkv_g2[l], rwkv_k_k[l], rwkv_k_a[l], rwkv_r_k[l], rwkv_ln_w[l], rwkv_ln_b[l],
                         ssm_a_re[l], ssm_a_im[l], ssm_b_re[l], ssm_b_im[l], ssm_c_re[l], ssm_c_im[l],
                         ssm_d[l], ssm_log_dt[l], ssm_glu_w[l], ssm_glu_b[l], w_up_rwkv[l],
                         w_up_moba[l], w_up_ssm[l], gate_b[l], w_out[l])
        x = layer_norm(DEEPNORM_ALPHA * x + h, ln1_w[l], ln1_b[l])
        h = hier_moe(x, router_group_w[l], router_group_b[l], router_expert_w[l], router_expert_b[l],
                     expert_w_gate[l], expert_w_up[l], expert_w_down[l])
        x = layer_norm(DEEPNORM_ALPHA * x + h, ln2_w[l], ln2_b[l])
    return x


def setup_inputs(seed=0):
    out = dict(first_inputs(seed))
    for name, value in second_inputs(seed + 1).items():
        if name != "x":
            out[name + "_2"] = value
    return out


def reference(
    x, c, positions, w_ada, b_ada, norm_g, w_in, diff_lambda, diff_subln_g, mla_q_norm_g, w_uq,
    mla_kv_norm_g, w_ukv, conv_w, conv_b, dt_bias, a_log, d_skip, ssm_norm_g, w_out, w_up,
    w_down, w_in_2, rwkv_mu_2, rwkv_w0_2, rwkv_w2_2, rwkv_a0_2, rwkv_a2_2, rwkv_g2_2,
    rwkv_k_k_2, rwkv_k_a_2, rwkv_r_k_2, rwkv_ln_w_2, rwkv_ln_b_2, ssm_a_re_2, ssm_a_im_2,
    ssm_b_re_2, ssm_b_im_2, ssm_c_re_2, ssm_c_im_2, ssm_d_2, ssm_log_dt_2, ssm_glu_w_2,
    ssm_glu_b_2, w_up_rwkv_2, w_up_moba_2, w_up_ssm_2, gate_b_2, w_out_2, ln1_w_2, ln1_b_2,
    router_group_w_2, router_group_b_2, router_expert_w_2, router_expert_b_2, expert_w_gate_2,
    expert_w_up_2, expert_w_down_2, ln2_w_2, ln2_b_2,
):
    x = first_block(
        x, c, positions, w_ada, b_ada, norm_g, w_in, diff_lambda, diff_subln_g, mla_q_norm_g,
        w_uq, mla_kv_norm_g, w_ukv, conv_w, conv_b, dt_bias, a_log, d_skip, ssm_norm_g, w_out,
        w_up, w_down,
    )
    return second_block(
        x, w_in_2, rwkv_mu_2, rwkv_w0_2, rwkv_w2_2, rwkv_a0_2, rwkv_a2_2, rwkv_g2_2, rwkv_k_k_2,
        rwkv_k_a_2, rwkv_r_k_2, rwkv_ln_w_2, rwkv_ln_b_2, ssm_a_re_2, ssm_a_im_2, ssm_b_re_2,
        ssm_b_im_2, ssm_c_re_2, ssm_c_im_2, ssm_d_2, ssm_log_dt_2, ssm_glu_w_2, ssm_glu_b_2,
        w_up_rwkv_2, w_up_moba_2, w_up_ssm_2, gate_b_2, w_out_2, ln1_w_2, ln1_b_2,
        router_group_w_2, router_group_b_2, router_expert_w_2, router_expert_b_2,
        expert_w_gate_2, expert_w_up_2, expert_w_down_2, ln2_w_2, ln2_b_2,
    )


_drawn_inputs = setup_inputs


def setup_inputs(seed=0):
    import zlib

    import numpy as np

    out = dict(_drawn_inputs(seed))
    spreads = {}
    factors = {'diff_lambda': 4.063,
     'diff_subln_g': 149.075,
     'mla_q_norm_g': 31.306,
     'mla_kv_norm_g': 28.959,
     'conv_b': 3.45,
     'ssm_norm_g': 118.792,
     'rwkv_w2_2': 4.917,
     'rwkv_a0_2': 6.912,
     'rwkv_k_k_2': 4.683,
     'rwkv_k_a_2': 3.62,
     'rwkv_ln_w_2': 4.846,
     'rwkv_ln_b_2': 8.0,
     'ssm_a_re_2': 200.0,
     'ssm_glu_b_2': 22.533,
     'gate_b_2': 4.346,
     'router_group_b_2': 8.0,
     'router_expert_b_2': 20.848,
     'ln2_b_2': 2.735,
     'ssm_a_im_2': 32.008,
     'ssm_b_re_2': 37.88,
     'ssm_b_im_2': 44.027,
     'ssm_c_re_2': 37.696,
     'ssm_c_im_2': 38.648,
     'ssm_log_dt_2': 32.568}
    for name, (base, spread) in spreads.items():
        noise = np.random.default_rng([zlib.crc32(name.encode()), seed]).standard_normal(out[name].shape)
        drawn = base * np.exp(spread * noise) if base else spread * noise
        out[name] = jnp.asarray(drawn.astype(out[name].dtype))
    for name, factor in factors.items():
        out[name] = (out[name] * factor).astype(out[name].dtype)
    return out
```

```python
import math

import numpy as np

import concourse.bass as bass
from concourse import mybir
from concourse.alu_op_type import AluOpType as ALU

F32 = mybir.dt.float32
I32 = mybir.dt.int32
ACT = mybir.ActivationFunctionType
AX = mybir.AxisListType.X

P = 128
SEQ = 256
TT = SEQ // P
D = 1024
KT = D // P
DEPTH = 2
FF = 4 * D
SLOT = 2048
RING = 4
EXPERTS, D_EXPERT = 32, 256
TWO_PI = 2 * math.pi
ARENA = 30000
ROUND = 1.5 * 2.0 ** 23


class Queue:

    def __init__(self, nc, engine, name, ordered=True):
        self.engine, self.sem, self.ordered = engine, nc.alloc_semaphore(name), ordered
        self.count, self.seen = 0, {}

    def wait(self, *marks):
        for mark in marks:
            if mark is not None and self.seen.get(mark[0].name, 0) < mark[1]:
                self.engine.wait_ge(mark[0], mark[1])
                self.seen[mark[0].name] = mark[1]

    def after(self, *marks):
        self.wait(*marks)
        if self.ordered and self.count:
            self.wait(self.last)
        return self.engine

    def did(self, instruction):
        instruction.then_inc(self.sem, 1)
        self.count += 1
        return self.last

    @property
    def last(self):
        return (self.sem, self.count) if self.count else None


class Loads:

    def __init__(self, nc, name):
        self.sem, self.count = nc.alloc_semaphore(name), 0

    def load(self, engine, out, in_):
        engine.dma_start(out, in_).then_inc(self.sem, 16)
        self.count += 16

    @property
    def last(self):
        return (self.sem, self.count) if self.count else None


class Core:

    def __init__(self, nc):
        self.nc = nc
        self.tensor = Queue(nc, nc.tensor, "tensor_done", ordered=False)
        self.vector = Queue(nc, nc.vector, "vector_done")
        self.scalar = Queue(nc, nc.scalar, "scalar_done")
        self.gpsimd = Queue(nc, nc.gpsimd, "gpsimd_done")
        self.sync = Queue(nc, nc.sync, "sync_done")
        self.small = Loads(nc, "small_loads")
        self.queues = [self.tensor, self.vector, self.scalar, self.gpsimd, self.sync]
        self.banks = [nc.alloc_psum_tensor(f"bank{i}", [P, 512], F32).ap() for i in range(8)]
        self.bank_free = [[] for _ in self.banks]
        self.bank_next, self.bank_used = 0, list(range(8))
        self.ring = [nc.alloc_sbuf_tensor(f"weights{i}", [P, SLOT], F32).ap() for i in range(6)]
        self.ring_full = [nc.alloc_semaphore(f"weights{i}_full") for i in range(6)]
        self.ring_loads, self.ring_plan, self.ring_taken = [0] * 6, [], 0
        self.arena = nc.alloc_sbuf_tensor("arena", [P, ARENA], F32).ap()
        self.carved = 0

    def keep(self, name, *shape, dtype=F32):
        return self.nc.alloc_sbuf_tensor(name, [P, *shape], dtype).ap()

    def carve(self, *shape):
        n = int(np.prod(shape))
        piece = self.arena[:, self.carved:self.carved + n]
        self.carved += n
        assert self.carved <= ARENA, self.carved
        if len(shape) == 2:
            piece = piece.rearrange("p (a b) -> p a b", b=shape[1])
        if len(shape) == 3:
            piece = piece.rearrange("p (a b c) -> p a b c", b=shape[1], c=shape[2])
        return piece

    def bank(self):
        i = self.bank_used[self.bank_next % len(self.bank_used)]
        self.bank_next += 1
        self.tensor.wait(*self.bank_free[i])
        self.bank_free[i] = []
        return i, self.banks[i]

    def read(self, i, *marks):
        self.bank_free[i] += [m for m in marks if m]

    def plan(self, pieces):
        self.ring_plan, self.ring_taken, self.ring_issued = pieces, 0, 0
        for _ in range(min(RING, len(pieces))):
            self.issue()

    def issue(self, *freed):
        if self.ring_issued < len(self.ring_plan):
            s, (view, source) = self.ring_issued % RING, self.ring_plan[self.ring_issued]
            self.sync.wait(*freed)
            self.nc.sync.dma_start(view(self.ring[s]), source).then_inc(self.ring_full[s], 16)
            self.ring_issued += 1

    def weights(self, queue):
        s, (view, _) = self.ring_taken % RING, self.ring_plan[self.ring_taken]
        self.ring_loads[s] += 16
        queue.wait((self.ring_full[s], self.ring_loads[s]))
        self.ring_taken += 1
        return view(self.ring[s])

    def release(self, *readers):
        self.issue(*readers)

    def restart(self, ring=False):
        nc = self.nc
        nc.all_engine_barrier()
        for q in self.queues:
            if q.count:
                nc.sync.sem_clear(q.sem)
        if self.small.count:
            nc.sync.sem_clear(self.small.sem)
        if ring:
            for s in range(RING):
                nc.sync.sem_clear(self.ring_full[s])
            self.ring_loads = [0] * 6
        nc.all_engine_barrier()
        for q in self.queues:
            q.count, q.seen = 0, {}
        self.small.count = 0
        self.bank_free = [[] for _ in self.banks]
        self.carved = 0

    def restart_in_loop(self):
        kept = self.carved
        self.restart()
        self.carved = kept

    def mm(self, out, lhsT, rhs, start=True, stop=True):
        return self.nc.tensor.matmul(out, lhsT, rhs, start=start, stop=stop)

    def tt(self, out, a, b, op, *marks, q=None):
        q = q or self.vector
        return q.did(q.after(*marks).tensor_tensor(out, a, b, op))

    def ts(self, out, a, s1, s2, op0, op1, *marks, q=None):
        q = q or self.vector
        if op1 is None:
            return q.did(q.after(*marks).tensor_scalar(out, a, s1, None, op0))
        return q.did(q.after(*marks).tensor_scalar(out, a, s1, s2, op0, op1))

    def stt(self, out, a, s, b, op0, op1, *marks):
        q = self.vector
        return q.did(q.after(*marks).scalar_tensor_tensor(out, a, s, b, op0, op1))

    def copy(self, out, a, *marks, q=None):
        q = q or self.vector
        if q is self.scalar:
            return q.did(q.after(*marks).activation(out, a, ACT.Copy))
        return q.did(q.after(*marks).tensor_copy(out, a))

    def act(self, out, a, func, *marks, **kw):
        q = self.scalar
        return q.did(q.after(*marks).activation(out, a, func, **kw))

    def reduce(self, out, a, op, *marks, negate=None):
        q = self.vector
        return q.did(q.after(*marks).tensor_reduce(out, a, AX, op, negate=negate))

    def recip(self, out, a, *marks):
        q = self.vector
        return q.did(q.after(*marks).reciprocal(out, a))

    def fill(self, out, value, *marks, q=None):
        q = q or self.vector
        return q.did(q.after(*marks).memset(out, value))

    def sumsq(self, out, a, b, junk, *marks):
        q = self.vector
        return q.did(q.after(*marks).tensor_tensor_reduce(out=junk, in0=a, in1=b, scale=1.0, scalar=0.0,
                                                          op0=ALU.mult, op1=ALU.add, accum_out=out))

    def rsqrt(self, out, total, n, eps, *marks):
        m = self.ts(out, total, 1.0 / n, eps, ALU.mult, ALU.add, *marks)
        m = self.act(out, out, ACT.Sqrt, m)
        return self.recip(out, out, m)

    def columns_from_rows(self, out, rows, identity, tiles, evacuate, *marks):
        self.tensor.wait(*marks)
        done = []
        for k0 in range(0, tiles, 2):
            i, bank = self.bank()
            n = min(2, tiles - k0)
            for k in range(k0, k0 + n):
                for t in range(TT):
                    c = ((k - k0) * TT + t) * P
                    ins = self.nc.tensor.transpose(bank[:, c:c + P], rows[:, t, k * P:(k + 1) * P], identity)
            m = self.tensor.did(ins)
            if evacuate is None:
                src = bank[:, 0:n * SEQ].rearrange("p (k s) -> p k s", s=SEQ)
                q = self.scalar if (k0 // 2) % 2 else self.vector
                d = [self.copy(out[:, k0:k0 + n, :], src, m, q=q)]
            else:
                d = [evacuate(k, out[:, k, :], bank[:, (k - k0) * SEQ:(k - k0 + 1) * SEQ], m)
                     for k in range(k0, k0 + n)]
            self.read(i, *d)
            done += d
        return done

    def product_cols(self, xT, w, tiles, width=2):
        i, bank = self.bank()
        for j in range(width):
            for n, k in enumerate(tiles):
                ins = self.mm(bank[:, j * SEQ:(j + 1) * SEQ], w[:, n, j * P:(j + 1) * P], xT[:, k, :],
                              start=(n == 0), stop=(n == len(tiles) - 1))
        return i, bank[:, 0:width * SEQ].rearrange("p (j s) -> p j s", s=SEQ), self.tensor.did(ins)

    def product_rows(self, xT, w, tiles, width=256):
        i, bank = self.bank()
        for t in range(TT):
            for n, k in enumerate(tiles):
                ins = self.mm(bank[:, t * width:(t + 1) * width], xT[:, k, t * P:(t + 1) * P], w[:, n, :],
                              start=(n == 0), stop=(n == len(tiles) - 1))
        return i, bank[:, 0:TT * width].rearrange("p (t n) -> p t n", t=TT), self.tensor.did(ins)

    def sincos(self, sin, cos, x, k, *marks):
        c1 = 6.28125
        c2 = round((TWO_PI - c1) * 2 ** 20) / 2 ** 20
        c3 = TWO_PI - c1 - c2
        m = self.ts(k, x, 1 / TWO_PI, ROUND, ALU.mult, ALU.add, *marks)
        m = self.ts(k, k, -ROUND, None, ALU.add, None)
        for c in (c1, c2, c3):
            m = self.stt(x, k, -c, x, ALU.mult, ALU.add)
        m = self.ts(x, x, 3.1415925, -3.1415925, ALU.min, ALU.max)
        ms = self.act(sin, x, ACT.Sin, m)
        m = self.act(cos, x, ACT.Sin, m, scale=0.5)
        m = self.tt(cos, cos, cos, ALU.mult, m)
        m = self.ts(cos, cos, -2.0, 1.0, ALU.mult, ALU.add)
        return [m, ms]

    def softmax_exp(self, scores, neg_max, total, n, keys, *marks):
        m = self.reduce(neg_max[:, 0:n], scores[:, 0:n, 0:keys], ALU.max, *marks, negate=True)
        for h in range(n):
            m = self.act(scores[:, h, 0:keys], scores[:, h, 0:keys], ACT.Exp, m,
                         bias=neg_max[:, h:h + 1], accum_out=total[:, h:h + 1])
        return self.recip(total[:, 0:n], total[:, 0:n], m)

    def transpose_maps(self, pT, maps, n, t, identity, *marks):
        self.tensor.wait(*marks)
        done = []
        kts = t + 1
        per = 4 // kts
        for h0 in range(0, n, per):
            i, bank = self.bank()
            for h in range(h0, h0 + per):
                for kt in range(kts):
                    c = ((h - h0) * kts + kt) * P
                    ins = self.nc.tensor.transpose(bank[:, c:c + P], maps[:, h, kt * P:(kt + 1) * P], identity)
            m = self.tensor.did(ins)
            src = bank[:, :].rearrange("p (h k s) -> p h k s", h=per, k=kts)
            q = self.scalar if (h0 // per) % 2 else self.vector
            d = self.copy(pT[:, h0:h0 + per, 0:kts, t * P:(t + 1) * P], src, m, q=q)
            self.read(i, d)
            done.append(d)
        return done


def constants(c):
    g = c.gpsimd

    def select(out, cmp, fill, base, pattern, channel):
        return g.did(g.after().affine_select(out=out, in_=out, compare_op=cmp, fill=fill, base=base,
                                             pattern=pattern, channel_multiplier=channel))

    c.identity = c.keep("identity", P)
    c.fill(c.identity, 0.0, q=g)
    select(c.identity, ALU.not_equal, 1.0, 0, [[-1, P]], 1)
    c.ones = c.keep("ones", P)
    c.fill(c.ones, 1.0, q=g)
    c.head_sum = c.keep("head_sum", P)
    c.fill(c.head_sum, 1.0, q=g)
    select(c.head_sum[:, 0:64], ALU.is_ge, 0.0, 63, [[0, 64]], -1)
    select(c.head_sum[:, 64:P], ALU.is_ge, 0.0, -64, [[0, 64]], 1)


def first_constants(c):
    g = c.gpsimd

    def select(out, cmp, fill, base, pattern, channel):
        return g.did(g.after().affine_select(out=out, in_=out, compare_op=cmp, fill=fill, base=base,
                                             pattern=pattern, channel_multiplier=channel))
    c.chunk_mask = c.keep("chunk_mask", TT, SEQ)
    c.fill(c.chunk_mask, 0.0, q=g)
    for t in range(TT):
        for half in range(2):
            rows = c.chunk_mask[64 * half:64 * half + 64, t, :]
            select(rows, ALU.is_ge, -1e30, t * P + 64 * half + 63, [[-1, SEQ]], 0)
    c.causal = c.keep("causal", TT, SEQ)
    c.fill(c.causal, 1.0, q=g)
    for t in range(TT):
        select(c.causal[:, t, :], ALU.is_ge, 0.0, -t * P, [[1, SEQ]], -1)


OFF_Q, OFF_K, OFF_V, OFF_CQ, OFF_CKV, OFF_Z, OFF_XBC, OFF_DT = 0, 256, 512, 768, 1024, 1184, 1696, 2464
LORA = 160


def k_tiles(n, width=256):
    return lambda slot: slot[:, 0:n * width].rearrange("p (k n) -> p k n", n=width)


def rope_tables(c, a):
    c.rope_cos, c.rope_sin = c.keep("rope_cos", TT, 16), c.keep("rope_sin", TT, 16)
    pos_i, pos = c.keep("position_int", TT, dtype=I32), c.keep("position", TT)
    freq, angle, turn = c.carve(16), c.carve(TT, 16), c.carve(TT, 16)
    for t in range(TT):
        c.small.load(c.nc.scalar, pos_i[:, t:t + 1], a["positions"][0:1, t * P:(t + 1) * P].rearrange("a p -> p a"))
    m = c.copy(pos, pos_i, c.small.last)
    for j in range(16):
        f = np.float32(1.0) / np.power(np.float32(10000.0), np.float32(2 * j) / np.float32(32))
        m = c.fill(freq[:, j:j + 1], float(f))
    for t in range(TT):
        m = c.ts(angle[:, t, :], freq, pos[:, t:t + 1], None, ALU.mult, None, m)
    c.sincos(c.rope_sin, c.rope_cos, angle, turn, m)


def rope(c, out, x, t, heads, stride_view, scratch, *marks):
    cos = c.rope_cos[:, t:t + 1, :].to_broadcast([P, heads, 16])
    sin = c.rope_sin[:, t:t + 1, :].to_broadcast([P, heads, 16])
    x1, x2 = x[:, :, 0:16], x[:, :, 16:32]
    m = c.tt(out[:, :, 0:16], x1, cos, ALU.mult, *marks)
    m = c.tt(scratch, x2, sin, ALU.mult)
    m = c.tt(out[:, :, 0:16], out[:, :, 0:16], scratch, ALU.subtract)
    m = c.tt(scratch, x1, sin, ALU.mult)
    m = c.tt(out[:, :, 16:32], x2, cos, ALU.mult)
    return c.tt(out[:, :, 16:32], out[:, :, 16:32], scratch, ALU.add)


def layer_pieces(a, l):
    w_ada = a["w_ada"][bass.ds(l, 1), :, :].rearrange("a k n -> (a k) n")
    w_in = a["w_in"][bass.ds(l, 1), :, :].rearrange("a (k p) n -> p (a k) n", p=P)
    w_out = a["w_out"][bass.ds(l, 1), :, :].rearrange("a (k p) n -> p (a k) n", p=P)
    w_up = a["w_up"][bass.ds(l, 1), :, :].rearrange("a (k p) n -> p (a k) n", p=P)
    w_down = a["w_down"][bass.ds(l, 1), :, :].rearrange("a (k p) n -> p (a k) n", p=P)
    pieces = [(lambda s: s, w_ada[k * P:(k + 1) * P, g * SLOT:(g + 1) * SLOT])
              for g in range(3) for k in range(KT)]
    for off in (OFF_Q, OFF_K, OFF_V, OFF_CQ):
        pieces.append((k_tiles(KT), w_in[:, :, off:off + 256]))
    pieces.append((k_tiles(KT, LORA), w_in[:, :, OFF_CKV:OFF_CKV + LORA]))
    for off in (OFF_Z, OFF_Z + 256, OFF_XBC, OFF_XBC + 256, OFF_XBC + 512):
        pieces.append((k_tiles(KT), w_in[:, :, off:off + 256]))
    pieces += [(k_tiles(KT), w_out[:, :, n * 256:(n + 1) * 256]) for n in range(4)]
    pieces += [(k_tiles(KT), w_up[:, :, n * 256:(n + 1) * 256]) for n in range(FF // 256)]
    pieces += [(k_tiles(KT), w_down[:, k * KT:(k + 1) * KT, n * 256:(n + 1) * 256])
               for n in range(4) for k in range(FF // D)]
    return pieces


V_NORM0, V_NORM2, V_QN, V_KVN, V_CONV_W, V_CONV_B, V_COND, V_ADA = 0, 8, 16, 18, 19, 43, 49, 57
V_ROWS = V_ADA + 48


def modulation(c, a, l, s):
    nc = c.nc
    vec = c.carve(P)
    junk = c.carve(8)
    row = lambda name: a[name][bass.ds(l, 1)]
    q = nc.scalar
    c.small.load(q, vec[V_NORM0:V_NORM0 + 8, :], row("norm_g")[:, 0, :].rearrange("a (r p) -> (a r) p", p=P))
    c.small.load(q, vec[V_NORM2:V_NORM2 + 8, :], row("norm_g")[:, 2, :].rearrange("a (r p) -> (a r) p", p=P))
    c.small.load(q, vec[V_QN:V_QN + 2, :], row("mla_q_norm_g").rearrange("a (r p) -> (a r) p", p=P))
    c.small.load(q, vec[V_KVN:V_KVN + 1, :], row("mla_kv_norm_g"))
    c.small.load(q, vec[V_CONV_W:V_CONV_W + 24, :], row("conv_w").rearrange("a j (r p) -> (a j r) p", p=P))
    c.small.load(q, vec[V_CONV_B:V_CONV_B + 6, :], row("conv_b").rearrange("a (r p) -> (a r) p", p=P))
    c.small.load(q, vec[V_COND:V_COND + 8, :], a["c"].rearrange("a (r p) -> (a r) p", p=P))
    c.small.load(q, vec[V_ADA:V_ADA + 48, :], row("b_ada").rearrange("a (r p) -> (a r) p", p=P))
    for dst, src in ((s.norm1, row("norm_g")[:, 1, :]), (s.norm3, row("norm_g")[:, 3, :])):
        c.small.load(q, dst, src.to_broadcast([P, D]))
    for dst, off in ((s.gate_m, 2 * D), (s.gate_f, 5 * D)):
        c.small.load(q, dst, row("b_ada")[:, off:off + D].to_broadcast([P, D]))
    c.tensor.wait(c.small.last, c.gpsimd.last)
    i, bank = c.bank()
    m = c.tensor.did(nc.tensor.transpose(bank[:, 0:V_ROWS], vec[0:V_ROWS, :], c.identity[0:V_ROWS, 0:V_ROWS]))
    m = c.copy(s.vec[:, 0:V_ROWS], bank[:, 0:V_ROWS], m)
    c.read(i, m)
    cond = c.carve(8)
    mc = c.act(cond, s.vec[:, V_COND:V_COND + 8], ACT.Silu, m)
    acc = c.carve(6 * D)
    for g in range(3):
        part = acc[:, g * SLOT:(g + 1) * SLOT]
        for k in range(KT):
            w = c.weights(c.vector)
            if k == 0:
                m = c.ts(part, w, cond[:, 0:1], None, ALU.mult, None, mc)
            else:
                m = c.stt(part, w, cond[:, k:k + 1], part, ALU.mult, ALU.add)
            c.release(m)
    c.tensor.wait(m)
    i, bank = c.bank()
    for n in range(48):
        ins = c.mm(bank[:, n:n + 1], acc[:, n * P:(n + 1) * P], c.ones[:, 0:1])
    m = c.tensor.did(ins)
    m = c.tt(s.mod, bank[:, 0:48], s.vec[:, V_ADA:V_ADA + 48], ALU.add, m)
    c.read(i, m)
    for gate, norm, off in ((s.gate_m, s.norm1, 2 * D), (s.gate_f, s.norm3, 5 * D)):
        for h in range(2):
            i, bank = c.bank()
            m = c.tensor.did(c.mm(bank, c.ones, acc[:, off + h * 512:off + (h + 1) * 512]))
            part = gate[:, h * 512:(h + 1) * 512]
            m = c.tt(part, bank, part, ALU.add, m, c.small.last)
            c.read(i, m)
            m = c.tt(part, part, norm[:, h * 512:(h + 1) * 512], ALU.mult, m)
    for out, g, sc in ((s.in_scale_m, V_NORM0, 8), (s.in_scale_f, V_NORM2, 32)):
        c.stt(out, s.mod[:, sc:sc + 8], 1.0, s.vec[:, g:g + 8], ALU.add, ALU.mult)


def normed_cols(c, hT, x, scale, shift, work, small, *marks):
    for t in range(TT):
        m = c.sumsq(small[:, t:t + 1], x[:, t, :], x[:, t, :], work[:, t, :], *marks)
    m = c.rsqrt(small[:, 0:TT], small[:, 0:TT], D, 1e-6, m)
    for t in range(TT):
        m = c.act(work[:, t, :], x[:, t, :], ACT.Copy, m, scale=small[:, t:t + 1])

    def evacuate(k, out, src, mark):
        if (k // 2) % 2:
            return c.act(out, src, ACT.Identity, mark, scale=scale[:, k:k + 1], bias=shift[:, k:k + 1])
        return c.ts(out, src, scale[:, k:k + 1], shift[:, k:k + 1], ALU.mult, ALU.add, mark)
    return c.columns_from_rows(hT, work, c.identity, KT, evacuate, m, c.vector.last)


def projections(c, a, l, s):
    hT = s.hT

    def cols(dst, width=2):
        w = c.weights(c.tensor)
        i, src, m = c.product_cols(hT, w, range(KT), width)
        c.release(m)
        c.read(i, c.copy(dst, src, m, q=c.scalar))

    def rows(dst, width=256):
        w = c.weights(c.tensor)
        i, src, m = c.product_rows(hT, w, range(KT), width)
        c.release(m)
        c.read(i, c.copy(dst, src, m))

    cols(s.qT)
    cols(s.kT)
    rows(s.vq[:, :, 0:256])
    rows(s.vq[:, :, 256:512])
    rows(s.lora, LORA)
    rows(s.z[:, :, 0:256])
    rows(s.z[:, :, 256:512])
    for j in range(3):
        cols(s.xbc[:, 2 * j:2 * j + 2, 3:3 + SEQ])
    i, bank = c.bank()
    for t in range(TT):
        for k in range(KT):
            ins = c.mm(bank[:, t * 8:t * 8 + 8], hT[:, k, t * P:(t + 1) * P], s.w_dt[:, k, :], k == 0, k == KT - 1)
    m = c.tensor.did(ins)
    c.read(i, c.copy(s.dt, bank[:, 0:16].rearrange("p (t h) -> p t h", t=TT), m))


def diff_attention(c, a, l, s, y):
    nc, lam = c.nc, s.lam
    for j in range(2):
        m = c.sumsq(lam[:, j:j + 1], s.lp[:, 2 * j, :], s.lp[:, 2 * j + 1, :], s.lp_work, c.small.last)
    m = c.act(lam[:, 2:4], lam[:, 0:2], ACT.Exp, m)
    m = c.stt(lam[:, 4:5], lam[:, 2:3], s.lam_init[:, 0:1], lam[:, 3:4], ALU.add, ALU.subtract, m)
    m = c.ts(lam[:, 4:5], lam[:, 4:5], -1.0, None, ALU.mult, None)
    scores, total, negmax = c.carve(8, SEQ), c.carve(8), c.carve(8)
    pT = s.pT
    work = c.carve(256)
    pv_done = None
    for t in range(TT):
        keys = P * (t + 1)
        c.tensor.wait(c.scalar.last)
        for r in range(4):
            i, bank = c.bank()
            for e in range(2):
                ins = c.mm(bank[:, e * SEQ:e * SEQ + keys], s.qT[32 * r:32 * r + 32, e, t * P:(t + 1) * P],
                           s.kT[32 * r:32 * r + 32, e, 0:keys])
            m = c.tensor.did(ins)
            src = bank[:, :].rearrange("p (e k) -> p e k", e=2)[:, :, 0:keys]
            mask = c.chunk_mask[:, t:t + 1, 0:keys].to_broadcast([P, 2, keys])
            both = scores[:, :, :].rearrange("p (e r) k -> p e r k", e=2)[:, :, r, 0:keys]
            m = c.stt(both, src, 32 ** -0.5, mask, ALU.mult, ALU.add, m, pv_done)
            c.read(i, m)
        m = c.softmax_exp(scores, negmax, total, 8, keys, m)
        pair = total[:, :].rearrange("p (h e) -> p h e", e=2)
        m = c.ts(pair[:, :, 1], pair[:, :, 1], lam[:, 4:5], None, ALU.mult, None)
        sc = scores[:, :, 0:keys]
        m = c.tt(sc, sc, total[:, 0:8].unsqueeze(2).to_broadcast([P, 8, keys]), ALU.mult)
        two = scores[:, :, :].rearrange("p (h e) k -> p h e k", e=2)
        m = c.tt(two[:, :, 0, 0:keys], two[:, :, 0, 0:keys], two[:, :, 1, 0:keys], ALU.add)
        done = c.transpose_maps(pT, two[:, :, 0, :], 4, t, c.identity, m)
        pv_done = c.tensor.last
        c.tensor.wait(*done, c.vector.last)
        i, bank = c.bank()
        for h in range(4):
            for kt in range(t + 1):
                ins = c.mm(bank[:, h * 64:(h + 1) * 64], pT[:, h, kt, t * P:(t + 1) * P],
                           s.vq[:, kt, h * 64:(h + 1) * 64], kt == 0, kt == t)
        m = c.tensor.did(ins)
        yt = y[:, t, 0:256]
        m = c.copy(yt, bank[:, 0:256], m)
        c.read(i, m)
        m = c.tt(work, yt, yt, ALU.mult, m)
        m = c.reduce(total[:, 0:4], work[:, :].rearrange("p (h e) -> p h e", h=4), ALU.add, m)
        m = c.rsqrt(total[:, 0:4], total[:, 0:4], 64, 1e-5, m)
        yh = yt.rearrange("p (h e) -> p h e", h=4)
        m = c.tt(yh, yh, total[:, 0:4].unsqueeze(2).to_broadcast([P, 4, 64]), ALU.mult, m)
        m = c.tt(yh, yh, s.subln.unsqueeze(1).to_broadcast([P, 4, 64]), ALU.mult, m)
        m = c.ts(yt, yt, s.lam_init[:, 1:2], None, ALU.mult, None)
    return m


def latent_attention(c, a, l, s, yT):
    cq, lora = s.vq, s.lora
    small, work = c.carve(8), c.carve(TT, 384)
    for t in range(TT):
        m = c.sumsq(small[:, t:t + 1], cq[:, t, 256:512], cq[:, t, 256:512], work[:, t, 0:256])
        m = c.sumsq(small[:, 2 + t:3 + t], lora[:, t, 0:128], lora[:, t, 0:128], work[:, t, 0:128])
    c.rsqrt(small[:, 0:2], small[:, 0:2], 256, 1e-6)
    m = c.rsqrt(small[:, 2:4], small[:, 2:4], 128, 1e-6)
    latT = c.carve(3, SEQ)
    for t in range(TT):
        c.ts(work[:, t, 0:256], cq[:, t, 256:512], small[:, t:t + 1], None, ALU.mult, None)
        m = c.ts(work[:, t, 256:384], lora[:, t, 0:128], small[:, 2 + t:3 + t], None, ALU.mult, None)
    done = c.columns_from_rows(latT, work, c.identity, 3,
                               lambda k, out, src, mark: c.ts(out, src, s.vec[:, V_QN + k:V_QN + k + 1], None,
                                                              ALU.mult, None, mark), m)
    q_rows, k_rows, v_rows = c.carve(TT, 4, 96), c.carve(TT, 4, 96), c.carve(TT, 256)
    qraw, kvraw, half = c.carve(384), c.carve(512), c.carve(4, 16)
    c.tensor.wait(*done)
    for t in range(TT):
        i, bank = c.bank()
        for k in range(2):
            ins = c.mm(bank[:, 0:384], latT[:, k, t * P:(t + 1) * P], s.w_uq[:, k, :], k == 0, k == 1)
        m = c.tensor.did(ins)
        m = c.copy(qraw, bank[:, 0:384], m)
        c.read(i, m)
        qh = qraw[:, :].rearrange("p (h e) -> p h e", h=4)
        c.copy(q_rows[:, t, :, 0:64], qh[:, :, 0:64])
        rope(c, q_rows[:, t, :, 64:96], qh[:, :, 64:96], t, 4, None, half)
        i, bank = c.bank()
        m = c.tensor.did(c.mm(bank, latT[:, 2, t * P:(t + 1) * P], s.w_ukv))
        m = c.copy(kvraw, bank, m)
        c.read(i, m)
        kh = kvraw[:, :].rearrange("p (h e) -> p h e", h=4)
        c.copy(k_rows[:, t, :, 0:64], kh[:, :, 0:64])
        c.copy(v_rows[:, t, :].rearrange("p (h e) -> p h e", h=4), kh[:, :, 64:128])
        kr = lora[:, t:t + 1, 128:160]
        rope(c, k_rows[:, t, 0:1, 64:96], kr, t, 1, None, half[:, 0:1, :])
        m = c.copy(k_rows[:, t, 1:4, 64:96], k_rows[:, t, 0:1, 64:96].to_broadcast([P, 3, 32]))
    qT, kT = c.carve(4, SEQ), c.carve(4, SEQ)
    c.tensor.wait(m)
    done = []
    for src, dst in ((q_rows, qT), (k_rows, kT)):
        for h in range(0, 4, 2):
            i, bank = c.bank()
            for e in range(2):
                for t in range(TT):
                    n = (e * TT + t) * P
                    ins = c.nc.tensor.transpose(bank[0:96, n:n + P], src[:, t, h + e, :], c.identity)
            m = c.tensor.did(ins)
            d = c.copy(dst[0:96, h:h + 2, :], bank[0:96, :].rearrange("p (h s) -> p h s", h=2), m, q=c.scalar)
            c.read(i, d)
            done.append(d)
    scores, total, negmax = c.carve(4, SEQ), c.carve(4), c.carve(4)
    pT = s.pT2
    c.tensor.wait(*done)
    pv_done = None
    for t in range(TT):
        keys = P * (t + 1)
        for h in range(0, 4, 2):
            i, bank = c.bank()
            for e in range(2):
                ins = c.mm(bank[:, e * SEQ:e * SEQ + keys], qT[0:96, h + e, t * P:(t + 1) * P], kT[0:96, h + e, 0:keys])
            m = c.tensor.did(ins)
            src = bank[:, :].rearrange("p (e k) -> p e k", e=2)[:, :, 0:keys]
            mask = c.chunk_mask[:, t:t + 1, 0:keys].to_broadcast([P, 2, keys])
            m = c.stt(scores[:, h:h + 2, 0:keys], src, 96 ** -0.5, mask, ALU.mult, ALU.add, m, pv_done)
            c.read(i, m)
        m = c.softmax_exp(scores, negmax, total, 4, keys, m)
        sc = scores[:, :, 0:keys]
        m = c.tt(sc, sc, total[:, 0:4].unsqueeze(2).to_broadcast([P, 4, keys]), ALU.mult, m)
        done = c.transpose_maps(pT, scores, 4, t, c.identity, m)
        pv_done = c.tensor.last
        c.tensor.wait(*done)
    return heads_out(c, yT, 2, pT, v_rows, 4)


def heads_out(c, yT, tile0, pT, v_rows, heads):
    done = []
    for h0 in range(0, heads, 4):
        i, bank = c.bank()
        for h in range(h0, h0 + 4):
            r, col = 64 * (h % 2), ((h - h0) // 2) * SEQ
            for t in range(TT):
                for kt in range(t + 1):
                    ins = c.mm(bank[r:r + 64, col + t * P:col + (t + 1) * P], v_rows[:, kt, h * 64:(h + 1) * 64],
                               pT[:, h, kt, t * P:(t + 1) * P], kt == 0, kt == t)
        m = c.tensor.did(ins)
        d = c.copy(yT[:, tile0 + h0 // 2:tile0 + h0 // 2 + 2, :], bank[:, :].rearrange("p (k s) -> p k s", k=2), m)
        c.read(i, d)
        done.append(d)
    return done


def log1p_positive(c, out, e, z, zz, *marks):
    m = c.ts(z, e, 2.0, None, ALU.add, None, *marks)
    m = c.recip(z, z)
    m = c.tt(z, z, e, ALU.mult)
    m = c.tt(zz, z, z, ALU.mult)
    m = c.ts(out, zz, 1.0 / 15, 1.0 / 13, ALU.mult, ALU.add)
    for n in (11, 9, 7, 5, 3, 1):
        m = c.tt(out, out, zz, ALU.mult)
        m = c.ts(out, out, 1.0 / n, None, ALU.add, None)
    m = c.tt(out, out, z, ALU.mult)
    return c.ts(out, out, 2.0, None, ALU.mult, None)


def state_space(c, a, l, s, y):
    conv = c.carve(6, SEQ)
    for r in range(6):
        w = lambda j: s.vec[:, V_CONV_W + 6 * j + r:V_CONV_W + 6 * j + r + 1]
        m = c.ts(conv[:, r, :], s.xbc[:, r, 0:SEQ], w(0), None, ALU.mult, None, c.scalar.last, c.gpsimd.last)
        for j in range(1, 4):
            m = c.stt(conv[:, r, :], s.xbc[:, r, j:j + SEQ], w(j), conv[:, r, :], ALU.mult, ALU.add)
        ms = c.act(conv[:, r, :], conv[:, r, :], ACT.Silu, m, bias=s.vec[:, V_CONV_B + r:V_CONV_B + r + 1])
    xs = c.carve(TT, 512)
    dt, da, e, z, zz, n = (c.carve(TT, 8) for _ in range(6))
    bias = s.dt_bias.unsqueeze(1).to_broadcast([P, TT, 8])
    m = c.tt(dt, s.dt, bias, ALU.add, c.small.last)
    m = c.ts(n, dt, -1.0, None, ALU.mult, None)
    m = c.tt(n, dt, n, ALU.min)
    m = c.act(e, n, ACT.Exp, m)
    m = log1p_positive(c, da, e, z, zz, m)
    m = c.stt(dt, dt, 0.0, da, ALU.max, ALU.add)
    neg_a = c.carve(8)
    ma = c.act(neg_a, s.a_log, ACT.Exp, c.small.last)
    m = c.stt(da, dt, -1.0, neg_a.unsqueeze(1).to_broadcast([P, TT, 8]), ALU.mult, ALU.mult, ma)
    wide = c.carve(TT, 8, P)
    m = c.copy(wide, da.unsqueeze(3).to_broadcast([P, TT, 8, P]), m)
    c.tensor.wait(m, c.gpsimd.last)
    i, bank = c.bank()
    for t in range(TT):
        for u in range(t + 1):
            ins = c.mm(bank[:, t * 8:t * 8 + 8], c.causal[:, u, t * P:(t + 1) * P], da[:, u, :], u == 0, u == t)
    m = c.tensor.did(ins)
    sum_col = c.carve(TT, 8)
    m = c.copy(sum_col, bank[:, 0:16].rearrange("p (t h) -> p t h", t=TT), m)
    c.read(i, m)
    bc = c.carve(TT * 2, SEQ)
    c.tensor.wait(ms)
    for g in range(2):
        i, bank = c.bank()
        for t in range(TT):
            ins = c.mm(bank[:, t * SEQ:(t + 1) * SEQ], conv[64 * g:64 * g + 64, 4, t * P:(t + 1) * P],
                       conv[64 * g:64 * g + 64, 5, :])
        m = c.tensor.did(ins)
        m = c.tt(bc[:, :, :].rearrange("p (t g) s -> p t g s", g=2)[:, :, g, :],
                 bank[:, :].rearrange("p (t s) -> p t s", t=TT), c.causal, ALU.mult, m)
        c.read(i, m)
    for t in range(TT):
        i, bank = c.bank()
        for k in range(4):
            ins = c.nc.tensor.transpose(bank[:, k * P:(k + 1) * P], conv[:, k, t * P:(t + 1) * P], c.identity)
        m = c.tensor.did(ins)
        c.read(i, c.copy(xs[:, t, :], bank, m, q=c.scalar))
    xd = c.carve(TT, 512)
    for t in range(TT):
        m = c.tt(xd[:, t, :].rearrange("p (h e) -> p h e", h=8), xs[:, t, :].rearrange("p (h e) -> p h e", h=8),
                 dt[:, t, :].unsqueeze(2).to_broadcast([P, 8, 64]), ALU.mult, c.scalar.last)
    mix = c.carve(16, SEQ)
    ready = [None] * 4
    for h in range(8):
        i, bank = c.bank()
        for u in range(TT):
            ins = c.mm(bank[:, 0:SEQ], wide[:, u, h, :], c.causal[:, u, :], u == 0, u == 1)
        m = c.tensor.did(ins)
        for t in range(TT):
            m1 = c.ts(mix[:, 2 * h + t, :], bank[:, 0:SEQ], sum_col[:, t, h:h + 1], 0.0, ALU.subtract, ALU.min, m)
        c.read(i, m1)
        m = c.act(mix[:, 2 * h:2 * h + 2, :], mix[:, 2 * h:2 * h + 2, :], ACT.Exp, m1)
        for t in range(TT):
            m = c.tt(mix[:, 2 * h + t, :], mix[:, 2 * h + t, :], bc[:, 2 * t + h // 4, :], ALU.mult, m)
    c.tensor.wait(m)
    work = c.carve(512)
    small = c.carve(2)
    for t in range(TT):
        i, bank = c.bank()
        for h in range(8):
            for u in range(t + 1):
                ins = c.mm(bank[:, h * 64:(h + 1) * 64], mix[:, 2 * h + u, t * P:(t + 1) * P],
                           xd[:, u, h * 64:(h + 1) * 64], u == 0, u == t)
        m = c.tensor.did(ins)
        out = y[:, t, 512:1024]
        m0 = c.tt(work[:, :].rearrange("p (h e) -> p h e", h=8), xs[:, t, :].rearrange("p (h e) -> p h e", h=8),
                  s.d_skip.unsqueeze(2).to_broadcast([P, 8, 64]), ALU.mult)
        m = c.tt(out, bank, work, ALU.add, m)
        c.read(i, m)
        mz = c.act(s.z[:, t, :], s.z[:, t, :], ACT.Silu, m0)
        m = c.tt(out, out, s.z[:, t, :], ALU.mult, mz)
        m = c.tt(work, out, out, ALU.mult)
        m = c.reduce(small, work[:, :].rearrange("p (g e) -> p g e", g=2), ALU.add)
        m = c.rsqrt(small, small, 256, 1e-6, m)
        og = out.rearrange("p (g e) -> p g e", g=2)
        m = c.tt(og, og, small.unsqueeze(2).to_broadcast([P, 2, 256]), ALU.mult, m)
        m = c.tt(out, out, s.ssm_norm, ALU.mult)
    return m


def add_gated(c, x, y, gate, small, junk, *marks):
    for t in range(TT):
        m = c.sumsq(small[:, t:t + 1], y[:, t, :], y[:, t, :], junk, *marks)
    m = c.rsqrt(small[:, 0:TT], small[:, 0:TT], D, 1e-6, m)
    for t in range(TT):
        m = c.stt(y[:, t, :], y[:, t, :], small[:, t:t + 1], gate, ALU.mult, ALU.mult, m)
        m = c.tt(x[:, t, :], x[:, t, :], y[:, t, :], ALU.add)
    return m


class State:
    pass


def first_block(c, a, x):
    nc = c.nc
    s = State()
    first_constants(c)
    s.hT = c.hT
    s.vec, s.mod = c.keep("vectors", V_ROWS), c.keep("modulation", 48)
    s.in_scale_m, s.in_scale_f = c.keep("scale_m", 8), c.keep("scale_f", 8)
    s.gate_m, s.gate_f = c.keep("gate_m", D), c.keep("gate_f", D)
    s.lam_init = c.keep("lambda_init", 2)
    rope_tables(c, a)
    c.restart()
    with nc.Fori(0, DEPTH) as l:
        c.plan(layer_pieces(a, l))
        s.norm1, s.norm3 = c.carve(D), c.carve(D)
        modulation(c, a, l, s)
        c.restart()

        work, small = c.carve(TT, D), c.carve(4)
        s.lam = c.carve(5)
        s.qT, s.kT = c.carve(2, SEQ), c.carve(2, SEQ)
        s.vq, s.lora, s.z = c.carve(TT, 512), c.carve(TT, LORA), c.carve(TT, 512)
        s.xbc, s.dt = c.carve(6, 3 + SEQ), c.carve(TT, 8)
        s.w_dt, s.w_uq, s.w_ukv = c.carve(KT, 8), c.carve(2, 384), c.carve(512)
        s.lp, s.lp_work, s.subln = c.carve(4, 32), c.carve(32), c.carve(64)
        s.d_skip, s.dt_bias, s.a_log, s.ssm_norm = c.carve(8), c.carve(8), c.carve(8), c.carve(512)
        row = lambda name: a[name][bass.ds(l, 1)]
        load = lambda dst, src: c.small.load(nc.scalar, dst, src)
        load(s.w_dt, row("w_in")[:, :, OFF_DT:OFF_DT + 8].rearrange("a (k p) n -> p (a k) n", p=P))
        load(s.w_uq, row("w_uq").rearrange("a (k p) n -> p (a k) n", p=P))
        load(s.w_ukv, row("w_ukv").rearrange("a p n -> (a p) n"))
        load(s.lp, row("diff_lambda").to_broadcast([P, 4, 32]))
        load(s.subln, row("diff_subln_g").to_broadcast([P, 64]))
        for dst, name, n in ((s.d_skip, "d_skip", 8), (s.dt_bias, "dt_bias", 8), (s.a_log, "a_log", 8),
                             (s.ssm_norm, "ssm_norm_g", 512)):
            load(dst, row(name).to_broadcast([P, n]))
        m = c.copy(s.lam_init, c.lam_table[:, bass.ds(l, 1), :].rearrange("p a n -> p (a n)"))
        c.fill(s.xbc[:, :, 0:3], 0.0, q=c.gpsimd)
        done = normed_cols(c, s.hT, x, s.in_scale_m, s.mod[:, 0:8], work, small)
        c.tensor.wait(c.small.last, *done)
        projections(c, a, l, s)
        mark = c.carved
        y, yT = work, s.hT
        s.pT = c.arena[:, ARENA - 4 * 2 * SEQ:ARENA].rearrange("p (h k s) -> p h k s", h=4, k=2)
        s.pT2 = s.pT
        diff_attention(c, a, l, s, y)
        c.restart()
        c.carved = mark
        state_space(c, a, l, s, y)
        c.restart()
        c.carved = mark
        d0 = latent_attention(c, a, l, s, yT)
        d1 = c.columns_from_rows(yT[:, 0:2, :], y[:, :, 0:256], c.identity, 2, None)
        d2 = c.columns_from_rows(yT[:, 4:8, :], y[:, :, 512:1024], c.identity, 4, None)
        c.tensor.wait(*d0, *d1, *d2)
        out_rows(c, s.hT, y, 1)
        add_gated(c, x, y, s.gate_m, small, c.arena[:, ARENA - D:ARENA])
        c.restart()

        work, small = c.carve(TT, D), c.carve(4)
        uT = c.carve(FF // P, SEQ)
        done = normed_cols(c, s.hT, x, s.in_scale_f, s.mod[:, 24:32], work, small)
        c.tensor.wait(*done)
        for n in range(FF // 256):
            w = c.weights(c.tensor)
            i, src, m = c.product_cols(s.hT, w, range(KT))
            c.release(m)
            m = c.act(uT[:, 2 * n:2 * n + 2, :], src, ACT.Relu, m)
            c.read(i, m)
            m = c.tt(uT[:, 2 * n:2 * n + 2, :], uT[:, 2 * n:2 * n + 2, :], uT[:, 2 * n:2 * n + 2, :], ALU.mult, m)
        c.tensor.wait(m)
        out_rows(c, uT, work, FF // D)
        add_gated(c, x, work, s.gate_f, small, c.arena[:, ARENA - D:ARENA])
        c.restart(ring=True)


def out_rows(c, inT, out, pieces):
    for n in range(4):
        pair = [c.bank() for _ in range(TT)]
        for p in range(pieces):
            w = c.weights(c.tensor)
            for t in range(TT):
                for k in range(KT):
                    ins = c.mm(pair[t][1][:, 0:256], inT[:, p * KT + k, t * P:(t + 1) * P], w[:, k, :],
                               p == 0 and k == 0, p == pieces - 1 and k == KT - 1)
            m = c.tensor.did(ins)
            c.release(m)
        for t in range(TT):
            c.read(pair[t][0], c.copy(out[:, t, n * 256:(n + 1) * 256], pair[t][1][:, 0:256], m,
                                      q=c.scalar if t else c.vector))
    c.vector.wait(c.scalar.last)


C = 32
N_CHUNK = SEQ // C
OFF_MOBA, OFF_SSM, OFF_GATE = 1792, 3328, 3840
HEADS = 8
ALPHA = 2.0 ** 0.25
VECTORS_2 = [("rwkv_mu_2", 14), ("rwkv_w0_2", 4), ("rwkv_a0_2", 4), ("rwkv_k_k_2", 4), ("rwkv_k_a_2", 4),
             ("rwkv_r_k_2", 4), ("rwkv_ln_w_2", 4), ("rwkv_ln_b_2", 4), ("ssm_d_2", 4), ("ssm_glu_b_2", 8),
             ("gate_b_2", 24), ("ssm_a_re_2", 16), ("ssm_a_im_2", 16), ("ssm_log_dt_2", 16)]


def second_pieces(a):
    w_in = a["w_in_2"].rearrange("a (k p) n -> p (a k) n", p=P)
    col = lambda off: (k_tiles(KT), w_in[:, :, off:off + 256])
    half = lambda w, n: (k_tiles(4, 512), a[w].rearrange("a (k p) n -> p (a k) n", p=P)[:, :, n * 512:(n + 1) * 512])
    gate = lambda branch: [col(OFF_GATE + D * branch + 256 * n) for n in range(4)]
    up = lambda name: [half(name, n) for n in range(2)]
    pieces = [col(256 * n) for n in range(7)] + gate(0) + up("w_up_rwkv_2")
    pieces += [col(OFF_MOBA + 256 * n) for n in range(6)] + gate(1) + up("w_up_moba_2")
    pieces += [col(OFF_SSM + 256 * n) for n in range(2)] + gate(2) + up("ssm_glu_w_2") + up("w_up_ssm_2")
    w_out = a["w_out_2"].rearrange("a (k p) n -> p (a k) n", p=P)
    return pieces + [(k_tiles(KT), w_out[:, :, n * 256:(n + 1) * 256]) for n in range(4)]


def second_constants(c, s):
    g = c.gpsimd

    def select(out, cmp, fill, base, pattern, channel):
        return g.did(g.after().affine_select(out=out, in_=out, compare_op=cmp, fill=fill, base=base,
                                             pattern=pattern, channel_multiplier=channel))
    s.distance = c.keep("distance", TT, SEQ)
    for t in range(TT):
        g.did(g.after().iota(s.distance[:, t, :], pattern=[[-1, SEQ]], base=t * P, channel_multiplier=1,
                             allow_small_or_imprecise_dtypes=True))
        select(s.distance[:, t, :], ALU.is_ge, 1e34, t * P, [[-1, SEQ]], 1)
    s.pair = c.keep("pair_masks", 5, P)
    c.fill(s.pair, 1.0, q=g)
    for kind, block in ((0, C), (1, C), (2, C), (3, 16), (4, 16)):
        for b in range(P // block):
            part = s.pair[:, kind, b * block:(b + 1) * block]
            if kind in (0, 3):
                select(part, ALU.is_gt, 0.0, b * block, [[1, block]], -1)
                select(part, ALU.is_ge, 0.0, -b * block, [[0, block]], 1)
            elif kind == 1:
                select(part, ALU.is_ge, 0.0, b * block, [[1, block]], -1)
                select(part, ALU.is_ge, 0.0, -b * block, [[0, block]], 1)
            else:
                select(part, ALU.is_gt, 0.0, -b * block, [[-1, block]], 1)
                select(part, ALU.is_ge, 0.0, (b + 1) * block - 1, [[0, block]], -1)
    s.chunk_start = c.keep("chunk_start", 4 * SEQ)
    c.fill(s.chunk_start, 1.0, q=g)
    c.fill(s.chunk_start[:, :].rearrange("p (n c) -> p n c", c=C)[:, :, 0:1], 0.0, q=g)
    s.time = c.keep("time", SEQ)
    g.did(g.after().iota(s.time, pattern=[[1, SEQ]], base=0, channel_multiplier=0,
                         allow_small_or_imprecise_dtypes=True))
    number, s.group_odd = c.keep("channel_number", 1, dtype=I32), c.keep("group_odd", 2)
    m = g.did(g.after().iota(number, pattern=[[0, 1]], base=0, channel_multiplier=1))
    m = c.ts(number, number, 4, 1, ALU.arith_shift_right, ALU.bitwise_and, m)
    m = c.copy(s.group_odd[:, 1:2], number, m)
    c.ts(s.group_odd[:, 0:1], s.group_odd[:, 1:2], -1.0, 1.0, ALU.mult, ALU.add)


def vectors_2(c, a, s):
    rows, s.v = c.carve(P), {}
    s.log_dt, each = c.keep("log_dt", 16), c.carve(16, 2)
    c.small.load(c.nc.scalar, each, a["ssm_log_dt_2"].rearrange("a (i e) -> a i e", e=2).to_broadcast([P, 16, 2]))
    n0 = 0
    for name, n in VECTORS_2:
        if name == "ssm_log_dt_2":
            continue
        flat = a[name]
        if name == "rwkv_r_k_2":
            flat = flat.rearrange("a h e -> a (h e)")
        elif name in ("ssm_a_re_2", "ssm_a_im_2"):
            flat = flat.rearrange("a g e -> a (g e)")
        flat = flat.rearrange("a (r p) -> (a r) p", p=P)
        c.small.load(c.nc.scalar, rows[n0:n0 + n, :], flat)
        s.v[name] = s.columns[:, n0:n0 + n]
        n0 += n
    c.tensor.wait(c.small.last, c.gpsimd.last)
    i, bank = c.bank()
    m = c.tensor.did(c.nc.tensor.transpose(bank[:, 0:n0], rows[0:n0, :], c.identity[0:n0, 0:n0]))
    c.read(i, c.copy(s.columns[:, 0:n0], bank[:, 0:n0], m))
    for e in range(2):
        c.copy(s.log_dt[64 * e:64 * e + 64, :], each[64 * e:64 * e + 64, :, e], c.small.last)


def rwkv_input(c, a, s, z):
    col = lambda name, k: s.v[name][:, k:k + 1]
    s.rwkv_gate, s.bonus = c.carve(4, SEQ), c.carve(4, SEQ)
    s.AR = c.carve(4, TT, 2 * P)
    s.b, s.k, s.bend, s.kend, s.chunk_decay = (c.carve(4, SEQ), c.carve(4, SEQ), c.carve(4, SEQ), c.carve(4, SEQ),
                                               c.carve(4, N_CHUNK))
    s.v_cols = c.carve(4, SEQ)
    s.rwkv_end = c.carved
    s.lora_w, s.g2 = c.carve(512), c.carve(512)
    c.small.load(c.nc.scalar, s.lora_w[0:64, :], a["rwkv_w2_2"][0, :, :])
    c.small.load(c.nc.scalar, s.lora_w[64:P, :], a["rwkv_a2_2"][0, :, :])
    c.small.load(c.nc.scalar, s.g2, a["rwkv_g2_2"][0, :, :])
    r, k_, low, gate_in, tmp = c.carve(4, SEQ), c.carve(4, SEQ), c.carve(SEQ), c.carve(SEQ), c.carve(SEQ)
    v = s.v_cols
    shifted = [part[:, n, :] for part in (r, k_, v) for n in range(4)] + [low, gate_in]
    for k in range(14):
        m = c.tt(tmp, z[:, k, 0:SEQ], z[:, k, 1:SEQ + 1], ALU.subtract, c.scalar.last, c.gpsimd.last)
        m = c.stt(shifted[k], tmp, col("rwkv_mu_2", k), z[:, k, 1:SEQ + 1], ALU.mult, ALU.add)
    m = c.act(low[0:64, :], low[0:64, :], ACT.Tanh, m)
    m = c.act(gate_in, gate_in, ACT.Sigmoid, m)
    c.tensor.wait(m, c.vector.last, c.small.last)
    logw, icl = c.carve(4, SEQ), c.carve(4, SEQ)
    for k in range(4):
        for out, r0, bias in ((logw, 0, "rwkv_w0_2"), (icl, 64, "rwkv_a0_2")):
            i, bank = c.bank()
            m = c.tensor.did(c.mm(bank[:, 0:SEQ], s.lora_w[r0:r0 + 64, k * P:(k + 1) * P], low[r0:r0 + 64, :]))
            c.read(i, c.act(out[:, k, :], bank[:, 0:SEQ], ACT.Sigmoid, m, bias=col(bias, k)))
        i, bank = c.bank()
        m = c.tensor.did(c.mm(bank[:, 0:SEQ], s.g2[:, k * P:(k + 1) * P], gate_in))
        c.read(i, c.copy(s.rwkv_gate[:, k, :], bank[:, 0:SEQ], m, q=c.scalar))
    c.ts(logw, logw, -math.exp(-0.5), None, ALU.mult, None, c.scalar.last)
    kk, work, ka = c.carve(4, SEQ), c.carve(4, SEQ), c.carve(4, SEQ)
    for k in range(4):
        m = c.ts(kk[:, k, :], k_[:, k, :], col("rwkv_k_k_2", k), None, ALU.mult, None)
    m = c.tt(work, kk, kk, ALU.mult)
    c.tensor.wait(m)
    for k in range(0, 4, 2):
        i, bank = c.bank()
        m = c.tensor.did(c.mm(bank, c.head_sum, work[:, k:k + 2, :].rearrange("p k s -> p (k s)")))
        m = c.ts(ka[:, k:k + 2, :], bank[:, :].rearrange("p (k s) -> p k s", k=2), 1e-24, None, ALU.max, None, m)
        c.read(i, m)
    m = c.act(ka, ka, ACT.Sqrt, m)
    m = c.recip(ka, ka, m)
    m = c.tt(kk, kk, ka, ALU.mult)
    for k in range(4):
        m = c.ts(ka[:, k, :], icl[:, k, :], -1.0, col("rwkv_k_a_2", k), ALU.add, ALU.mult)
    m = c.stt(k_, ka, 1.0, k_, ALU.add, ALU.mult)
    for k in range(4):
        m = c.stt(work[:, k, :], r[:, k, :], col("rwkv_r_k_2", k), k_[:, k, :], ALU.mult, ALU.mult, c.tensor.last)
    c.tensor.wait(m)
    for k in range(0, 4, 2):
        i, bank = c.bank()
        m = c.tensor.did(c.mm(bank, c.head_sum, work[:, k:k + 2, :].rearrange("p k s -> p (k s)")))
        m = c.tt(s.bonus[:, k:k + 2, :], bank[:, :].rearrange("p (k s) -> p k s", k=2), v[:, k:k + 2, :], ALU.mult, m)
        c.read(i, m)
    run = c.carve(4, SEQ)
    flat = lambda t: t.rearrange("p k s -> p (k s)")
    v1 = c.vector
    m = v1.did(v1.after().tensor_tensor_scan(flat(run), s.chunk_start, flat(logw), 0.0, ALU.mult, ALU.add))
    part = lambda n: s.AR[:, :, :, n * P:(n + 1) * P].rearrange("p k t s -> p (k t) s")
    tiled = lambda t: t.rearrange("p k (t s) -> p (k t) s", t=TT)
    m = c.tt(work, run, logw, ALU.subtract, c.tensor.last)
    m = c.act(work, work, ACT.Exp, m)
    m = c.stt(part(0), tiled(kk), -1.0, tiled(work), ALU.mult, ALU.mult, m)
    m = c.act(work, run, ACT.Exp, m)
    m = c.tt(part(1), tiled(r), tiled(work), ALU.mult, m)
    chunks = lambda t: t.rearrange("p k (n c) -> p (k n) c", c=C)
    m = c.copy(s.chunk_decay[:, :, :].rearrange("p k n -> p (k n)"), chunks(work)[:, :, C - 1])
    m = c.act(work, run, ACT.Exp, m, scale=-1.0)
    c.tt(kk, kk, icl, ALU.mult)
    m = c.tt(s.b, kk, work, ALU.mult, m)
    m = c.tt(s.k, k_, work, ALU.mult)
    m = c.tt(chunks(work), chunks(run)[:, :, C - 1:C].to_broadcast([P, 4 * N_CHUNK, C]), chunks(run), ALU.subtract)
    m = c.act(work, work, ACT.Exp, m)
    m = c.tt(s.bend, kk, work, ALU.mult, m)
    m = c.tt(s.kend, k_, work, ALU.mult)
    return m


def rwkv_scan(c, s, yT):
    nc, I = c.nc, c.identity
    eight = c.scalar, c.vector
    state = c.carve(4, 64)
    m = c.fill(state, 0.0)
    for t in range(TT):
        rows = {}
        inner = c.carved
        W = c.carve(HEADS, P)
        for n, name in enumerate(("a", "bend", "kend", "v")):
            src = {"bend": s.bend, "kend": s.kend, "v": s.v_cols}.get(name)
            c.tensor.wait(c.vector.last)
            i, bank = c.bank()
            for k in range(4):
                part = s.AR[:, k, t, 0:P] if name == "a" else src[:, k, t * P:(t + 1) * P]
                ins = nc.tensor.transpose(bank[:, k * P:(k + 1) * P], part, I)
            m = c.tensor.did(ins)
            heads = bank[:, :].rearrange("p (h e) -> p h e", h=HEADS)
            rows[name] = W[:, :, 0:64] if name == "a" else c.carve(HEADS, 64)
            c.read(i, c.copy(rows[name], heads, m, q=eight[n % 2]))
        G, N, PP = c.carve(HEADS, 4 * P), c.carve(HEADS, P), c.carve(HEADS, P)
        N1, P2, N2 = c.carve(HEADS, P), c.carve(HEADS, P), c.carve(HEADS, P)
        Z = c.carve(HEADS, P)
        for h in range(HEADS):
            k, r = h // 2, 64 * (h % 2)
            hs = slice(r, r + 64)
            tok = slice(t * P, (t + 1) * P)
            i, bank = c.bank()
            c.mm(bank[:, 0:2 * P], s.b[hs, k, tok], s.AR[hs, k, t, :])
            m = c.tensor.did(c.mm(bank[:, 2 * P:4 * P], s.k[hs, k, tok], s.AR[hs, k, t, :]))
            m = c.tt(G[:, h, :].rearrange("p (a b s) -> p a (b s)", a=2, b=2),
                     bank[:, :].rearrange("p (a s) -> p a s", a=2),
                     s.pair[:, 0:2, :].rearrange("p b s -> p (b s)").unsqueeze(1).to_broadcast([P, 2, 2 * P]),
                     ALU.mult, m)
            c.read(i, m)
            i, bank = c.bank()
            m = c.tensor.did(c.mm(bank[:, 0:P], s.AR[hs, k, t, 0:P], s.b[hs, k, tok]))
            m = c.tt(N1[:, h, :], bank[:, 0:P], s.pair[:, 2, :], ALU.mult, m)
            c.read(i, m)
        bc8 = lambda kind: s.pair[:, kind:kind + 1, :].to_broadcast([P, HEADS, P])
        m = c.tt(PP, G[:, :, 0:P], bc8(3), ALU.mult)
        m = c.tt(N, N1, bc8(4), ALU.mult)
        m = c.tt(Z, PP, I.unsqueeze(1).to_broadcast([P, HEADS, P]), ALU.add)
        m = c.tt(N1, N1, N, ALU.subtract)
        tensor_ready = m

        def per_head(out, left, right, combine=None, marks=()):
            c.tensor.wait(c.vector.last, c.scalar.last, *marks)
            done = []
            for h0 in range(0, HEADS, 4):
                i, bank = c.bank()
                for h in range(h0, h0 + 4):
                    ins = c.mm(bank[:, (h - h0) * P:(h - h0 + 1) * P], left[:, h, :], right[:, h, :])
                m = c.tensor.did(ins)
                src = bank[:, :].rearrange("p (h s) -> p h s", h=4)
                if combine is None:
                    d = c.copy(out[:, h0:h0 + 4, :], src, m, q=c.scalar)
                else:
                    d = c.tt(out[:, h0:h0 + 4, :], src, combine[:, h0:h0 + 4, :], ALU.add, m)
                c.read(i, d)
                done.append(d)
            return done
        p, n, p_next, n_next = PP, N, P2, N2
        for level in range(3):
            per_head(n_next, p, n)
            if level < 2:
                per_head(p_next, n, p)
            per_head(Z, n_next, Z, Z)
            p, n, p_next, n_next = p_next, n_next, p, n
        X, M = P2, N2
        c.tensor.wait(c.vector.last)
        for h0 in range(0, HEADS, 4):
            i, bank = c.bank()
            for h in range(h0, h0 + 4):
                ins = nc.tensor.transpose(bank[:, (h - h0) * P:(h - h0 + 1) * P], Z[:, h, :], I)
            m = c.tensor.did(ins)
            c.read(i, c.copy(X[:, h0:h0 + 4, :], bank[:, :].rearrange("p (h s) -> p h s", h=4), m, q=c.scalar))
        per_head(M, N1, Z)
        per_head(Z, X, M, Z)
        AK = G[:, :, 2 * P:3 * P]
        c.tensor.wait(c.vector.last)
        i, bank = c.bank()
        for h in range(HEADS):
            ins = c.mm(bank[:, h * 64:(h + 1) * 64], AK[:, h, :], rows["v"][:, h, :])
        m = c.tensor.did(ins)
        c.read(i, c.copy(W[:, :, 64:P], bank[:, :].rearrange("p (h e) -> p h e", h=HEADS), m))
        G12 = PP
        per_head(G12, Z, W)
        c.tensor.wait(c.scalar.last, c.vector.last)
        R2, Y0 = c.carve(4, P), c.carve(4, P)
        i, bank = c.bank()
        for h in range(HEADS):
            o = bank[64 * (h % 2):64 * (h % 2) + 64, (h // 2) * P:(h // 2 + 1) * P]
            ins = c.mm(o, G12[:, h, 0:64], G[:, h, P:2 * P])
        m = c.tensor.did(ins)
        m = c.tt(R2, bank[:, :].rearrange("p (k s) -> p k s", k=4), s.AR[:, :, t, P:2 * P], ALU.add, m)
        c.read(i, m)
        i, bank = c.bank()
        for h in range(HEADS):
            o = bank[64 * (h % 2):64 * (h % 2) + 64, (h // 2) * P:(h // 2 + 1) * P]
            c.mm(o, G12[:, h, 64:P], G[:, h, P:2 * P], True, False)
            ins = c.mm(o, rows["v"][:, h, :], G[:, h, 3 * P:4 * P], False, True)
        m = c.tensor.did(ins)
        c.read(i, c.copy(Y0, bank[:, :].rearrange("p (k s) -> p k s", k=4), m))
        n_here = P // C
        gain, states = (part.rearrange("p (n e) -> p n e", n=n_here) for part in
                        (c.arena[:, 0:n_here * 256], c.arena[:, n_here * 256:n_here * 512]))
        step = N1, P2, N2, Z
        for n in range(n_here):
            ts_ = slice(n * C, (n + 1) * C)
            decay = s.chunk_decay[:, :, t * n_here + n]
            m = c.tt(step[n][:, 0:4, :], I.unsqueeze(1).to_broadcast([P, 4, P]),
                     decay.unsqueeze(2).to_broadcast([P, 4, P]), ALU.mult, c.tensor.last)
            i, bank = c.bank()
            for h in range(HEADS):
                r, k = 64 * (h % 2), h // 2
                ins = c.mm(bank[r:r + 64, k * P + r:k * P + r + 64], G12[ts_, h, 0:64], rows["bend"][ts_, h, :])
            m = c.tensor.did(ins)
            for r in (0, 64):
                d = step[n][r:r + 64, 0:4, r:r + 64]
                b = bank[r:r + 64, :].rearrange("p (k s) -> p k s", k=4)[:, :, r:r + 64]
                m1 = c.tt(d, b, d, ALU.add, m)
            c.read(i, m1)
            i, bank = c.bank()
            for h in range(HEADS):
                r, k = 64 * (h % 2), h // 2
                o = bank[r:r + 64, k * 64:(k + 1) * 64]
                c.mm(o, rows["bend"][ts_, h, :], G12[ts_, h, 64:P], True, False)
                ins = c.mm(o, rows["kend"][ts_, h, :], rows["v"][ts_, h, :], False, True)
            m = c.tensor.did(ins)
            c.read(i, c.copy(gain[:, n, :], bank[:, 0:256], m, q=c.scalar))
        current = state[:, :, :].rearrange("p k e -> p (k e)")
        for n in range(n_here):
            m = c.copy(states[:, n, :], current, c.scalar.last)
            c.tensor.wait(m)
            i, bank = c.bank()
            for k in range(4):
                ins = c.mm(bank[:, k * 64:(k + 1) * 64], step[n][:, k, :], states[:, n, k * 64:(k + 1) * 64])
            m = c.tensor.did(ins)
            m = c.tt(current, bank[:, 0:256], gain[:, n, :], ALU.add, m)
            c.read(i, m)
        pair_banks = [c.bank() for _ in range(2)]
        for n in range(n_here):
            for h in range(HEADS):
                r, k = 64 * (h % 2), h // 2
                o = pair_banks[h % 2][1][r:r + 64, k * P + n * C:k * P + (n + 1) * C]
                ins = c.mm(o, states[r:r + 64, n, k * 64:(k + 1) * 64], R2[r:r + 64, k, n * C:(n + 1) * C])
        m = c.tensor.did(ins)
        for e, (i, bank) in enumerate(pair_banks):
            r = 64 * e
            c.read(i, c.tt(yT[r:r + 64, :, t * P:(t + 1) * P], bank[r:r + 64, :].rearrange("p (k s) -> p k s", k=4),
                           Y0[r:r + 64, :, :], ALU.add, m))
        c.carved = inner
        c.vector.wait(c.tensor.last)
        c.scalar.wait(c.tensor.last, c.vector.last)


def rwkv_output(c, s, yT):
    col = lambda name, k: s.v[name][:, k:k + 1]
    work = c.carve(4, SEQ)

    def head_mean(src, out, sub):
        c.tensor.wait(c.vector.last)
        for k in range(0, 4, 2):
            i, bank = c.bank()
            m = c.tensor.did(c.mm(bank, c.head_sum, src[:, k:k + 2, :].rearrange("p k s -> p (k s)")))
            b = bank[:, :].rearrange("p (k s) -> p k s", k=2)
            if sub is not None:
                m = c.stt(out[:, k:k + 2, :], b, -1.0 / 64, sub[:, k:k + 2, :], ALU.mult, ALU.add, m)
            else:
                m = c.ts(out[:, k:k + 2, :], b, 1.0 / 64, 64e-5, ALU.mult, ALU.add, m)
            c.read(i, m)
        return m
    head_mean(yT, yT, yT)
    c.tt(work, yT, yT, ALU.mult)
    m = head_mean(work, work, None)
    m = c.act(work, work, ACT.Sqrt, m)
    m = c.recip(work, work, m)
    c.tt(yT, yT, work, ALU.mult)
    for k in range(4):
        m = c.ts(yT[:, k, :], yT[:, k, :], col("rwkv_ln_w_2", k), col("rwkv_ln_b_2", k), ALU.mult, ALU.add)
    c.tt(yT, yT, s.bonus, ALU.add)
    return c.tt(yT, yT, s.rwkv_gate, ALU.mult)


def add_branch(c, merged, gates, yT, first):
    tmp = c.branch_tmp
    c.tensor.wait(c.vector.last, c.scalar.last)
    for half in range(2):
        w = c.weights(c.tensor)
        for k in range(0, 4, 2):
            i, src, m = c.product_cols(yT, w[:, :, k * P:(k + 2) * P], range(4))
            f = 4 * half + k
            g = gates[:, f:f + 2, :]
            if first:
                d = c.tt(merged[:, f:f + 2, :], src, g, ALU.mult, m)
            else:
                d = c.tt(tmp, src, g, ALU.mult, m)
                c.tt(merged[:, f:f + 2, :], merged[:, f:f + 2, :], tmp, ALU.add, d)
            c.read(i, d)
        c.release(m)
    return c.vector.last


def moba(c, s, qkT, v_rows, yT):
    scores, total, negmax = c.carve(HEADS, SEQ), c.carve(HEADS), c.carve(HEADS)
    pT = c.pT8
    pv_done = None
    for t in range(TT):
        keys = P * (t + 1)
        for k in range(0, 4, 2):
            for e in range(2):
                i, bank = c.bank()
                hs = slice(64 * e, 64 * e + 64)
                for j in range(2):
                    ins = c.mm(bank[:, j * SEQ:j * SEQ + keys], qkT[hs, k + j, t * P:(t + 1) * P], qkT[hs, 4 + k + j, 0:keys])
                m = c.tensor.did(ins)
                for j in range(2):
                    h = 2 * (k + j) + e
                    m1 = c.ts(scores[:, h, 0:keys], s.distance[:, t, 0:keys], -2.0 ** -(h + 1), None, ALU.mult, None, m, pv_done)
                    m1 = c.stt(scores[:, h, 0:keys], bank[:, j * SEQ:j * SEQ + keys], 0.125, scores[:, h, 0:keys],
                               ALU.mult, ALU.add)
                c.read(i, m1)
        m = c.softmax_exp(scores, negmax, total, HEADS, keys, m1)
        sc = scores[:, :, 0:keys]
        m = c.tt(sc, sc, total[:, 0:HEADS].unsqueeze(2).to_broadcast([P, HEADS, keys]), ALU.mult, m)
        done = c.transpose_maps(pT, scores, HEADS, t, c.identity, m)
        pv_done = c.tensor.last
        c.tensor.wait(*done)
    return heads_out(c, yT, 0, pT, v_rows, HEADS)


def s5(c, a, s, u, yT):
    nc = c.nc
    G16 = 16
    dt, mag, th, turn, sn, cs = (c.carve(G16) for _ in range(6))
    re, im = s.v["ssm_a_re_2"], s.v["ssm_a_im_2"]
    m = c.act(dt, s.log_dt, ACT.Exp, c.small.last)
    m = c.tt(mag, re, dt, ALU.mult, m)
    m = c.act(mag, mag, ACT.Exp, m)
    m = c.tt(th, im, dt, ALU.mult, m)
    m = c.sincos(sn, cs, th, turn, m)
    lr, li, den, cr, ci, t1 = (c.carve(G16) for _ in range(6))
    c.vector.wait(c.scalar.last)
    c.tt(lr, mag, cs, ALU.mult)
    c.tt(li, mag, sn, ALU.mult)
    c.ts(lr, lr, -1.0, None, ALU.add, None)
    c.tt(den, re, re, ALU.mult)
    c.tt(t1, im, im, ALU.mult)
    c.tt(den, den, t1, ALU.add)
    c.recip(den, den)
    c.tt(cr, lr, re, ALU.mult)
    c.tt(t1, li, im, ALU.mult)
    c.tt(cr, cr, t1, ALU.add)
    c.tt(cr, cr, den, ALU.mult)
    c.tt(ci, li, re, ALU.mult)
    c.tt(t1, lr, im, ALU.mult)
    c.tt(ci, ci, t1, ALU.subtract)
    c.tt(ci, ci, den, ALU.mult)
    bb = [c.carve(G16, 32) for _ in range(2)]
    t2 = c.carve(G16, 16)
    for part in bb:
        c.fill(part, 0.0)
    for e in range(2):
        hs = slice(64 * e, 64 * e + 64)
        n = slice(16 * e, 16 * e + 16)
        crb, cib = (x[hs, :].unsqueeze(2).to_broadcast([64, G16, 16]) for x in (cr, ci))
        bre, bim = s.b_re[hs, :, :], s.b_im[hs, :, :]
        c.tt(bb[0][hs, :, n], crb, bre, ALU.mult)
        c.tt(t2[hs, :, :], cib, bim, ALU.mult)
        c.tt(bb[0][hs, :, n], bb[0][hs, :, n], t2[hs, :, :], ALU.subtract)
        c.tt(bb[1][hs, :, n], crb, bim, ALU.mult)
        c.tt(t2[hs, :, :], cib, bre, ALU.mult)
        c.tt(bb[1][hs, :, n], bb[1][hs, :, n], t2[hs, :, :], ALU.add)
    cc = [c.carve(4, P) for _ in range(2)]
    for dst, src, sign in ((cc[0], s.c_re, 1.0), (cc[1], s.c_im, -1.0)):
        for e in range(2):
            m = c.ts(dst[:, :, 64 * e:64 * e + 64], src, s.group_odd[:, e:e + 1], sign, ALU.mult, ALU.mult)
    bT, cT = [c.carve(4, P) for _ in range(2)], [c.carve(4, P) for _ in range(2)]
    c.tensor.wait(m)
    done = []
    for src, dst in ((bb[0], bT[0]), (bb[1], bT[1]), (cc[0], cT[0]), (cc[1], cT[1])):
        flat = src.rearrange("p a b -> p (a b)")
        i, bank = c.bank()
        for k in range(4):
            ins = nc.tensor.transpose(bank[:, k * P:(k + 1) * P], flat[:, k * P:(k + 1) * P], c.identity)
        m = c.tensor.did(ins)
        d = c.copy(dst, bank[:, :].rearrange("p (k s) -> p k s", k=4), m, q=c.scalar)
        c.read(i, d)
        done.append(d)
    c.tensor.wait(*done)
    cos, sin, turns, angle, br, bi, gr, gi = (c.carve(4, SEQ) for _ in range(8))
    for k in range(4):
        i0 = 4 * k
        for j in range(4):
            m = c.ts(angle[:, j, :], s.time, th[:, i0 + j:i0 + j + 1], None, ALU.mult, None, c.scalar.last)
        m = c.sincos(sin, cos, angle, turns, m)
        c.vector.wait(c.scalar.last)
        for j in range(4):
            i, bank = c.bank()
            i2, bank2 = c.bank()
            ch = slice(32 * j, 32 * j + 32)
            m = c.tensor.did(c.mm(bank[:, 0:SEQ], bT[0][ch, k, :], u[ch, k, :]))
            m2 = c.tensor.did(c.mm(bank2[:, 0:SEQ], bT[1][ch, k, :], u[ch, k, :]))
            c.tt(br[:, j, :], bank[:, 0:SEQ], cos[:, j, :], ALU.mult, m)
            m = c.tt(gi[:, j, :], bank[:, 0:SEQ], sin[:, j, :], ALU.mult, c.tensor.last)
            c.read(i, m)
            c.tt(bi[:, j, :], bank2[:, 0:SEQ], cos[:, j, :], ALU.mult, m2)
            m = c.tt(gr[:, j, :], bank2[:, 0:SEQ], sin[:, j, :], ALU.mult)
            c.read(i2, m)
        c.tt(br, br, gr, ALU.add)
        c.tt(bi, bi, gi, ALU.subtract)
        v = c.vector
        for j in range(4):
            keep = mag[:, i0 + j:i0 + j + 1].to_broadcast([P, SEQ])
            for src, dst in ((br, gr), (bi, gi)):
                m = v.did(v.after().tensor_tensor_scan(dst[:, j, :], keep, src[:, j, :], 0.0, ALU.mult, ALU.add))
        c.tt(br, cos, gr, ALU.mult)
        c.tt(bi, sin, gr, ALU.mult)
        c.tt(gr, sin, gi, ALU.mult)
        c.tt(gi, cos, gi, ALU.mult)
        c.tt(br, br, gr, ALU.subtract)
        m = c.tt(bi, bi, gi, ALU.add)
        c.tensor.wait(m)
        i, bank = c.bank()
        for j in range(4):
            ch = slice(32 * j, 32 * j + 32)
            c.mm(bank[ch, 0:SEQ], cT[0][:, k, ch], br[:, j, :], True, False)
            ins = c.mm(bank[ch, 0:SEQ], cT[1][:, k, ch], bi[:, j, :], False, True)
        m = c.tensor.did(ins)
        m = c.stt(yT[:, k, :], u[:, k, :], s.v["ssm_d_2"][:, k:k + 1], bank[:, 0:SEQ], ALU.mult, ALU.add, m)
        c.read(i, m)
    m = c.act(yT, yT, ACT.Gelu_apprx_tanh, m)
    c.tensor.wait(m)
    glu = br[:, :, :], bi[:, :, :]
    for half in range(2):
        w = c.weights(c.tensor)
        for k in range(0, 4, 2):
            i, src, m = c.product_cols(yT, w[:, :, k * P:(k + 2) * P], range(4))
            for j in range(2):
                bias = s.v["ssm_glu_b_2"][:, 4 * half + k + j:4 * half + k + j + 1]
                d = c.act(glu[half][:, k + j, :], src[:, j, :], ACT.Sigmoid if half else ACT.Identity, m, bias=bias)
            c.read(i, d)
        c.release(m)
    return c.tt(yT, glu[0], glu[1], ALU.mult, d)


def layer_norm(c, out, x, w, b, small, junk, *marks):
    for t in range(TT):
        m = c.reduce(small[:, t:t + 1], x[:, t, :], ALU.add, *marks)
        m = c.ts(small[:, t:t + 1], small[:, t:t + 1], 1.0 / D, None, ALU.mult, None)
        m = c.ts(x[:, t, :], x[:, t, :], small[:, t:t + 1], None, ALU.subtract, None)
        m = c.sumsq(small[:, 2 + t:3 + t], x[:, t, :], x[:, t, :], junk)
    m = c.rsqrt(small[:, 2:4], small[:, 2:4], D, 1e-5, m)
    for t in range(TT):
        m = c.stt(x[:, t, :], x[:, t, :], small[:, 2 + t:3 + t], w, ALU.mult, ALU.mult, m)
        m = c.tt(out[:, t, :], x[:, t, :], b, ALU.add, m)
    return m


def route(c, s, x1T):
    nc = c.nc
    i, bank = c.bank()
    for t in range(TT):
        for k in range(KT):
            ins = c.mm(bank[:, t * 36:t * 36 + 36], x1T[:, k, t * P:(t + 1) * P], s.w_router[:, k, :], k == 0, k == KT - 1)
    m = c.tensor.did(ins)
    logits = c.carve(TT, 36)
    m = c.tt(logits, bank[:, 0:72].rearrange("p (t n) -> p t n", t=TT), s.b_router.unsqueeze(1).to_broadcast([P, TT, 36]),
             ALU.add, m)
    c.read(i, m)
    top, pick, work, hot = c.carve(TT), c.carve(TT), c.carve(TT, 32), [c.carve(TT, 32) for _ in range(2)]
    group, p_group, exps = c.carve(TT, 4), c.carve(TT), c.carve(TT, 4)
    wide = lambda t, n: t.unsqueeze(2).to_broadcast([P, TT, n])

    def first_of(out, values, best, n):
        index = s.time[:, 0:n].unsqueeze(1).to_broadcast([P, TT, n])
        w = work[:, :, 0:n]
        c.tt(w, values, wide(best, n), ALU.is_lt)
        c.stt(w, w, 1000.0, index, ALU.mult, ALU.add)
        c.reduce(pick, w, ALU.min)
        return c.tt(out, index, wide(pick, n), ALU.is_equal)
    g = logits[:, :, 0:4]
    c.reduce(top, g, ALU.max)
    first_of(group, g, top, 4)
    m = c.tt(exps, g, wide(top, 4), ALU.subtract)
    m = c.act(exps, exps, ACT.Exp, m)
    m = c.reduce(p_group, exps, ALU.add, m)
    c.recip(p_group, p_group)
    e = c.carve(TT, 32)
    outside = c.carve(TT, 4)
    c.ts(outside, group, -1.0, 3e38, ALU.add, ALU.mult)
    for t in range(TT):
        inside = group[:, t, :].unsqueeze(2).to_broadcast([P, 4, 8])
        ev, lv = (v.rearrange("p (g n) -> p g n", g=4) for v in (e[:, t, :], logits[:, t, 4:36]))
        c.tt(ev, lv, inside, ALU.mult)
        c.tt(ev, ev, outside[:, t, :].unsqueeze(2).to_broadcast([P, 4, 8]), ALU.add)
    second = c.carve(TT)
    c.reduce(top, e, ALU.max)
    first_of(hot[0], e, top, 32)
    c.stt(e, hot[0], -3.3e38, e, ALU.mult, ALU.add)
    c.ts(e, e, -3.3e38, None, ALU.max, None)
    c.reduce(second, e, ALU.max)
    first_of(hot[1], e, second, 32)
    m = c.tt(second, second, top, ALU.subtract)
    m = c.act(second, second, ACT.Exp, m)
    c.ts(top, second, 1.0, None, ALU.add, None, m)
    c.recip(top, top)
    c.tt(top, top, p_group, ALU.mult)
    c.tt(second, second, top, ALU.mult)
    c.tt(hot[0], hot[0], wide(top, 32), ALU.mult)
    c.tt(hot[1], hot[1], wide(second, 32), ALU.mult)
    m = c.tt(hot[0], hot[0], hot[1], ALU.add)
    c.tensor.wait(m)
    i, bank = c.bank()
    for t in range(TT):
        ins = nc.tensor.transpose(bank[0:32, t * P:(t + 1) * P], hot[0][:, t, :], c.identity)
    m = c.tensor.did(ins)
    wT = c.carve(SEQ)
    m = c.copy(wT[0:32, :], bank[0:32, 0:SEQ], m)
    c.read(i, m)
    spread = s.weight
    some = c.carve(8, SEQ)
    for e0 in range(0, EXPERTS, 8):
        m = c.tt(some[0:32], wT[0:32].unsqueeze(1).to_broadcast([32, 8, SEQ]),
                 c.identity[0:32, e0:e0 + 8].unsqueeze(2).to_broadcast([32, 8, SEQ]), ALU.mult, c.tensor.last)
        c.tensor.wait(m)
        for n in range(0, 8, 2):
            i, bank = c.bank()
            m = c.tensor.did(c.mm(bank, c.ones[0:32, :], some[0:32, n:n + 2, :].rearrange("p a s -> p (a s)")))
            c.read(i, c.copy(spread[:, e0 + n:e0 + n + 2, :], bank[:, :].rearrange("p (a s) -> p a s", a=2), m, q=c.scalar))


def experts(c, a, s, x1T, y):
    nc = c.nc
    out_banks = c.banks[0:4]
    c.bank_used = [4, 5, 6, 7]
    w_gate = a["expert_w_gate_2"].rearrange("a e (k p) n -> (a e) p k n", p=P)
    w_up = a["expert_w_up_2"].rearrange("a e (k p) n -> (a e) p k n", p=P)
    w_down = a["expert_w_down_2"].rearrange("a e (k p) n -> (a e) p k n", p=P)
    hidden, act = [c.carve(2, SEQ) for _ in range(2)], [c.carve(2, SEQ) for _ in range(2)]
    zero = c.carve(P)
    full = [c.nc.alloc_semaphore(f"expert_weights{i}_full") for i in range(6)]

    def one(w, e):
        return w[e, :, :, :] if isinstance(e, int) else w[bass.ds(e, 1), :, :, :].rearrange("a p k n -> p (a k) n")

    def load(parity, e, freed=()):
        for n, (w, view) in enumerate(((w_gate, k_tiles(8)), (w_up, k_tiles(8)), (w_down, k_tiles(2, D)))):
            s_ = 3 * parity + n
            if freed:
                c.sync.wait(freed[n])
            nc.sync.dma_start(view(c.ring[s_]), one(w, e)).then_inc(full[s_], 16)

    for parity in range(2):
        load(parity, parity)
    m = c.fill(zero, 0.0)
    c.tensor.wait(m)
    for bank in out_banks:
        c.mm(bank, zero, s.weight[:, 0:2, :].rearrange("p a s -> p (a s)"))

    def pair(first_expert, turn, last):
        for parity in range(2):
            slots = c.ring[3 * parity:3 * parity + 3]
            gate_up = []
            for n in range(2):
                c.tensor.engine.wait_ge(full[3 * parity + n], turn * 16 + 16)
                i, src, m = c.product_cols(x1T, k_tiles(8)(slots[n]), range(KT))
                gate_up.append((i, src, m))
            (ig, gate, mg), (iu, up, mu) = gate_up
            h, silu = hidden[parity], act[parity]
            ms = c.act(silu, gate, ACT.Silu, mg)
            c.read(ig, ms)
            weight = s.weight[:, bass.ds(first_expert + parity, 1), :].to_broadcast([P, 2, SEQ])
            m1 = c.tt(silu, silu, weight, ALU.mult, ms)
            m1 = c.tt(h, up, silu, ALU.mult, mu)
            c.read(iu, m1)
            c.tensor.wait(m1)
            c.tensor.engine.wait_ge(full[3 * parity + 2], turn * 16 + 16)
            w = k_tiles(2, D)(slots[2])
            for t in range(TT):
                for half in range(2):
                    for k in range(2):
                        ins = nc.tensor.matmul(out_banks[2 * t + half], h[:, k, t * P:(t + 1) * P],
                                               w[:, k, half * 512:(half + 1) * 512], start=False,
                                               stop=True, skip_group_check=True)
            md = c.tensor.did(ins)
            if not last:
                load(parity, first_expert + parity + 2, (mg, mu, md))
    c.restart_in_loop()
    with nc.Fori(0, EXPERTS // 2 - 1) as n:
        pair(n * 2, n, False)
        c.restart_in_loop()
    pair(EXPERTS - 2, EXPERTS // 2 - 1, True)
    c.bank_used = list(range(8))
    for t in range(TT):
        for half in range(2):
            m = c.copy(y[:, t, half * 512:(half + 1) * 512], out_banks[2 * t + half], c.tensor.last)
    return m


def second_block(c, a, x):
    nc = c.nc
    s = State()
    s.columns = c.keep("columns_2", P)
    second_constants(c, s)
    c.restart()
    vectors_2(c, a, s)
    c.plan(second_pieces(a))
    c.vector.wait(c.gpsimd.last)
    c.restart()
    load = lambda dst, src: c.small.load(nc.scalar, dst, src)
    xT = c.hT
    merged, c.branch_tmp = c.carve(8, SEQ), c.carve(2, SEQ)
    done = c.columns_from_rows(xT, x, c.identity, KT, None)
    c.tensor.wait(*done)

    def cols(dst):
        w = c.weights(c.tensor)
        i, src, m = c.product_cols(xT, w, range(KT))
        c.release(m)
        c.read(i, c.copy(dst, src, m, q=c.scalar))

    def branch_gates(branch):
        gates = c.carve(8, SEQ)
        for n in range(4):
            w = c.weights(c.tensor)
            i, src, m = c.product_cols(xT, w, range(KT))
            c.release(m)
            for j in range(2):
                f = 8 * branch + 2 * n + j
                d = c.act(gates[:, 2 * n + j, :], src[:, j, :], ACT.Sigmoid, m, bias=s.v["gate_b_2"][:, f:f + 1])
            c.read(i, d)
        return gates

    base = c.carved
    yT = c.carve(4, SEQ)
    z = c.arena[:, ARENA - 14 * 257:ARENA].rearrange("p (k s) -> p k s", k=14)
    c.fill(z[:, :, 0:1], 0.0, q=c.gpsimd)
    for n in range(7):
        cols(z[:, 2 * n:2 * n + 2, 1:SEQ + 1])
    rwkv_input(c, a, s, z)
    c.restart()
    c.carved = s.rwkv_end
    rwkv_scan(c, s, yT)
    c.restart()
    c.carved = s.rwkv_end
    gates = branch_gates(0)
    rwkv_output(c, s, yT)
    add_branch(c, merged, gates, yT, True)
    c.restart()
    c.carved = base
    yT = c.carve(4, SEQ)
    qkT, v_rows = c.carve(8, SEQ), c.carve(TT, 512)
    for n in range(4):
        cols(qkT[:, 2 * n:2 * n + 2, :])
    for n in range(2):
        w = c.weights(c.tensor)
        i, src, m = c.product_rows(xT, w, range(KT))
        c.release(m)
        c.read(i, c.copy(v_rows[:, :, 256 * n:256 * n + 256], src, m, q=c.scalar))
    gates = branch_gates(1)
    c.pT8 = c.carve(2 * HEADS, SEQ).rearrange("p (h k) s -> p h k s", k=2)
    done = moba(c, s, qkT, v_rows, yT)
    c.tensor.wait(*done)
    add_branch(c, merged, gates, yT, False)
    c.restart()
    c.carved = base
    yT, u = c.carve(4, SEQ), c.carve(4, SEQ)
    s.b_re, s.b_im, s.c_re, s.c_im = c.carve(16, 16), c.carve(16, 16), c.carve(4, 64), c.carve(4, 64)
    for dst, name in ((s.b_re, "ssm_b_re_2"), (s.b_im, "ssm_b_im_2")):
        load(dst, a[name].rearrange("a (i e) q h -> (a e q) i h", e=2))
    for dst, name in ((s.c_re, "ssm_c_re_2"), (s.c_im, "ssm_c_im_2")):
        load(dst, a[name].rearrange("a (k g) h q -> (a g h) k q", g=8))
    for n in range(2):
        cols(u[:, 2 * n:2 * n + 2, :])
    gates = branch_gates(2)
    s5(c, a, s, u, yT)
    add_branch(c, merged, gates, yT, False)
    c.restart()
    c.carved = base
    y, small, junk = c.carve(TT, D), c.carve(4), c.carve(D)
    ln = [c.carve(D) for _ in range(4)]
    s.w_router, s.b_router = c.carve(KT, 36), c.carve(36)
    for dst, name in zip(ln, ("ln1_w_2", "ln1_b_2", "ln2_w_2", "ln2_b_2")):
        load(dst, a[name].to_broadcast([P, D]))
    load(s.w_router[:, :, 0:4], a["router_group_w_2"].rearrange("a (k p) n -> p (a k) n", p=P))
    load(s.w_router[:, :, 4:36], a["router_expert_w_2"].rearrange("a (k p) n -> p (a k) n", p=P))
    load(s.b_router[:, 0:4], a["router_group_b_2"].to_broadcast([P, 4]))
    load(s.b_router[:, 4:36], a["router_expert_b_2"].to_broadcast([P, 32]))
    out_rows(c, merged, y, 1)
    for t in range(TT):
        m = c.stt(y[:, t, :], x[:, t, :], ALPHA, y[:, t, :], ALU.mult, ALU.add)
    m = layer_norm(c, x, y, ln[0], ln[1], small, junk, m, c.small.last)
    x1T = c.hT
    done = c.columns_from_rows(x1T, x, c.identity, KT, None, m)
    c.tensor.wait(*done)
    s.weight = c.carve(EXPERTS, SEQ)
    c.tensor.wait(c.small.last)
    route(c, s, x1T)
    c.restart_in_loop()
    experts(c, a, s, x1T, y)
    for t in range(TT):
        m = c.stt(y[:, t, :], x[:, t, :], ALPHA, y[:, t, :], ALU.mult, ALU.add)
    layer_norm(c, x, y, ln[2], ln[3], small, junk, m)


def build(nc, a, out):
    c = Core(nc)
    x = c.keep("x", TT, D)
    c.hT = c.keep("hT", KT, SEQ)
    c.lam_table = c.keep("lambda_table", DEPTH, 2)
    for layer in range(DEPTH):
        lam = 0.8 - 0.6 * math.exp(-0.3 * layer)
        c.fill(c.lam_table[:, layer, 0:1], lam)
        c.fill(c.lam_table[:, layer, 1:2], 1.0 - lam)
    constants(c)
    c.small.load(nc.sync, x, a["x"].rearrange("a (t p) d -> p (a t) d", p=P))
    c.vector.wait(c.small.last)
    first_block(c, a, x)
    second_block(c, a, x)
    c.sync.wait(c.vector.last)
    s_out = nc.alloc_semaphore("stored")
    nc.sync.dma_start(out.rearrange("a (t p) d -> p (a t) d", p=P), x).then_inc(s_out, 16)
    nc.sync.wait_ge(s_out, 16)


INPUTS = [
    'x', 'c', 'positions', 'w_ada', 'b_ada', 'norm_g', 'w_in', 'diff_lambda', 'diff_subln_g',
    'mla_q_norm_g', 'w_uq', 'mla_kv_norm_g', 'w_ukv', 'conv_w', 'conv_b', 'dt_bias', 'a_log', 'd_skip',
    'ssm_norm_g', 'w_out', 'w_up', 'w_down', 'w_in_2', 'rwkv_mu_2', 'rwkv_w0_2', 'rwkv_w2_2',
    'rwkv_a0_2', 'rwkv_a2_2', 'rwkv_g2_2', 'rwkv_k_k_2', 'rwkv_k_a_2', 'rwkv_r_k_2', 'rwkv_ln_w_2',
    'rwkv_ln_b_2', 'ssm_a_re_2', 'ssm_a_im_2', 'ssm_b_re_2', 'ssm_b_im_2', 'ssm_c_re_2', 'ssm_c_im_2',
    'ssm_d_2', 'ssm_log_dt_2', 'ssm_glu_w_2', 'ssm_glu_b_2', 'w_up_rwkv_2', 'w_up_moba_2', 'w_up_ssm_2',
    'gate_b_2', 'w_out_2', 'ln1_w_2', 'ln1_b_2', 'router_group_w_2', 'router_group_b_2',
    'router_expert_w_2', 'router_expert_b_2', 'expert_w_gate_2', 'expert_w_up_2', 'expert_w_down_2',
    'ln2_w_2', 'ln2_b_2'
]


def kernel(**inputs):
    import numpy as _np
    import concourse.bacc as _bacc
    from concourse import mybir as _mybir
    from concourse.bass_utils import run_bass_kernel_spmd as _run

    nc = _bacc.Bacc("TRN2", target_bir_lowering=False, num_devices=1)
    arrays, handles = {}, {}
    for name in INPUTS:
        array = _np.ascontiguousarray(inputs[name])
        arrays[f"in_{name}"] = array
        handles[name] = nc.dram_tensor(f"in_{name}", array.shape, _mybir.dt.from_np(array.dtype),
                                       kind="ExternalInput").ap()
    out = nc.dram_tensor("out", (1, SEQ, D), F32, kind="ExternalOutput").ap()
    build(nc, handles, out)
    result = _run(nc, [arrays], core_ids=[0])
    return result.results[0]["out"]
```

```python
import math

import numpy as np

import concourse.bass as bass
from concourse import mybir
from concourse.alu_op_type import AluOpType as ALU

F32 = mybir.dt.float32
I32 = mybir.dt.int32
ACT = mybir.ActivationFunctionType
AX = mybir.AxisListType.X

P = 128
SEQ = 256
TT = SEQ // P
D = 1024
KT = D // P
DEPTH = 2
FF = 4 * D
SLOT = 2048
RING = 4
EXPERTS, D_EXPERT = 32, 256
TWO_PI = 2 * math.pi
ARENA = 40448
ROUND = 1.5 * 2.0 ** 23


class Queue:

    def __init__(self, nc, engine, name, ordered=True):
        self.engine, self.sem, self.ordered = engine, nc.alloc_semaphore(name), ordered
        self.count, self.seen = 0, {}

    def wait(self, *marks):
        for mark in marks:
            if mark is not None and self.seen.get(mark[0].name, 0) < mark[1]:
                self.engine.wait_ge(mark[0], mark[1])
                self.seen[mark[0].name] = mark[1]

    def after(self, *marks):
        self.wait(*marks)
        if self.ordered and self.count:
            self.wait(self.last)
        return self.engine

    def did(self, instruction):
        instruction.then_inc(self.sem, 1)
        self.count += 1
        return self.last

    @property
    def last(self):
        return (self.sem, self.count) if self.count else None


class Loads:

    def __init__(self, nc, name):
        self.sem, self.count = nc.alloc_semaphore(name), 0

    def load(self, engine, out, in_):
        engine.dma_start(out, in_).then_inc(self.sem, 16)
        self.count += 16

    @property
    def last(self):
        return (self.sem, self.count) if self.count else None


class Region:

    def __init__(self, arena, start, end):
        self.arena, self.at, self.end = arena, start, end

    def carve(self, *shape):
        n = int(np.prod(shape))
        piece = self.arena[:, self.at:self.at + n]
        self.at += n
        assert self.at <= self.end, (self.at, self.end)
        if len(shape) == 2:
            piece = piece.rearrange("p (a b) -> p a b", b=shape[1])
        if len(shape) == 3:
            piece = piece.rearrange("p (a b c) -> p a b c", b=shape[1], c=shape[2])
        return piece

    def rest(self, size=None):
        start = self.at
        if size is None:
            return Region(self.arena, start, self.end)
        self.at += size
        assert self.at <= self.end, (self.at, self.end)
        return Region(self.arena, start, start + size)


class Core:

    def __init__(self, nc):
        self.nc = nc
        self.tensor = Queue(nc, nc.tensor, "tensor_done", ordered=False)
        self.vector = Queue(nc, nc.vector, "vector_done")
        self.scalar = Queue(nc, nc.scalar, "scalar_done")
        self.gpsimd = Queue(nc, nc.gpsimd, "gpsimd_done")
        self.sync = Queue(nc, nc.sync, "sync_done")
        self.banks = [nc.alloc_psum_tensor(f"bank{i}", [P, 512], F32).ap() for i in range(8)]
        self.bank_free = [[] for _ in self.banks]
        self.bank_next, self.bank_used, self.held = 0, list(range(8)), set()
        self.ring = [nc.alloc_sbuf_tensor(f"weights{i}", [P, SLOT], F32).ap() for i in range(RING)]
        self.ring_full = [nc.alloc_semaphore(f"weights{i}_full") for i in range(RING)]
        self.ring_free, self.ring_count = [()] * RING, 0
        self.arena = nc.alloc_sbuf_tensor("arena", [P, ARENA], F32).ap()
        self.mem = Region(self.arena, 0, ARENA)

    def keep(self, name, *shape, dtype=F32):
        return self.nc.alloc_sbuf_tensor(name, [P, *shape], dtype).ap()

    def carve(self, *shape):
        return self.mem.carve(*shape)

    def bank(self):
        i = self.bank_used[self.bank_next % len(self.bank_used)]
        while i in self.held:
            self.bank_next += 1
            i = self.bank_used[self.bank_next % len(self.bank_used)]
        self.bank_next += 1
        self.tensor.wait(*self.bank_free[i])
        self.bank_free[i] = []
        return i, self.banks[i]

    def read(self, i, *marks):
        self.bank_free[i] += [m for m in marks if m]

    def weights(self, queue, piece):
        (view, source), s = piece, self.ring_count % RING
        self.sync.wait(*self.ring_free[s])
        self.nc.sync.dma_start(view(self.ring[s]), source).then_inc(self.ring_full[s], 16)
        queue.wait((self.ring_full[s], 16 * (self.ring_count // RING + 1)))
        self.ring_count += 1
        return view(self.ring[s])

    def release(self, *readers):
        self.ring_free[(self.ring_count - 1) % RING] = readers

    def meet(self):
        queues = [self.tensor, self.vector, self.scalar, self.gpsimd]
        for q in queues:
            q.wait(*(other.last for other in queues))

    def weave(self, *streams):
        streams = list(streams)
        while streams:
            for stream in list(streams):
                steps, region = stream
                self.mem = region
                if next(steps, "end") == "end":
                    streams.remove(stream)

    def mm(self, out, lhsT, rhs, start=True, stop=True):
        return self.nc.tensor.matmul(out, lhsT, rhs, start=start, stop=stop)

    def tt(self, out, a, b, op, *marks, q=None):
        q = q or self.vector
        return q.did(q.after(*marks).tensor_tensor(out, a, b, op))

    def ts(self, out, a, s1, s2, op0, op1, *marks, q=None):
        q = q or self.vector
        if op1 is None:
            return q.did(q.after(*marks).tensor_scalar(out, a, s1, None, op0))
        return q.did(q.after(*marks).tensor_scalar(out, a, s1, s2, op0, op1))

    def stt(self, out, a, s, b, op0, op1, *marks):
        q = self.vector
        return q.did(q.after(*marks).scalar_tensor_tensor(out, a, s, b, op0, op1))

    def copy(self, out, a, *marks, q=None):
        q = q or self.vector
        if q is self.scalar:
            return q.did(q.after(*marks).activation(out, a, ACT.Copy))
        return q.did(q.after(*marks).tensor_copy(out, a))

    def act(self, out, a, func, *marks, **kw):
        q = self.scalar
        return q.did(q.after(*marks).activation(out, a, func, **kw))

    def reduce(self, out, a, op, *marks, negate=None):
        q = self.vector
        return q.did(q.after(*marks).tensor_reduce(out, a, AX, op, negate=negate))

    def recip(self, out, a, *marks):
        q = self.vector
        return q.did(q.after(*marks).reciprocal(out, a))

    def fill(self, out, value, *marks, q=None):
        q = q or self.vector
        return q.did(q.after(*marks).memset(out, value))

    def sumsq(self, out, a, b, junk, *marks):
        q = self.vector
        return q.did(q.after(*marks).tensor_tensor_reduce(out=junk, in0=a, in1=b, scale=1.0, scalar=0.0,
                                                          op0=ALU.mult, op1=ALU.add, accum_out=out))

    def rsqrt(self, out, total, n, eps, *marks):
        m = self.ts(out, total, 1.0 / n, eps, ALU.mult, ALU.add, *marks)
        m = self.act(out, out, ACT.Sqrt, m)
        return self.recip(out, out, m)

    def columns_from_rows(self, out, rows, identity, tiles, evacuate, *marks):
        self.tensor.wait(*marks)
        done = []
        for k0 in range(0, tiles, 2):
            i, bank = self.bank()
            n = min(2, tiles - k0)
            for k in range(k0, k0 + n):
                for t in range(TT):
                    c = ((k - k0) * TT + t) * P
                    ins = self.nc.tensor.transpose(bank[:, c:c + P], rows[:, t, k * P:(k + 1) * P], identity)
            m = self.tensor.did(ins)
            if evacuate is None:
                src = bank[:, 0:n * SEQ].rearrange("p (k s) -> p k s", s=SEQ)
                q = self.scalar if (k0 // 2) % 2 else self.vector
                d = [self.copy(out[:, k0:k0 + n, :], src, m, q=q)]
            else:
                d = [evacuate(k, out[:, k, :], bank[:, (k - k0) * SEQ:(k - k0 + 1) * SEQ], m)
                     for k in range(k0, k0 + n)]
            self.read(i, *d)
            done += d
        return done

    def product_cols(self, xT, w, tiles, width=2):
        i, bank = self.bank()
        for j in range(width):
            for n, k in enumerate(tiles):
                ins = self.mm(bank[:, j * SEQ:(j + 1) * SEQ], w[:, n, j * P:(j + 1) * P], xT[:, k, :],
                              start=(n == 0), stop=(n == len(tiles) - 1))
        return i, bank[:, 0:width * SEQ].rearrange("p (j s) -> p j s", s=SEQ), self.tensor.did(ins)

    def product_rows(self, xT, w, tiles, width=256):
        i, bank = self.bank()
        for t in range(TT):
            for n, k in enumerate(tiles):
                ins = self.mm(bank[:, t * width:(t + 1) * width], xT[:, k, t * P:(t + 1) * P], w[:, n, :],
                              start=(n == 0), stop=(n == len(tiles) - 1))
        return i, bank[:, 0:TT * width].rearrange("p (t n) -> p t n", t=TT), self.tensor.did(ins)

    def sincos(self, sin, cos, x, k, *marks):
        c1 = 6.28125
        c2 = round((TWO_PI - c1) * 2 ** 20) / 2 ** 20
        c3 = TWO_PI - c1 - c2
        m = self.ts(k, x, 1 / TWO_PI, ROUND, ALU.mult, ALU.add, *marks)
        m = self.ts(k, k, -ROUND, None, ALU.add, None)
        for c in (c1, c2, c3):
            m = self.stt(x, k, -c, x, ALU.mult, ALU.add)
        m = self.ts(x, x, 3.1415925, -3.1415925, ALU.min, ALU.max)
        ms = self.act(sin, x, ACT.Sin, m)
        m = self.act(cos, x, ACT.Sin, m, scale=0.5)
        m = self.tt(cos, cos, cos, ALU.mult, m)
        m = self.ts(cos, cos, -2.0, 1.0, ALU.mult, ALU.add)
        return [m, ms]

    def softmax_exp(self, scores, neg_max, total, n, keys, *marks):
        m = self.reduce(neg_max[:, 0:n], scores[:, 0:n, 0:keys], ALU.max, *marks, negate=True)
        for h in range(n):
            m = self.act(scores[:, h, 0:keys], scores[:, h, 0:keys], ACT.Exp, m,
                         bias=neg_max[:, h:h + 1], accum_out=total[:, h:h + 1])
        return self.recip(total[:, 0:n], total[:, 0:n], m)

    def transpose_maps(self, pT, maps, n, t, identity, *marks):
        self.tensor.wait(*marks)
        done = []
        kts = t + 1
        per = 4 // kts
        for h0 in range(0, n, per):
            i, bank = self.bank()
            for h in range(h0, h0 + per):
                for kt in range(kts):
                    c = ((h - h0) * kts + kt) * P
                    ins = self.nc.tensor.transpose(bank[:, c:c + P], maps[:, h, kt * P:(kt + 1) * P], identity)
            m = self.tensor.did(ins)
            src = bank[:, :].rearrange("p (h k s) -> p h k s", h=per, k=kts)
            q = self.scalar if (h0 // per) % 2 else self.vector
            d = self.copy(pT[:, h0:h0 + per, 0:kts, t * P:(t + 1) * P], src, m, q=q)
            self.read(i, d)
            done.append(d)
        return done


def constants(c):
    g = c.gpsimd

    def select(out, cmp, fill, base, pattern, channel):
        return g.did(g.after().affine_select(out=out, in_=out, compare_op=cmp, fill=fill, base=base,
                                             pattern=pattern, channel_multiplier=channel))

    c.identity = c.keep("identity", P)
    c.fill(c.identity, 0.0, q=g)
    select(c.identity, ALU.not_equal, 1.0, 0, [[-1, P]], 1)
    c.ones = c.keep("ones", P)
    c.fill(c.ones, 1.0, q=g)
    c.head_sum = c.keep("head_sum", P)
    c.fill(c.head_sum, 1.0, q=g)
    select(c.head_sum[:, 0:64], ALU.is_ge, 0.0, 63, [[0, 64]], -1)
    select(c.head_sum[:, 64:P], ALU.is_ge, 0.0, -64, [[0, 64]], 1)


def first_constants(c):
    g = c.gpsimd

    def select(out, cmp, fill, base, pattern, channel):
        return g.did(g.after().affine_select(out=out, in_=out, compare_op=cmp, fill=fill, base=base,
                                             pattern=pattern, channel_multiplier=channel))
    c.chunk_mask = c.carve(TT, SEQ)
    c.fill(c.chunk_mask, 0.0, q=g)
    for t in range(TT):
        for half in range(2):
            rows = c.chunk_mask[64 * half:64 * half + 64, t, :]
            select(rows, ALU.is_ge, -1e30, t * P + 64 * half + 63, [[-1, SEQ]], 0)
    c.causal = c.carve(TT, SEQ)
    c.fill(c.causal, 1.0, q=g)
    for t in range(TT):
        select(c.causal[:, t, :], ALU.is_ge, 0.0, -t * P, [[1, SEQ]], -1)


OFF_Q, OFF_K, OFF_V, OFF_CQ, OFF_CKV, OFF_Z, OFF_XBC, OFF_DT = 0, 256, 512, 768, 1024, 1184, 1696, 2464
LORA = 160


def k_tiles(n, width=256):
    return lambda slot: slot[:, 0:n * width].rearrange("p (k n) -> p k n", n=width)


def rope_tables(c, a):
    c.rope_cos, c.rope_sin = c.carve(TT, 16), c.carve(TT, 16)
    pos_i, pos = c.carve(TT).bitcast(I32), c.carve(TT)
    loads = Loads(c.nc, "position_loads")
    freq, angle, turn = c.carve(16), c.carve(TT, 16), c.carve(TT, 16)
    for t in range(TT):
        loads.load(c.nc.scalar, pos_i[:, t:t + 1], a["positions"][0:1, t * P:(t + 1) * P].rearrange("a p -> p a"))
    m = c.copy(pos, pos_i, loads.last)
    for j in range(16):
        f = np.float32(1.0) / np.power(np.float32(10000.0), np.float32(2 * j) / np.float32(32))
        m = c.fill(freq[:, j:j + 1], float(f))
    for t in range(TT):
        m = c.ts(angle[:, t, :], freq, pos[:, t:t + 1], None, ALU.mult, None, m)
    c.sincos(c.rope_sin, c.rope_cos, angle, turn, m)


def rope(c, out, x, t, heads, stride_view, scratch, *marks):
    cos = c.rope_cos[:, t:t + 1, :].to_broadcast([P, heads, 16])
    sin = c.rope_sin[:, t:t + 1, :].to_broadcast([P, heads, 16])
    x1, x2 = x[:, :, 0:16], x[:, :, 16:32]
    m = c.tt(out[:, :, 0:16], x1, cos, ALU.mult, *marks)
    m = c.tt(scratch, x2, sin, ALU.mult)
    m = c.tt(out[:, :, 0:16], out[:, :, 0:16], scratch, ALU.subtract)
    m = c.tt(scratch, x1, sin, ALU.mult)
    m = c.tt(out[:, :, 16:32], x2, cos, ALU.mult)
    return c.tt(out[:, :, 16:32], out[:, :, 16:32], scratch, ALU.add)


def layer_pieces(a, l):
    w = {name: a[name][l].rearrange("(k p) n -> p k n", p=P) for name in ("w_ada", "w_in", "w_out", "w_up", "w_down")}
    col = lambda name, off: (k_tiles(KT), w[name][:, :, off:off + 256])
    pieces = {"ada": [(lambda s: s, w["w_ada"][:, k, g * SLOT:(g + 1) * SLOT]) for g in range(3) for k in range(KT)]}
    pieces["in"] = [col("w_in", off) for off in (OFF_Q, OFF_K, OFF_V, OFF_CQ)]
    pieces["in"].append((k_tiles(KT, LORA), w["w_in"][:, :, OFF_CKV:OFF_CKV + LORA]))
    pieces["in"] += [col("w_in", off + 256 * n) for off, count in ((OFF_Z, 2), (OFF_XBC, 3)) for n in range(count)]
    pieces["out"] = [col("w_out", n * 256) for n in range(4)]
    pieces["up"] = [col("w_up", n * 256) for n in range(FF // 256)]
    pieces["down"] = [(k_tiles(KT), w["w_down"][:, k * KT:(k + 1) * KT, n * 256:(n + 1) * 256])
                      for n in range(4) for k in range(FF // D)]
    return pieces


ATTENTION_FLOATS = 10000

V_NORM0, V_NORM2, V_QN, V_KVN, V_CONV_W, V_CONV_B, V_COND, V_ADA = 0, 8, 16, 18, 19, 43, 49, 57
V_ROWS = V_ADA + 48


def modulation(c, a, l, s, pieces):
    nc = c.nc
    vec, norm, acc = c.carve(P), c.carve(D), [c.carve(SLOT) for _ in range(2)]
    loads, rows = Loads(nc, f"vector_loads{l}"), Loads(nc, f"row_loads{l}")
    q = nc.scalar
    for n0, n, src in ((V_NORM0, 8, a["norm_g"][l, 0:1, :]), (V_NORM2, 8, a["norm_g"][l, 2:3, :]),
                       (V_QN, 2, a["mla_q_norm_g"][l:l + 1]), (V_KVN, 1, a["mla_kv_norm_g"][l:l + 1]),
                       (V_CONV_W, 24, a["conv_w"][l]), (V_CONV_B, 6, a["conv_b"][l:l + 1]), (V_COND, 8, a["c"]),
                       (V_ADA, 48, a["b_ada"][l:l + 1])):
        loads.load(q, vec[n0:n0 + n, :], src.rearrange("a (r p) -> (a r) p", p=P))
    for dst, off in ((s.gate_m, 2 * D), (s.gate_f, 5 * D)):
        loads.load(q, dst, a["b_ada"][l:l + 1, off:off + D].to_broadcast([P, D]))
    rows.load(q, norm, a["norm_g"][l, 1:2, :].to_broadcast([P, D]))
    c.tensor.wait(loads.last, c.gpsimd.last)
    i, bank = c.bank()
    m = c.tensor.did(nc.tensor.transpose(bank[:, 0:V_ROWS], vec[0:V_ROWS, :], c.identity[0:V_ROWS, 0:V_ROWS]))
    m = c.copy(s.vec, bank[:, 0:V_ROWS], m, loads.last)
    c.read(i, m)
    cond = c.carve(8)
    mc = c.act(cond, s.vec[:, V_COND:V_COND + 8], ACT.Silu, m)
    for g in range(3):
        part = acc[g % 2]
        for k in range(KT):
            w = c.weights(c.vector, pieces[g * KT + k])
            if k == 0:
                m = c.ts(part, w, cond[:, 0:1], None, ALU.mult, None, mc, done if g == 2 else None)
            else:
                m = c.stt(part, w, cond[:, k:k + 1], part, ALU.mult, ALU.add)
            c.release(m)
            yield
        c.tensor.wait(m)
        i, bank = c.bank()
        for n in range(16):
            ins = c.mm(bank[:, n:n + 1], part[:, n * P:(n + 1) * P], c.ones[:, 0:1])
        done = c.tensor.did(ins)
        m = c.tt(s.mod[:, 16 * g:16 * g + 16], bank[:, 0:16], s.vec[:, V_ADA + 16 * g:V_ADA + 16 * g + 16], ALU.add, done)
        c.read(i, m)
        if g == 0:
            c.stt(s.in_scale_m, s.mod[:, 8:16], 1.0, s.vec[:, V_NORM0:V_NORM0 + 8], ALU.add, ALU.mult)
            continue
        if g == 2:
            c.stt(s.in_scale_f, s.mod[:, 32:40], 1.0, s.vec[:, V_NORM2:V_NORM2 + 8], ALU.add, ALU.mult)
        gate, off = ((s.gate_m, 0), (s.gate_f, D))[g - 1]
        for h in range(2):
            i, bank = c.bank()
            m = done = c.tensor.did(c.mm(bank, c.ones, part[:, off + h * 512:off + (h + 1) * 512]))
            half = gate[:, h * 512:(h + 1) * 512]
            m = c.tt(half, bank, half, ALU.add, m)
            c.read(i, m)
            m = c.tt(half, half, norm[:, h * 512:(h + 1) * 512], ALU.mult, rows.last)
        if g == 1:
            c.scalar.wait(m)
            rows.load(q, norm, a["norm_g"][l, 3:4, :].to_broadcast([P, D]))
        yield


def normed_cols(c, hT, x, scale, shift, work, small, *marks):
    for t in range(TT):
        m = c.sumsq(small[:, t:t + 1], x[:, t, :], x[:, t, :], work[:, t, :], *marks)
    m = c.rsqrt(small[:, 0:TT], small[:, 0:TT], D, 1e-6, m)
    for t in range(TT):
        m = c.act(work[:, t, :], x[:, t, :], ACT.Copy, m, scale=small[:, t:t + 1])

    def evacuate(k, out, src, mark):
        if (k // 2) % 2:
            return c.act(out, src, ACT.Identity, mark, scale=scale[:, k:k + 1], bias=shift[:, k:k + 1])
        return c.ts(out, src, scale[:, k:k + 1], shift[:, k:k + 1], ALU.mult, ALU.add, mark)
    return c.columns_from_rows(hT, work, c.identity, KT, evacuate, m, c.vector.last)


def projections(c, s, loads, pieces):
    hT, pieces = s.hT, iter(pieces)

    def cols(dst, width=2):
        w = c.weights(c.tensor, next(pieces))
        i, src, m = c.product_cols(hT, w, range(KT), width)
        c.release(m)
        c.read(i, c.copy(dst, src, m, q=c.scalar))

    def rows(dst, width=256):
        w = c.weights(c.tensor, next(pieces))
        i, src, m = c.product_rows(hT, w, range(KT), width)
        c.release(m)
        c.read(i, c.copy(dst, src, m))

    cols(s.qT)
    yield
    cols(s.kT)
    yield
    for dst in (s.vq[:, :, 0:256], s.vq[:, :, 256:512]):
        rows(dst)
        yield
    rows(s.lora, LORA)
    yield
    for dst in (s.z[:, :, 0:256], s.z[:, :, 256:512]):
        rows(dst)
        yield
    for j in range(3):
        cols(s.xbc[:, 2 * j:2 * j + 2, 3:3 + SEQ])
        yield
    c.tensor.wait(loads.last)
    i, bank = c.bank()
    for t in range(TT):
        for k in range(KT):
            ins = c.mm(bank[:, t * 8:t * 8 + 8], hT[:, k, t * P:(t + 1) * P], s.w_dt[:, k, :], k == 0, k == KT - 1)
    m = c.tensor.did(ins)
    c.read(i, c.copy(s.dt, bank[:, 0:16].rearrange("p (t h) -> p t h", t=TT), m))


def diff_attention(c, s, loads, y):
    nc, lam = c.nc, s.lam
    for j in range(2):
        m = c.sumsq(lam[:, j:j + 1], s.lp[:, 2 * j, :], s.lp[:, 2 * j + 1, :], s.lp_work, loads.last)
    m = c.act(lam[:, 2:4], lam[:, 0:2], ACT.Exp, m)
    m = c.stt(lam[:, 4:5], lam[:, 2:3], s.lambda_init, lam[:, 3:4], ALU.add, ALU.subtract, m)
    m = c.ts(lam[:, 4:5], lam[:, 4:5], -1.0, None, ALU.mult, None)
    scores, total, negmax = c.carve(8, SEQ), c.carve(8), c.carve(8)
    pT, work = c.carve(4, 2, SEQ), c.carve(256)
    pv_done = None
    for t in range(TT):
        keys = P * (t + 1)
        c.tensor.wait(c.scalar.last)
        for r in range(4):
            i, bank = c.bank()
            for e in range(2):
                ins = c.mm(bank[:, e * SEQ:e * SEQ + keys], s.qT[32 * r:32 * r + 32, e, t * P:(t + 1) * P],
                           s.kT[32 * r:32 * r + 32, e, 0:keys])
            m = c.tensor.did(ins)
            src = bank[:, :].rearrange("p (e k) -> p e k", e=2)[:, :, 0:keys]
            mask = c.chunk_mask[:, t:t + 1, 0:keys].to_broadcast([P, 2, keys])
            both = scores[:, :, :].rearrange("p (e r) k -> p e r k", e=2)[:, :, r, 0:keys]
            m = c.stt(both, src, 32 ** -0.5, mask, ALU.mult, ALU.add, m, pv_done)
            c.read(i, m)
            if r % 2:
                yield
        m = c.softmax_exp(scores, negmax, total, 8, keys, m)
        yield
        pair = total[:, :].rearrange("p (h e) -> p h e", e=2)
        m = c.ts(pair[:, :, 1], pair[:, :, 1], lam[:, 4:5], None, ALU.mult, None)
        sc = scores[:, :, 0:keys]
        m = c.tt(sc, sc, total[:, 0:8].unsqueeze(2).to_broadcast([P, 8, keys]), ALU.mult)
        two = scores[:, :, :].rearrange("p (h e) k -> p h e k", e=2)
        m = c.tt(two[:, :, 0, 0:keys], two[:, :, 0, 0:keys], two[:, :, 1, 0:keys], ALU.add)
        yield
        done = c.transpose_maps(pT, two[:, :, 0, :], 4, t, c.identity, m)
        pv_done = c.tensor.last
        yield
        c.tensor.wait(*done, c.vector.last)
        i, bank = c.bank()
        for h in range(4):
            for kt in range(t + 1):
                ins = c.mm(bank[:, h * 64:(h + 1) * 64], pT[:, h, kt, t * P:(t + 1) * P],
                           s.vq[:, kt, h * 64:(h + 1) * 64], kt == 0, kt == t)
        m = c.tensor.did(ins)
        yt = y[:, t, 0:256]
        m = c.copy(yt, bank[:, 0:256], m)
        c.read(i, m)
        m = c.tt(work, yt, yt, ALU.mult, m)
        m = c.reduce(total[:, 0:4], work[:, :].rearrange("p (h e) -> p h e", h=4), ALU.add, m)
        yield
        m = c.rsqrt(total[:, 0:4], total[:, 0:4], 64, 1e-5, m)
        yh = yt.rearrange("p (h e) -> p h e", h=4)
        m = c.tt(yh, yh, total[:, 0:4].unsqueeze(2).to_broadcast([P, 4, 64]), ALU.mult, m)
        m = c.tt(yh, yh, s.subln.unsqueeze(1).to_broadcast([P, 4, 64]), ALU.mult, m)
        m = c.ts(yt, yt, 1.0 - s.lambda_init, None, ALU.mult, None)
        yield


def latent_attention(c, s, yT):
    cq, lora = s.vq, s.lora
    small, work = c.carve(8), c.carve(TT, 384)
    for t in range(TT):
        m = c.sumsq(small[:, t:t + 1], cq[:, t, 256:512], cq[:, t, 256:512], work[:, t, 0:256])
        m = c.sumsq(small[:, 2 + t:3 + t], lora[:, t, 0:128], lora[:, t, 0:128], work[:, t, 0:128])
    c.rsqrt(small[:, 0:2], small[:, 0:2], 256, 1e-6)
    m = c.rsqrt(small[:, 2:4], small[:, 2:4], 128, 1e-6)
    latT = c.carve(3, SEQ)
    for t in range(TT):
        c.ts(work[:, t, 0:256], cq[:, t, 256:512], small[:, t:t + 1], None, ALU.mult, None)
        m = c.ts(work[:, t, 256:384], lora[:, t, 0:128], small[:, 2 + t:3 + t], None, ALU.mult, None)
    yield
    done = c.columns_from_rows(latT, work, c.identity, 3,
                               lambda k, out, src, mark: c.ts(out, src, s.vec[:, V_QN + k:V_QN + k + 1], None,
                                                              ALU.mult, None, mark), m)
    q_rows, k_rows, v_rows = c.carve(TT, 4, 96), c.carve(TT, 4, 96), c.carve(TT, 256)
    qraw, kvraw, half = c.carve(384), c.carve(512), c.carve(4, 16)
    c.tensor.wait(*done)
    for t in range(TT):
        i, bank = c.bank()
        for k in range(2):
            ins = c.mm(bank[:, 0:384], latT[:, k, t * P:(t + 1) * P], s.w_uq[:, k, :], k == 0, k == 1)
        m = c.tensor.did(ins)
        m = c.copy(qraw, bank[:, 0:384], m)
        c.read(i, m)
        qh = qraw[:, :].rearrange("p (h e) -> p h e", h=4)
        c.copy(q_rows[:, t, :, 0:64], qh[:, :, 0:64])
        rope(c, q_rows[:, t, :, 64:96], qh[:, :, 64:96], t, 4, None, half)
        i, bank = c.bank()
        m = c.tensor.did(c.mm(bank, latT[:, 2, t * P:(t + 1) * P], s.w_ukv))
        m = c.copy(kvraw, bank, m)
        c.read(i, m)
        kh = kvraw[:, :].rearrange("p (h e) -> p h e", h=4)
        c.copy(k_rows[:, t, :, 0:64], kh[:, :, 0:64])
        c.copy(v_rows[:, t, :].rearrange("p (h e) -> p h e", h=4), kh[:, :, 64:128])
        kr = lora[:, t:t + 1, 128:160]
        rope(c, k_rows[:, t, 0:1, 64:96], kr, t, 1, None, half[:, 0:1, :])
        m = c.copy(k_rows[:, t, 1:4, 64:96], k_rows[:, t, 0:1, 64:96].to_broadcast([P, 3, 32]))
        yield
    qT, kT = c.carve(4, SEQ), c.carve(4, SEQ)
    c.tensor.wait(m)
    done = []
    for src, dst in ((q_rows, qT), (k_rows, kT)):
        for h in range(0, 4, 2):
            i, bank = c.bank()
            for e in range(2):
                for t in range(TT):
                    n = (e * TT + t) * P
                    ins = c.nc.tensor.transpose(bank[0:96, n:n + P], src[:, t, h + e, :], c.identity)
            m = c.tensor.did(ins)
            d = c.copy(dst[0:96, h:h + 2, :], bank[0:96, :].rearrange("p (h s) -> p h s", h=2), m, q=c.scalar)
            c.read(i, d)
            done.append(d)
        yield
    scores, total, negmax = c.carve(4, SEQ), c.carve(4), c.carve(4)
    pT = c.carve(4, 2, SEQ)
    c.tensor.wait(*done)
    pv_done = None
    for t in range(TT):
        keys = P * (t + 1)
        for h in range(0, 4, 2):
            i, bank = c.bank()
            for e in range(2):
                ins = c.mm(bank[:, e * SEQ:e * SEQ + keys], qT[0:96, h + e, t * P:(t + 1) * P], kT[0:96, h + e, 0:keys])
            m = c.tensor.did(ins)
            src = bank[:, :].rearrange("p (e k) -> p e k", e=2)[:, :, 0:keys]
            mask = c.chunk_mask[:, t:t + 1, 0:keys].to_broadcast([P, 2, keys])
            m = c.stt(scores[:, h:h + 2, 0:keys], src, 96 ** -0.5, mask, ALU.mult, ALU.add, m, pv_done)
            c.read(i, m)
        yield
        m = c.softmax_exp(scores, negmax, total, 4, keys, m)
        yield
        sc = scores[:, :, 0:keys]
        m = c.tt(sc, sc, total[:, 0:4].unsqueeze(2).to_broadcast([P, 4, keys]), ALU.mult, m)
        done = c.transpose_maps(pT, scores, 4, t, c.identity, m)
        pv_done = c.tensor.last
        yield
        c.tensor.wait(*done)
    c.tensor.wait(*heads_out(c, yT, 2, pT, v_rows, 4))


def heads_out(c, yT, tile0, pT, v_rows, heads):
    done = []
    for h0 in range(0, heads, 4):
        i, bank = c.bank()
        for h in range(h0, h0 + 4):
            r, col = 64 * (h % 2), ((h - h0) // 2) * SEQ
            for t in range(TT):
                for kt in range(t + 1):
                    ins = c.mm(bank[r:r + 64, col + t * P:col + (t + 1) * P], v_rows[:, kt, h * 64:(h + 1) * 64],
                               pT[:, h, kt, t * P:(t + 1) * P], kt == 0, kt == t)
        m = c.tensor.did(ins)
        d = c.copy(yT[:, tile0 + h0 // 2:tile0 + h0 // 2 + 2, :], bank[:, :].rearrange("p (k s) -> p k s", k=2), m)
        c.read(i, d)
        done.append(d)
    return done


def log1p_positive(c, out, e, z, zz, *marks):
    m = c.ts(z, e, 2.0, None, ALU.add, None, *marks)
    m = c.recip(z, z)
    m = c.tt(z, z, e, ALU.mult)
    m = c.tt(zz, z, z, ALU.mult)
    m = c.ts(out, zz, 1.0 / 15, 1.0 / 13, ALU.mult, ALU.add)
    for n in (11, 9, 7, 5, 3, 1):
        m = c.tt(out, out, zz, ALU.mult)
        m = c.ts(out, out, 1.0 / n, None, ALU.add, None)
    m = c.tt(out, out, z, ALU.mult)
    return c.ts(out, out, 2.0, None, ALU.mult, None)


def state_space(c, s, loads, y):
    conv = c.carve(6, SEQ)
    for r in range(6):
        w = lambda j: s.vec[:, V_CONV_W + 6 * j + r:V_CONV_W + 6 * j + r + 1]
        m = c.ts(conv[:, r, :], s.xbc[:, r, 0:SEQ], w(0), None, ALU.mult, None, c.scalar.last, c.gpsimd.last)
        for j in range(1, 4):
            m = c.stt(conv[:, r, :], s.xbc[:, r, j:j + SEQ], w(j), conv[:, r, :], ALU.mult, ALU.add)
        ms = c.act(conv[:, r, :], conv[:, r, :], ACT.Silu, m, bias=s.vec[:, V_CONV_B + r:V_CONV_B + r + 1])
        if r % 2:
            yield
    xs = c.carve(TT, 512)
    dt, da, e, z, zz, n = (c.carve(TT, 8) for _ in range(6))
    bias = s.dt_bias.unsqueeze(1).to_broadcast([P, TT, 8])
    m = c.tt(dt, s.dt, bias, ALU.add, loads.last)
    m = c.ts(n, dt, -1.0, None, ALU.mult, None)
    m = c.tt(n, dt, n, ALU.min)
    m = c.act(e, n, ACT.Exp, m)
    m = log1p_positive(c, da, e, z, zz, m)
    m = c.stt(dt, dt, 0.0, da, ALU.max, ALU.add)
    yield
    neg_a = c.carve(8)
    ma = c.act(neg_a, s.a_log, ACT.Exp, loads.last)
    m = c.stt(da, dt, -1.0, neg_a.unsqueeze(1).to_broadcast([P, TT, 8]), ALU.mult, ALU.mult, ma)
    wide = c.carve(TT, 8, P)
    m = c.copy(wide, da.unsqueeze(3).to_broadcast([P, TT, 8, P]), m)
    c.tensor.wait(m, c.gpsimd.last)
    i, bank = c.bank()
    for t in range(TT):
        for u in range(t + 1):
            ins = c.mm(bank[:, t * 8:t * 8 + 8], c.causal[:, u, t * P:(t + 1) * P], da[:, u, :], u == 0, u == t)
    m = c.tensor.did(ins)
    sum_col = c.carve(TT, 8)
    m = c.copy(sum_col, bank[:, 0:16].rearrange("p (t h) -> p t h", t=TT), m)
    c.read(i, m)
    yield
    bc = c.carve(TT * 2, SEQ)
    c.tensor.wait(ms)
    for g in range(2):
        i, bank = c.bank()
        for t in range(TT):
            ins = c.mm(bank[:, t * SEQ:(t + 1) * SEQ], conv[64 * g:64 * g + 64, 4, t * P:(t + 1) * P],
                       conv[64 * g:64 * g + 64, 5, :])
        m = c.tensor.did(ins)
        m = c.tt(bc[:, :, :].rearrange("p (t g) s -> p t g s", g=2)[:, :, g, :],
                 bank[:, :].rearrange("p (t s) -> p t s", t=TT), c.causal, ALU.mult, m)
        c.read(i, m)
    yield
    for t in range(TT):
        i, bank = c.bank()
        for k in range(4):
            ins = c.nc.tensor.transpose(bank[:, k * P:(k + 1) * P], conv[:, k, t * P:(t + 1) * P], c.identity)
        m = c.tensor.did(ins)
        c.read(i, c.copy(xs[:, t, :], bank, m, q=c.scalar))
    xd = c.carve(TT, 512)
    for t in range(TT):
        m = c.tt(xd[:, t, :].rearrange("p (h e) -> p h e", h=8), xs[:, t, :].rearrange("p (h e) -> p h e", h=8),
                 dt[:, t, :].unsqueeze(2).to_broadcast([P, 8, 64]), ALU.mult, c.scalar.last)
    yield
    mix = [c.carve(TT, SEQ) for _ in range(2)]
    outs = [c.bank() for _ in range(TT)]
    c.held.update(i for i, _ in outs)
    mixed = [None] * 2

    def apply(h):
        c.tensor.wait(mixed[h % 2])
        for t in range(TT):
            for u in range(t + 1):
                ins = c.mm(outs[t][1][:, h * 64:(h + 1) * 64], mix[h % 2][:, u, t * P:(t + 1) * P],
                           xd[:, u, h * 64:(h + 1) * 64], u == 0, u == t)
        return c.tensor.did(ins)
    applied = [None] * 2
    for h in range(8):
        i, bank = c.bank()
        for u in range(TT):
            ins = c.mm(bank[:, 0:SEQ], wide[:, u, h, :], c.causal[:, u, :], u == 0, u == 1)
        m = c.tensor.did(ins)
        part = mix[h % 2]
        for t in range(TT):
            m1 = c.ts(part[:, t, :], bank[:, 0:SEQ], sum_col[:, t, h:h + 1], 0.0, ALU.subtract, ALU.min, m, applied[h % 2])
        c.read(i, m1)
        m = c.act(part, part, ACT.Exp, m1)
        if h:
            applied[(h - 1) % 2] = apply(h - 1)
        mixed[h % 2] = c.tt(part, part, bc[:, :, :].rearrange("p (t g) s -> p t g s", g=2)[:, :, h // 4, :], ALU.mult, m)
        yield
    m_all = apply(7)
    work = c.carve(512)
    small = c.carve(2)
    for t in range(TT):
        (i, bank), m = outs[t], m_all
        out = y[:, t, 512:1024]
        m0 = c.tt(work[:, :].rearrange("p (h e) -> p h e", h=8), xs[:, t, :].rearrange("p (h e) -> p h e", h=8),
                  s.d_skip.unsqueeze(2).to_broadcast([P, 8, 64]), ALU.mult)
        m = c.tt(out, bank, work, ALU.add, m)
        c.read(i, m)
        c.held.discard(i)
        yield
        mz = c.act(s.z[:, t, :], s.z[:, t, :], ACT.Silu, m0)
        m = c.tt(out, out, s.z[:, t, :], ALU.mult, mz)
        m = c.tt(work, out, out, ALU.mult)
        m = c.reduce(small, work[:, :].rearrange("p (g e) -> p g e", g=2), ALU.add)
        m = c.rsqrt(small, small, 256, 1e-6, m)
        og = out.rearrange("p (g e) -> p g e", g=2)
        m = c.tt(og, og, small.unsqueeze(2).to_broadcast([P, 2, 256]), ALU.mult, m)
        m = c.tt(out, out, s.ssm_norm, ALU.mult)
        yield


def add_gated(c, x, y, gate, small, junk, *marks):
    for t in range(TT):
        m = c.sumsq(small[:, t:t + 1], y[:, t, :], y[:, t, :], junk, *marks)
    m = c.rsqrt(small[:, 0:TT], small[:, 0:TT], D, 1e-6, m)
    for t in range(TT):
        m = c.stt(y[:, t, :], y[:, t, :], small[:, t:t + 1], gate, ALU.mult, ALU.mult, m)
        m = c.tt(x[:, t, :], x[:, t, :], y[:, t, :], ALU.add)
    return m


class State:
    pass


def mixer_loads(c, a, l, s):
    loads = Loads(c.nc, f"mixer_loads{l}")
    load = lambda dst, src: loads.load(c.nc.scalar, dst, src)
    s.w_dt, s.w_uq, s.w_ukv = c.carve(KT, 8), c.carve(2, 384), c.carve(512)
    s.lp, s.lp_work, s.subln = c.carve(4, 32), c.carve(32), c.carve(64)
    load(s.w_dt, a["w_in"][l, :, OFF_DT:OFF_DT + 8].rearrange("(k p) n -> p k n", p=P))
    load(s.w_uq, a["w_uq"][l].rearrange("(k p) n -> p k n", p=P))
    load(s.w_ukv, a["w_ukv"][l])
    load(s.lp, a["diff_lambda"][l:l + 1].to_broadcast([P, 4, 32]))
    load(s.subln, a["diff_subln_g"][l:l + 1].to_broadcast([P, 64]))
    s.d_skip, s.dt_bias, s.a_log, s.ssm_norm = c.carve(8), c.carve(8), c.carve(8), c.carve(512)
    for dst, name in ((s.d_skip, "d_skip"), (s.dt_bias, "dt_bias"), (s.a_log, "a_log"), (s.ssm_norm, "ssm_norm_g")):
        load(dst, a[name][l:l + 1].to_broadcast([P, dst.shape[1]]))
    return loads


def mixer(c, a, l, s, x, pieces, ada):
    work, small, junk = c.carve(TT, D), c.carve(4), c.carve(D)
    loads = mixer_loads(c, a, l, s)
    s.lam = c.carve(5)
    s.qT, s.kT = c.carve(2, SEQ), c.carve(2, SEQ)
    s.vq, s.lora, s.z = c.carve(TT, 512), c.carve(TT, LORA), c.carve(TT, 512)
    s.xbc, s.dt = c.carve(6, 3 + SEQ), c.carve(TT, 8)
    c.fill(s.xbc[:, :, 0:3], 0.0, q=c.gpsimd)
    done = normed_cols(c, s.hT, x, s.in_scale_m, s.mod[:, 0:8], work, small)
    c.tensor.wait(*done)
    here = c.mem
    c.weave((projections(c, s, loads, pieces["in"]), here), *ada)
    c.meet()
    y, yT = work, s.hT
    attention_mem, ssm_mem = here.rest(ATTENTION_FLOATS), here.rest()

    def attentions():
        yield from diff_attention(c, s, loads, y)
        c.tensor.wait(c.vector.last)
        c.columns_from_rows(yT[:, 0:2, :], y[:, :, 0:256], c.identity, 2, None)
        c.meet()
        c.mem.at = attention_start
        yield from latent_attention(c, s, yT)

    attention_start = attention_mem.at
    c.weave((state_space(c, s, loads, y), ssm_mem), (attentions(), attention_mem))
    c.tensor.wait(c.vector.last)
    done = c.columns_from_rows(yT[:, 4:8, :], y[:, :, 512:1024], c.identity, 4, None)
    c.tensor.wait(*done, c.scalar.last, c.vector.last)
    c.vector.wait(c.tensor.last)
    c.scalar.wait(c.tensor.last)
    for _ in out_rows(c, s.hT, y, pieces["out"]):
        pass
    add_gated(c, x, y, s.gate_m, small, junk)


def mlp(c, l, s, x, pieces, ada):
    work, small, junk = c.carve(TT, D), c.carve(4), c.carve(D)
    uT = c.carve(FF // P, SEQ)
    done = normed_cols(c, s.hT, x, s.in_scale_f, s.mod[:, 24:32], work, small)
    c.tensor.wait(*done)
    here = c.mem

    def steps():
        for n, piece in enumerate(pieces["up"]):
            w = c.weights(c.tensor, piece)
            i, src, m = c.product_cols(s.hT, w, range(KT))
            c.release(m)
            part = uT[:, 2 * n:2 * n + 2, :]
            m = c.act(part, src, ACT.Relu, m)
            c.read(i, m)
            m = c.act(part, part, ACT.Square, m)
            yield
        c.tensor.wait(m)
        yield from out_rows(c, uT, work, pieces["down"])

    c.weave((steps(), here), *ada)
    add_gated(c, x, work, s.gate_f, small, junk)


def first_block(c, a, x):
    first_constants(c)
    rope_tables(c, a)
    layers = []
    for l in range(DEPTH):
        s = State()
        s.hT, s.lambda_init = c.hT, 0.8 - 0.6 * math.exp(-0.3 * l)
        s.vec, s.mod = c.carve(V_ROWS), c.carve(48)
        s.in_scale_m, s.in_scale_f, s.gate_m, s.gate_f = c.carve(8), c.carve(8), c.carve(D), c.carve(D)
        layers.append(s)
    ada_floats = P + D + 2 * SLOT + 8
    ada_mem = c.mem.rest(ada_floats)
    free = c.mem
    steps = modulation(c, a, 0, layers[0], layer_pieces(a, 0)["ada"])
    c.mem = ada_mem
    for _ in range(KT + 1):
        next(steps)
    left = [(steps, ada_mem)]
    for l, s in enumerate(layers):
        pieces = layer_pieces(a, l)
        c.mem = free.rest()
        mixer(c, a, l, s, x, pieces, left)
        c.meet()
        left = []
        if l + 1 < DEPTH:
            again = Region(c.arena, ada_mem.end - ada_floats, ada_mem.end)
            left = [(modulation(c, a, l + 1, layers[l + 1], layer_pieces(a, l + 1)["ada"]), again)]
        c.mem = free.rest()
        mlp(c, l, s, x, pieces, left)
        left = []
        c.meet()


def out_rows(c, inT, out, pieces):
    each = len(pieces) // 4
    for n in range(4):
        (i0, bank0), (i1, bank1) = c.bank(), c.bank()
        for p in range(each):
            w = c.weights(c.tensor, pieces[n * each + p])
            for t, bank in enumerate((bank0, bank1)):
                for k in range(KT):
                    ins = c.mm(bank[:, 0:256], inT[:, p * KT + k, t * P:(t + 1) * P], w[:, k, :],
                               p == 0 and k == 0, p == each - 1 and k == KT - 1)
            m = c.tensor.did(ins)
            c.release(m)
            if each > 1:
                c.held.update((i0, i1))
                yield
                c.held.difference_update((i0, i1))
        c.read(i0, c.copy(out[:, 0, n * 256:(n + 1) * 256], bank0[:, 0:256], m))
        c.read(i1, c.copy(out[:, 1, n * 256:(n + 1) * 256], bank1[:, 0:256], m, q=c.scalar))
    c.vector.wait(c.scalar.last)


C = 32
N_CHUNK = SEQ // C
OFF_MOBA, OFF_SSM, OFF_GATE = 1792, 3328, 3840
HEADS = 8
ALPHA = 2.0 ** 0.25
SSM_MOBA_FLOATS = 9400
VECTORS_2 = [("rwkv_mu_2", 14), ("rwkv_w0_2", 4), ("rwkv_a0_2", 4), ("rwkv_k_k_2", 4), ("rwkv_k_a_2", 4),
             ("rwkv_r_k_2", 4), ("rwkv_ln_w_2", 4), ("rwkv_ln_b_2", 4), ("ssm_d_2", 4), ("ssm_glu_b_2", 8),
             ("gate_b_2", 24), ("ssm_a_re_2", 16), ("ssm_a_im_2", 16), ("ssm_log_dt_2", 16)]


def second_pieces(a):
    w_in = a["w_in_2"].rearrange("a (k p) n -> p (a k) n", p=P)
    col = lambda off: (k_tiles(KT), w_in[:, :, off:off + 256])
    half = lambda w, n: (k_tiles(4, 512), a[w].rearrange("a (k p) n -> p (a k) n", p=P)[:, :, n * 512:(n + 1) * 512])
    gate = lambda branch: [col(OFF_GATE + D * branch + 256 * n) for n in range(4)]
    up = lambda name: [half(name, n) for n in range(2)]
    pieces = {"rwkv": [col(256 * n) for n in range(7)], "moba": [col(OFF_MOBA + 256 * n) for n in range(6)],
              "ssm": [col(OFF_SSM + 256 * n) for n in range(2)], "gate": [gate(branch) for branch in range(3)],
              "up": [up("w_up_rwkv_2"), up("w_up_moba_2"), up("w_up_ssm_2")], "glu": up("ssm_glu_w_2")}
    w_out = a["w_out_2"].rearrange("a (k p) n -> p (a k) n", p=P)
    pieces["out"] = [(k_tiles(KT), w_out[:, :, n * 256:(n + 1) * 256]) for n in range(4)]
    return pieces


def second_constants(c, s):
    g = c.gpsimd

    def select(out, cmp, fill, base, pattern, channel):
        return g.did(g.after().affine_select(out=out, in_=out, compare_op=cmp, fill=fill, base=base,
                                             pattern=pattern, channel_multiplier=channel))
    s.distance = c.carve(TT, SEQ)
    for t in range(TT):
        g.did(g.after().iota(s.distance[:, t, :], pattern=[[-1, SEQ]], base=t * P, channel_multiplier=1,
                             allow_small_or_imprecise_dtypes=True))
        select(s.distance[:, t, :], ALU.is_ge, 1e34, t * P, [[-1, SEQ]], 1)
    s.pair = c.carve(5, P)
    c.fill(s.pair, 1.0, q=g)
    for kind, block in ((0, C), (1, C), (2, C), (3, 16), (4, 16)):
        for b in range(P // block):
            part = s.pair[:, kind, b * block:(b + 1) * block]
            if kind in (0, 3):
                select(part, ALU.is_gt, 0.0, b * block, [[1, block]], -1)
                select(part, ALU.is_ge, 0.0, -b * block, [[0, block]], 1)
            elif kind == 1:
                select(part, ALU.is_ge, 0.0, b * block, [[1, block]], -1)
                select(part, ALU.is_ge, 0.0, -b * block, [[0, block]], 1)
            else:
                select(part, ALU.is_gt, 0.0, -b * block, [[-1, block]], 1)
                select(part, ALU.is_ge, 0.0, (b + 1) * block - 1, [[0, block]], -1)
    s.chunk_start = c.carve(4 * SEQ)
    c.fill(s.chunk_start, 1.0, q=g)
    c.fill(s.chunk_start[:, :].rearrange("p (n c) -> p n c", c=C)[:, :, 0:1], 0.0, q=g)
    s.time = c.carve(SEQ)
    g.did(g.after().iota(s.time, pattern=[[1, SEQ]], base=0, channel_multiplier=0,
                         allow_small_or_imprecise_dtypes=True))
    number, s.group_odd = c.carve(1).bitcast(I32), c.carve(2)
    m = g.did(g.after().iota(number, pattern=[[0, 1]], base=0, channel_multiplier=1))
    m = c.ts(number, number, 4, 1, ALU.arith_shift_right, ALU.bitwise_and, m)
    m = c.copy(s.group_odd[:, 1:2], number, m)
    c.ts(s.group_odd[:, 0:1], s.group_odd[:, 1:2], -1.0, 1.0, ALU.mult, ALU.add)


def vectors_2(c, a, s):
    s.columns, s.log_dt, s.v = c.carve(P), c.carve(16), {}
    rows, each = c.carve(P), c.carve(16, 2)
    loads = Loads(c.nc, "vector_loads_2")
    loads.load(c.nc.scalar, each, a["ssm_log_dt_2"].rearrange("a (i e) -> a i e", e=2).to_broadcast([P, 16, 2]))
    n0 = 0
    for name, n in VECTORS_2:
        if name == "ssm_log_dt_2":
            continue
        flat = a[name]
        if name == "rwkv_r_k_2":
            flat = flat.rearrange("a h e -> a (h e)")
        elif name in ("ssm_a_re_2", "ssm_a_im_2"):
            flat = flat.rearrange("a g e -> a (g e)")
        flat = flat.rearrange("a (r p) -> (a r) p", p=P)
        loads.load(c.nc.scalar, rows[n0:n0 + n, :], flat)
        s.v[name] = s.columns[:, n0:n0 + n]
        n0 += n
    c.tensor.wait(loads.last, c.gpsimd.last)
    i, bank = c.bank()
    m = c.tensor.did(c.nc.tensor.transpose(bank[:, 0:n0], rows[0:n0, :], c.identity[0:n0, 0:n0]))
    c.read(i, c.copy(s.columns[:, 0:n0], bank[:, 0:n0], m))
    for e in range(2):
        c.copy(s.log_dt[64 * e:64 * e + 64, :], each[64 * e:64 * e + 64, :, e], loads.last)


def rwkv_input(c, a, s, project, pieces):
    col = lambda name, k: s.v[name][:, k:k + 1]
    s.rwkv_gate, s.bonus = c.carve(4, SEQ), c.carve(4, SEQ)
    s.AR = c.carve(4, TT, 2 * P)
    s.b, s.k, s.bend, s.kend, s.chunk_decay = (c.carve(4, SEQ), c.carve(4, SEQ), c.carve(4, SEQ), c.carve(4, SEQ),
                                               c.carve(4, N_CHUNK))
    s.v_cols = c.carve(4, SEQ)
    s.rwkv_end = c.mem.at
    s.lora_w, s.g2 = c.carve(512), c.carve(512)
    z = c.carve(14, SEQ + 1)
    loads = Loads(c.nc, "rwkv_loads")
    loads.load(c.nc.scalar, s.lora_w[0:64, :], a["rwkv_w2_2"][0, :, :])
    loads.load(c.nc.scalar, s.lora_w[64:P, :], a["rwkv_a2_2"][0, :, :])
    loads.load(c.nc.scalar, s.g2, a["rwkv_g2_2"][0, :, :])
    c.fill(z[:, :, 0:1], 0.0, q=c.gpsimd)
    for n in range(7):
        project(z[:, 2 * n:2 * n + 2, 1:SEQ + 1], pieces[n])
        yield
    r, k_, low, gate_in, tmp = c.carve(4, SEQ), c.carve(4, SEQ), c.carve(SEQ), c.carve(SEQ), c.carve(SEQ)
    v = s.v_cols
    shifted = [part[:, n, :] for part in (r, k_, v) for n in range(4)] + [low, gate_in]
    for k in range(14):
        m = c.tt(tmp, z[:, k, 0:SEQ], z[:, k, 1:SEQ + 1], ALU.subtract, c.scalar.last, c.gpsimd.last)
        m = c.stt(shifted[k], tmp, col("rwkv_mu_2", k), z[:, k, 1:SEQ + 1], ALU.mult, ALU.add)
        if k % 4 == 3:
            yield
    m = c.act(low[0:64, :], low[0:64, :], ACT.Tanh, m)
    m = c.act(gate_in, gate_in, ACT.Sigmoid, m)
    c.tensor.wait(m, c.vector.last, loads.last)
    logw, icl = c.carve(4, SEQ), c.carve(4, SEQ)
    for k in range(4):
        for out, r0, bias in ((logw, 0, "rwkv_w0_2"), (icl, 64, "rwkv_a0_2")):
            i, bank = c.bank()
            m = c.tensor.did(c.mm(bank[:, 0:SEQ], s.lora_w[r0:r0 + 64, k * P:(k + 1) * P], low[r0:r0 + 64, :]))
            c.read(i, c.act(out[:, k, :], bank[:, 0:SEQ], ACT.Sigmoid, m, bias=col(bias, k)))
        i, bank = c.bank()
        m = c.tensor.did(c.mm(bank[:, 0:SEQ], s.g2[:, k * P:(k + 1) * P], gate_in))
        c.read(i, c.copy(s.rwkv_gate[:, k, :], bank[:, 0:SEQ], m, q=c.scalar))
        yield
    c.ts(logw, logw, -math.exp(-0.5), None, ALU.mult, None, c.scalar.last)
    kk, work, ka = c.carve(4, SEQ), c.carve(4, SEQ), c.carve(4, SEQ)
    for k in range(4):
        m = c.ts(kk[:, k, :], k_[:, k, :], col("rwkv_k_k_2", k), None, ALU.mult, None)
    m = c.tt(work, kk, kk, ALU.mult)
    c.tensor.wait(m)
    for k in range(0, 4, 2):
        i, bank = c.bank()
        m = c.tensor.did(c.mm(bank, c.head_sum, work[:, k:k + 2, :].rearrange("p k s -> p (k s)")))
        m = c.ts(ka[:, k:k + 2, :], bank[:, :].rearrange("p (k s) -> p k s", k=2), 1e-24, None, ALU.max, None, m)
        c.read(i, m)
    yield
    m = c.act(ka, ka, ACT.Sqrt, m)
    m = c.recip(ka, ka, m)
    yield
    m = c.tt(kk, kk, ka, ALU.mult)
    for k in range(4):
        m = c.ts(ka[:, k, :], icl[:, k, :], -1.0, col("rwkv_k_a_2", k), ALU.add, ALU.mult)
    m = c.stt(k_, ka, 1.0, k_, ALU.add, ALU.mult)
    for k in range(4):
        m = c.stt(work[:, k, :], r[:, k, :], col("rwkv_r_k_2", k), k_[:, k, :], ALU.mult, ALU.mult, c.tensor.last)
    c.tensor.wait(m)
    for k in range(0, 4, 2):
        i, bank = c.bank()
        m = c.tensor.did(c.mm(bank, c.head_sum, work[:, k:k + 2, :].rearrange("p k s -> p (k s)")))
        m = c.tt(s.bonus[:, k:k + 2, :], bank[:, :].rearrange("p (k s) -> p k s", k=2), v[:, k:k + 2, :], ALU.mult, m)
        c.read(i, m)
    yield
    run = c.carve(4, SEQ)
    flat = lambda t: t.rearrange("p k s -> p (k s)")
    v1 = c.vector
    m = v1.did(v1.after().tensor_tensor_scan(flat(run), s.chunk_start, flat(logw), 0.0, ALU.mult, ALU.add))
    part = lambda n: s.AR[:, :, :, n * P:(n + 1) * P].rearrange("p k t s -> p (k t) s")
    tiled = lambda t: t.rearrange("p k (t s) -> p (k t) s", t=TT)
    m = c.tt(work, run, logw, ALU.subtract, c.tensor.last)
    m = c.act(work, work, ACT.Exp, m)
    yield
    m = c.stt(part(0), tiled(kk), -1.0, tiled(work), ALU.mult, ALU.mult, m)
    m = c.act(work, run, ACT.Exp, m)
    yield
    m = c.tt(part(1), tiled(r), tiled(work), ALU.mult, m)
    chunks = lambda t: t.rearrange("p k (n c) -> p (k n) c", c=C)
    m = c.copy(s.chunk_decay[:, :, :].rearrange("p k n -> p (k n)"), chunks(work)[:, :, C - 1])
    m = c.act(work, run, ACT.Exp, m, scale=-1.0)
    yield
    c.tt(kk, kk, icl, ALU.mult)
    m = c.tt(s.b, kk, work, ALU.mult, m)
    m = c.tt(s.k, k_, work, ALU.mult)
    m = c.tt(chunks(work), chunks(run)[:, :, C - 1:C].to_broadcast([P, 4 * N_CHUNK, C]), chunks(run), ALU.subtract)
    m = c.act(work, work, ACT.Exp, m)
    yield
    m = c.tt(s.bend, kk, work, ALU.mult, m)
    m = c.tt(s.kend, k_, work, ALU.mult)


def rwkv_scan(c, s, yT):
    nc, I = c.nc, c.identity
    eight = c.scalar, c.vector
    state = c.carve(4, 64)
    m = c.fill(state, 0.0)
    for t in range(TT):
        rows = {}
        inner = c.mem.at
        W = c.carve(HEADS, P)
        for n, name in enumerate(("a", "bend", "kend", "v")):
            src = {"bend": s.bend, "kend": s.kend, "v": s.v_cols}.get(name)
            c.tensor.wait(c.vector.last)
            i, bank = c.bank()
            for k in range(4):
                part = s.AR[:, k, t, 0:P] if name == "a" else src[:, k, t * P:(t + 1) * P]
                ins = nc.tensor.transpose(bank[:, k * P:(k + 1) * P], part, I)
            m = c.tensor.did(ins)
            heads = bank[:, :].rearrange("p (h e) -> p h e", h=HEADS)
            rows[name] = W[:, :, 0:64] if name == "a" else c.carve(HEADS, 64)
            c.read(i, c.copy(rows[name], heads, m, q=eight[n % 2]))
            yield
        G, N, PP = c.carve(HEADS, 4 * P), c.carve(HEADS, P), c.carve(HEADS, P)
        N1, P2, N2 = c.carve(HEADS, P), c.carve(HEADS, P), c.carve(HEADS, P)
        Z = c.carve(HEADS, P)
        for h in range(HEADS):
            k, r = h // 2, 64 * (h % 2)
            hs = slice(r, r + 64)
            tok = slice(t * P, (t + 1) * P)
            i, bank = c.bank()
            c.mm(bank[:, 0:2 * P], s.b[hs, k, tok], s.AR[hs, k, t, :])
            m = c.tensor.did(c.mm(bank[:, 2 * P:4 * P], s.k[hs, k, tok], s.AR[hs, k, t, :]))
            m = c.tt(G[:, h, :].rearrange("p (a b s) -> p a (b s)", a=2, b=2),
                     bank[:, :].rearrange("p (a s) -> p a s", a=2),
                     s.pair[:, 0:2, :].rearrange("p b s -> p (b s)").unsqueeze(1).to_broadcast([P, 2, 2 * P]),
                     ALU.mult, m)
            c.read(i, m)
            i, bank = c.bank()
            m = c.tensor.did(c.mm(bank[:, 0:P], s.AR[hs, k, t, 0:P], s.b[hs, k, tok]))
            m = c.tt(N1[:, h, :], bank[:, 0:P], s.pair[:, 2, :], ALU.mult, m)
            c.read(i, m)
            if h % 2:
                yield
        bc8 = lambda kind: s.pair[:, kind:kind + 1, :].to_broadcast([P, HEADS, P])
        m = c.tt(PP, G[:, :, 0:P], bc8(3), ALU.mult)
        m = c.tt(N, N1, bc8(4), ALU.mult)
        m = c.tt(Z, PP, I.unsqueeze(1).to_broadcast([P, HEADS, P]), ALU.add)
        m = c.tt(N1, N1, N, ALU.subtract)
        yield

        def per_head(out, left, right, combine=None, marks=()):
            c.tensor.wait(c.vector.last, c.scalar.last, *marks)
            done = []
            for h0 in range(0, HEADS, 4):
                i, bank = c.bank()
                for h in range(h0, h0 + 4):
                    ins = c.mm(bank[:, (h - h0) * P:(h - h0 + 1) * P], left[:, h, :], right[:, h, :])
                m = c.tensor.did(ins)
                src = bank[:, :].rearrange("p (h s) -> p h s", h=4)
                if combine is None:
                    d = c.copy(out[:, h0:h0 + 4, :], src, m, q=c.scalar)
                else:
                    d = c.tt(out[:, h0:h0 + 4, :], src, combine[:, h0:h0 + 4, :], ALU.add, m)
                c.read(i, d)
                done.append(d)
            return done
        p, n, p_next, n_next = PP, N, P2, N2
        for level in range(3):
            per_head(n_next, p, n)
            yield
            if level < 2:
                per_head(p_next, n, p)
            per_head(Z, n_next, Z, Z)
            yield
            p, n, p_next, n_next = p_next, n_next, p, n
        X, M = P2, N2
        c.tensor.wait(c.vector.last)
        for h0 in range(0, HEADS, 4):
            i, bank = c.bank()
            for h in range(h0, h0 + 4):
                ins = nc.tensor.transpose(bank[:, (h - h0) * P:(h - h0 + 1) * P], Z[:, h, :], I)
            m = c.tensor.did(ins)
            c.read(i, c.copy(X[:, h0:h0 + 4, :], bank[:, :].rearrange("p (h s) -> p h s", h=4), m, q=c.scalar))
        yield
        per_head(M, N1, Z)
        yield
        per_head(Z, X, M, Z)
        yield
        AK = G[:, :, 2 * P:3 * P]
        c.tensor.wait(c.vector.last)
        i, bank = c.bank()
        for h in range(HEADS):
            ins = c.mm(bank[:, h * 64:(h + 1) * 64], AK[:, h, :], rows["v"][:, h, :])
        m = c.tensor.did(ins)
        c.read(i, c.copy(W[:, :, 64:P], bank[:, :].rearrange("p (h e) -> p h e", h=HEADS), m))
        yield
        G12 = PP
        per_head(G12, Z, W)
        yield
        c.tensor.wait(c.scalar.last, c.vector.last)
        R2, Y0 = N1[:, 4:8, :], P2[:, 4:8, :]
        i, bank = c.bank()
        for h in range(HEADS):
            o = bank[64 * (h % 2):64 * (h % 2) + 64, (h // 2) * P:(h // 2 + 1) * P]
            ins = c.mm(o, G12[:, h, 0:64], G[:, h, P:2 * P])
        m = c.tensor.did(ins)
        m = c.tt(R2, bank[:, :].rearrange("p (k s) -> p k s", k=4), s.AR[:, :, t, P:2 * P], ALU.add, m)
        c.read(i, m)
        i, bank = c.bank()
        for h in range(HEADS):
            o = bank[64 * (h % 2):64 * (h % 2) + 64, (h // 2) * P:(h // 2 + 1) * P]
            c.mm(o, G12[:, h, 64:P], G[:, h, P:2 * P], True, False)
            ins = c.mm(o, rows["v"][:, h, :], G[:, h, 3 * P:4 * P], False, True)
        m = c.tensor.did(ins)
        c.read(i, c.copy(Y0, bank[:, :].rearrange("p (k s) -> p k s", k=4), m))
        yield
        n_here = P // C
        gain, states = c.carve(n_here, 4 * 64), c.carve(n_here, 4 * 64)
        step = N1, P2, N2, Z
        for n in range(n_here):
            ts_ = slice(n * C, (n + 1) * C)
            decay = s.chunk_decay[:, :, t * n_here + n]
            m = c.tt(step[n][:, 0:4, :], I.unsqueeze(1).to_broadcast([P, 4, P]),
                     decay.unsqueeze(2).to_broadcast([P, 4, P]), ALU.mult, c.tensor.last)
            i, bank = c.bank()
            for h in range(HEADS):
                r, k = 64 * (h % 2), h // 2
                ins = c.mm(bank[r:r + 64, k * P + r:k * P + r + 64], G12[ts_, h, 0:64], rows["bend"][ts_, h, :])
            m = c.tensor.did(ins)
            for r in (0, 64):
                d = step[n][r:r + 64, 0:4, r:r + 64]
                b = bank[r:r + 64, :].rearrange("p (k s) -> p k s", k=4)[:, :, r:r + 64]
                m1 = c.tt(d, b, d, ALU.add, m)
            c.read(i, m1)
            i, bank = c.bank()
            for h in range(HEADS):
                r, k = 64 * (h % 2), h // 2
                o = bank[r:r + 64, k * 64:(k + 1) * 64]
                c.mm(o, rows["bend"][ts_, h, :], G12[ts_, h, 64:P], True, False)
                ins = c.mm(o, rows["kend"][ts_, h, :], rows["v"][ts_, h, :], False, True)
            m = c.tensor.did(ins)
            c.read(i, c.copy(gain[:, n, :], bank[:, 0:256], m, q=c.scalar))
            yield
        current = state[:, :, :].rearrange("p k e -> p (k e)")
        for n in range(n_here):
            m = c.copy(states[:, n, :], current, c.scalar.last)
            c.tensor.wait(m)
            i, bank = c.bank()
            for k in range(4):
                ins = c.mm(bank[:, k * 64:(k + 1) * 64], step[n][:, k, :], states[:, n, k * 64:(k + 1) * 64])
            m = c.tensor.did(ins)
            m = c.tt(current, bank[:, 0:256], gain[:, n, :], ALU.add, m)
            c.read(i, m)
            yield
        pair_banks = [c.bank() for _ in range(2)]
        for n in range(n_here):
            for h in range(HEADS):
                r, k = 64 * (h % 2), h // 2
                o = pair_banks[h % 2][1][r:r + 64, k * P + n * C:k * P + (n + 1) * C]
                ins = c.mm(o, states[r:r + 64, n, k * 64:(k + 1) * 64], R2[r:r + 64, k, n * C:(n + 1) * C])
        m = c.tensor.did(ins)
        for e, (i, bank) in enumerate(pair_banks):
            r = 64 * e
            c.read(i, c.tt(yT[r:r + 64, :, t * P:(t + 1) * P], bank[r:r + 64, :].rearrange("p (k s) -> p k s", k=4),
                           Y0[r:r + 64, :, :], ALU.add, m))
        c.mem.at = inner
        yield
        c.vector.wait(c.tensor.last)
        c.scalar.wait(c.tensor.last, c.vector.last)


def rwkv_output(c, s, yT):
    col = lambda name, k: s.v[name][:, k:k + 1]
    work = c.carve(4, SEQ)

    def head_mean(src, out, sub):
        c.tensor.wait(c.vector.last)
        for k in range(0, 4, 2):
            i, bank = c.bank()
            m = c.tensor.did(c.mm(bank, c.head_sum, src[:, k:k + 2, :].rearrange("p k s -> p (k s)")))
            b = bank[:, :].rearrange("p (k s) -> p k s", k=2)
            if sub is not None:
                m = c.stt(out[:, k:k + 2, :], b, -1.0 / 64, sub[:, k:k + 2, :], ALU.mult, ALU.add, m)
            else:
                m = c.ts(out[:, k:k + 2, :], b, 1.0 / 64, 64e-5, ALU.mult, ALU.add, m)
            c.read(i, m)
        return m
    head_mean(yT, yT, yT)
    yield
    c.tt(work, yT, yT, ALU.mult)
    m = head_mean(work, work, None)
    yield
    m = c.act(work, work, ACT.Sqrt, m)
    m = c.recip(work, work, m)
    yield
    c.tt(yT, yT, work, ALU.mult)
    for k in range(4):
        m = c.ts(yT[:, k, :], yT[:, k, :], col("rwkv_ln_w_2", k), col("rwkv_ln_b_2", k), ALU.mult, ALU.add)
    c.tt(yT, yT, s.bonus, ALU.add)
    c.tt(yT, yT, s.rwkv_gate, ALU.mult)


def add_branch(c, s, gates, yT, pieces):
    tmp = c.carve(2, SEQ)
    c.tensor.wait(c.vector.last, c.scalar.last)
    first, s.merged_begun = not s.merged_begun, True
    for half in range(2):
        w = c.weights(c.tensor, pieces[half])
        products = [c.product_cols(yT, w[:, :, k * P:(k + 2) * P], range(4)) for k in (0, 2)]
        c.release(products[1][2])
        for k, (i, src, m) in zip((0, 2), products):
            f = 4 * half + k
            g, total = gates[:, f:f + 2, :], s.merged[:, f:f + 2, :]
            if first:
                d = c.tt(total, src, g, ALU.mult, m)
            else:
                d = c.tt(tmp, src, g, ALU.mult, m)
                c.tt(total, total, tmp, ALU.add, d)
            c.read(i, d)
        yield


def moba(c, s, qkT, v_rows, yT, h0):
    n_heads = 4
    scores, total, negmax = c.carve(n_heads, SEQ), c.carve(n_heads), c.carve(n_heads)
    pT = c.carve(n_heads, 2, SEQ)
    pv_done = None
    for t in range(TT):
        keys = P * (t + 1)
        for k in (h0 // 2,):
            for e in range(2):
                i, bank = c.bank()
                hs = slice(64 * e, 64 * e + 64)
                for j in range(2):
                    ins = c.mm(bank[:, j * SEQ:j * SEQ + keys], qkT[hs, k + j, t * P:(t + 1) * P], qkT[hs, 4 + k + j, 0:keys])
                m = c.tensor.did(ins)
                for j in range(2):
                    h = 2 * (k + j) + e
                    part = scores[:, h - h0, 0:keys]
                    m1 = c.ts(part, s.distance[:, t, 0:keys], -2.0 ** -(h + 1), None, ALU.mult, None, m, pv_done)
                    m1 = c.stt(part, bank[:, j * SEQ:j * SEQ + keys], 0.125, part, ALU.mult, ALU.add)
                c.read(i, m1)
            yield
        m = c.softmax_exp(scores, negmax, total, n_heads, keys, m1)
        yield
        sc = scores[:, :, 0:keys]
        m = c.tt(sc, sc, total[:, 0:n_heads].unsqueeze(2).to_broadcast([P, n_heads, keys]), ALU.mult, m)
        done = c.transpose_maps(pT, scores, n_heads, t, c.identity, m)
        pv_done = c.tensor.last
        yield
        c.tensor.wait(*done)
    heads_out(c, yT, h0 // 2, pT, v_rows[:, :, h0 * 64:], n_heads)
    yield
    c.vector.wait(c.tensor.last)
    c.scalar.wait(c.tensor.last)


def s5(c, a, s, u, yT, glu_pieces):
    nc = c.nc
    G16 = 16
    dt, mag, th, turn, sn, cs = (c.carve(G16) for _ in range(6))
    lr, li, den, cr, ci, t1 = (c.carve(G16) for _ in range(6))
    bT, cT = [c.carve(4, P) for _ in range(2)], [c.carve(4, P) for _ in range(2)]
    later = c.mem.at
    b_re, b_im, c_re, c_im = c.carve(16, 16), c.carve(16, 16), c.carve(4, 64), c.carve(4, 64)
    loads = Loads(nc, "ssm_loads")
    for dst, name in ((b_re, "ssm_b_re_2"), (b_im, "ssm_b_im_2")):
        loads.load(nc.scalar, dst, a[name].rearrange("a (i e) q h -> (a e q) i h", e=2))
    for dst, name in ((c_re, "ssm_c_re_2"), (c_im, "ssm_c_im_2")):
        loads.load(nc.scalar, dst, a[name].rearrange("a (k g) h q -> (a g h) k q", g=8))
    re, im = s.v["ssm_a_re_2"], s.v["ssm_a_im_2"]
    m = c.act(dt, s.log_dt, ACT.Exp, c.vector.last)
    m = c.tt(mag, re, dt, ALU.mult, m)
    m = c.act(mag, mag, ACT.Exp, m)
    m = c.tt(th, im, dt, ALU.mult, m)
    m = c.sincos(sn, cs, th, turn, m)
    yield
    c.vector.wait(c.scalar.last, loads.last, c.gpsimd.last)
    c.tt(lr, mag, cs, ALU.mult)
    c.tt(li, mag, sn, ALU.mult)
    c.ts(lr, lr, -1.0, None, ALU.add, None)
    c.tt(den, re, re, ALU.mult)
    c.tt(t1, im, im, ALU.mult)
    c.tt(den, den, t1, ALU.add)
    c.recip(den, den)
    c.tt(cr, lr, re, ALU.mult)
    c.tt(t1, li, im, ALU.mult)
    c.tt(cr, cr, t1, ALU.add)
    c.tt(cr, cr, den, ALU.mult)
    c.tt(ci, li, re, ALU.mult)
    c.tt(t1, lr, im, ALU.mult)
    c.tt(ci, ci, t1, ALU.subtract)
    c.tt(ci, ci, den, ALU.mult)
    bb = [c.carve(G16, 32) for _ in range(2)]
    t2 = c.carve(G16, 16)
    for part in bb:
        c.fill(part, 0.0)
    for e in range(2):
        hs = slice(64 * e, 64 * e + 64)
        n = slice(16 * e, 16 * e + 16)
        crb, cib = (x[hs, :].unsqueeze(2).to_broadcast([64, G16, 16]) for x in (cr, ci))
        bre, bim = b_re[hs, :, :], b_im[hs, :, :]
        c.tt(bb[0][hs, :, n], crb, bre, ALU.mult)
        c.tt(t2[hs, :, :], cib, bim, ALU.mult)
        c.tt(bb[0][hs, :, n], bb[0][hs, :, n], t2[hs, :, :], ALU.subtract)
        c.tt(bb[1][hs, :, n], crb, bim, ALU.mult)
        c.tt(t2[hs, :, :], cib, bre, ALU.mult)
        c.tt(bb[1][hs, :, n], bb[1][hs, :, n], t2[hs, :, :], ALU.add)
    cc = [c.carve(4, P) for _ in range(2)]
    for dst, src, sign in ((cc[0], c_re, 1.0), (cc[1], c_im, -1.0)):
        for e in range(2):
            m = c.ts(dst[:, :, 64 * e:64 * e + 64], src, s.group_odd[:, e:e + 1], sign, ALU.mult, ALU.mult)
    yield
    c.tensor.wait(m)
    done = []
    for src, dst in ((bb[0], bT[0]), (bb[1], bT[1]), (cc[0], cT[0]), (cc[1], cT[1])):
        flat = src.rearrange("p a b -> p (a b)")
        i, bank = c.bank()
        for k in range(4):
            ins = nc.tensor.transpose(bank[:, k * P:(k + 1) * P], flat[:, k * P:(k + 1) * P], c.identity)
        m = c.tensor.did(ins)
        d = c.copy(dst, bank[:, :].rearrange("p (k s) -> p k s", k=4), m, q=c.scalar)
        c.read(i, d)
        done.append(d)
    c.tensor.wait(*done)
    yield
    c.vector.wait(c.tensor.last)
    c.scalar.wait(c.tensor.last, c.vector.last)
    c.mem.at = later
    cos, sin, turns, angle, br, bi, gr, gi = (c.carve(2, SEQ) for _ in range(8))
    for part in range(8):
        k, i0, r0 = part // 2, 2 * part, 64 * (part % 2)
        for j in range(2):
            m = c.ts(angle[:, j, :], s.time, th[:, i0 + j:i0 + j + 1], None, ALU.mult, None, c.scalar.last)
        m = c.sincos(sin, cos, angle, turns, m)
        yield
        c.vector.wait(c.scalar.last)
        for j in range(2):
            i, bank = c.bank()
            ch = slice(r0 + 32 * j, r0 + 32 * j + 32)
            c.mm(bank[:, 0:SEQ], bT[0][ch, k, :], u[ch, k, :])
            m = c.tensor.did(c.mm(bank[:, SEQ:2 * SEQ], bT[1][ch, k, :], u[ch, k, :]))
            c.tt(br[:, j, :], bank[:, 0:SEQ], cos[:, j, :], ALU.mult, m, c.tensor.last)
            c.tt(gi[:, j, :], bank[:, 0:SEQ], sin[:, j, :], ALU.mult)
            c.tt(bi[:, j, :], bank[:, SEQ:2 * SEQ], cos[:, j, :], ALU.mult)
            c.read(i, c.tt(gr[:, j, :], bank[:, SEQ:2 * SEQ], sin[:, j, :], ALU.mult))
        c.tt(br, br, gr, ALU.add)
        c.tt(bi, bi, gi, ALU.subtract)
        yield
        v = c.vector
        for j in range(2):
            keep = mag[:, i0 + j:i0 + j + 1].to_broadcast([P, SEQ])
            for src, dst in ((br, gr), (bi, gi)):
                m = v.did(v.after().tensor_tensor_scan(dst[:, j, :], keep, src[:, j, :], 0.0, ALU.mult, ALU.add))
        yield
        c.tt(br, cos, gr, ALU.mult)
        c.tt(bi, sin, gr, ALU.mult)
        c.tt(gr, sin, gi, ALU.mult)
        c.tt(gi, cos, gi, ALU.mult)
        c.tt(br, br, gr, ALU.subtract)
        m = c.tt(bi, bi, gi, ALU.add)
        c.tensor.wait(m)
        i, bank = c.bank()
        for j in range(2):
            ch = slice(r0 + 32 * j, r0 + 32 * j + 32)
            c.mm(bank[ch, 0:SEQ], cT[0][:, k, ch], br[:, j, :], True, False)
            ins = c.mm(bank[ch, 0:SEQ], cT[1][:, k, ch], bi[:, j, :], False, True)
        m = c.tensor.did(ins)
        ch = slice(r0, r0 + 64)
        m = c.stt(yT[ch, k, :], u[ch, k, :], s.v["ssm_d_2"][ch, k:k + 1], bank[ch, 0:SEQ], ALU.mult, ALU.add, m)
        c.read(i, m)
    m = c.act(yT, yT, ACT.Gelu_apprx_tanh, m)
    c.tensor.wait(m)
    c.mem.at = later
    glu = c.carve(4, SEQ), c.carve(4, SEQ)
    for half in range(2):
        w = c.weights(c.tensor, glu_pieces[half])
        products = [c.product_cols(yT, w[:, :, k * P:(k + 2) * P], range(4)) for k in (0, 2)]
        c.release(products[1][2])
        for k, (i, src, m) in zip((0, 2), products):
            for j in range(2):
                bias = s.v["ssm_glu_b_2"][:, 4 * half + k + j:4 * half + k + j + 1]
                d = c.act(glu[half][:, k + j, :], src[:, j, :], ACT.Sigmoid if half else ACT.Identity, m, bias=bias)
            c.read(i, d)
        yield
    c.tt(yT, glu[0], glu[1], ALU.mult, d, c.tensor.last)


def layer_norm(c, out, x, w, b, small, junk, *marks):
    for t in range(TT):
        m = c.reduce(small[:, t:t + 1], x[:, t, :], ALU.add, *marks)
        m = c.ts(small[:, t:t + 1], small[:, t:t + 1], 1.0 / D, None, ALU.mult, None)
        m = c.ts(x[:, t, :], x[:, t, :], small[:, t:t + 1], None, ALU.subtract, None)
        m = c.sumsq(small[:, 2 + t:3 + t], x[:, t, :], x[:, t, :], junk)
    m = c.rsqrt(small[:, 2:4], small[:, 2:4], D, 1e-5, m)
    for t in range(TT):
        m = c.stt(x[:, t, :], x[:, t, :], small[:, 2 + t:3 + t], w, ALU.mult, ALU.mult, m)
        m = c.tt(out[:, t, :], x[:, t, :], b, ALU.add, m)
    return m


def route(c, s, x1T):
    nc = c.nc
    i, bank = c.bank()
    for t in range(TT):
        for k in range(KT):
            ins = c.mm(bank[:, t * 36:t * 36 + 36], x1T[:, k, t * P:(t + 1) * P], s.w_router[:, k, :], k == 0, k == KT - 1)
    m = c.tensor.did(ins)
    logits = c.carve(TT, 36)
    m = c.tt(logits, bank[:, 0:72].rearrange("p (t n) -> p t n", t=TT), s.b_router.unsqueeze(1).to_broadcast([P, TT, 36]),
             ALU.add, m)
    c.read(i, m)
    top, pick, work, hot = c.carve(TT), c.carve(TT), c.carve(TT, 32), [c.carve(TT, 32) for _ in range(2)]
    group, p_group, exps = c.carve(TT, 4), c.carve(TT), c.carve(TT, 4)
    wide = lambda t, n: t.unsqueeze(2).to_broadcast([P, TT, n])

    def first_of(out, values, best, n):
        index = s.time[:, 0:n].unsqueeze(1).to_broadcast([P, TT, n])
        w = work[:, :, 0:n]
        c.tt(w, values, wide(best, n), ALU.is_lt)
        c.stt(w, w, 1000.0, index, ALU.mult, ALU.add)
        c.reduce(pick, w, ALU.min)
        return c.tt(out, index, wide(pick, n), ALU.is_equal)
    g = logits[:, :, 0:4]
    c.reduce(top, g, ALU.max)
    first_of(group, g, top, 4)
    m = c.tt(exps, g, wide(top, 4), ALU.subtract)
    m = c.act(exps, exps, ACT.Exp, m)
    m = c.reduce(p_group, exps, ALU.add, m)
    c.recip(p_group, p_group)
    e = c.carve(TT, 32)
    outside = c.carve(TT, 4)
    c.ts(outside, group, -1.0, 3e38, ALU.add, ALU.mult)
    for t in range(TT):
        inside = group[:, t, :].unsqueeze(2).to_broadcast([P, 4, 8])
        ev, lv = (v.rearrange("p (g n) -> p g n", g=4) for v in (e[:, t, :], logits[:, t, 4:36]))
        c.tt(ev, lv, inside, ALU.mult)
        c.tt(ev, ev, outside[:, t, :].unsqueeze(2).to_broadcast([P, 4, 8]), ALU.add)
    second = c.carve(TT)
    c.reduce(top, e, ALU.max)
    first_of(hot[0], e, top, 32)
    c.stt(e, hot[0], -3.3e38, e, ALU.mult, ALU.add)
    c.ts(e, e, -3.3e38, None, ALU.max, None)
    c.reduce(second, e, ALU.max)
    first_of(hot[1], e, second, 32)
    m = c.tt(second, second, top, ALU.subtract)
    m = c.act(second, second, ACT.Exp, m)
    c.ts(top, second, 1.0, None, ALU.add, None, m)
    c.recip(top, top)
    c.tt(top, top, p_group, ALU.mult)
    c.tt(second, second, top, ALU.mult)
    c.tt(hot[0], hot[0], wide(top, 32), ALU.mult)
    c.tt(hot[1], hot[1], wide(second, 32), ALU.mult)
    m = c.tt(hot[0], hot[0], hot[1], ALU.add)
    c.tensor.wait(m)
    i, bank = c.bank()
    for t in range(TT):
        ins = nc.tensor.transpose(bank[0:32, t * P:(t + 1) * P], hot[0][:, t, :], c.identity)
    m = c.tensor.did(ins)
    wT = c.carve(SEQ)
    m = c.copy(wT[0:32, :], bank[0:32, 0:SEQ], m)
    c.read(i, m)
    spread = s.weight
    some = c.carve(8, SEQ)
    for e0 in range(0, EXPERTS, 8):
        m = c.tt(some[0:32], wT[0:32].unsqueeze(1).to_broadcast([32, 8, SEQ]),
                 c.identity[0:32, e0:e0 + 8].unsqueeze(2).to_broadcast([32, 8, SEQ]), ALU.mult, c.tensor.last)
        c.tensor.wait(m)
        for n in range(0, 8, 2):
            i, bank = c.bank()
            m = c.tensor.did(c.mm(bank, c.ones[0:32, :], some[0:32, n:n + 2, :].rearrange("p a s -> p (a s)")))
            c.read(i, c.copy(spread[:, e0 + n:e0 + n + 2, :], bank[:, :].rearrange("p (a s) -> p a s", a=2), m, q=c.scalar))


def experts(c, a, s, x1T, y):
    nc = c.nc
    c.meet()
    c.sync.wait(c.tensor.last)
    w_gate, w_up, w_down = (a[name].rearrange("a e (k p) n -> (a e) p k n", p=P)
                            for name in ("expert_w_gate_2", "expert_w_up_2", "expert_w_down_2"))
    slots = [(k_tiles(8)(c.ring[2 * e]), k_tiles(8)(c.ring[2 * e + 1]), c.carve(2, D)) for e in range(2)]
    hidden, silu = [c.carve(2, SEQ) for _ in range(2)], [c.carve(2, SEQ) for _ in range(2)]
    banks = [(c.banks[4 + e].rearrange("p (j s) -> p j s", s=SEQ), c.banks[6 + e].rearrange("p (j s) -> p j s", s=SEQ))
             for e in range(2)]
    out_banks, zero = c.banks[0:4], c.carve(P)
    full = [[nc.alloc_semaphore(f"{name}_full{e}") for name in ("gate", "up", "down")] for e in range(2)]

    def load(n, e, parity):
        source = (w_gate, w_up, w_down)[n]
        source = source[e] if isinstance(e, int) else source[bass.ds(e, 1)].rearrange("a p k n -> p (a k) n")
        nc.sync.dma_start(slots[parity][n], source).then_inc(full[parity][n], 16)

    m = c.fill(zero, 0.0)
    c.tensor.wait(m)
    for bank in out_banks:
        ins = c.mm(bank, zero, s.weight[:, 0:2, :].rearrange("p a s -> p (a s)"))
    c.tensor.did(ins)
    t0, s0, v0 = c.tensor.count, c.scalar.count, c.vector.count
    tensor, scalar, vector = c.tensor, c.scalar, c.vector
    gate_done = lambda e: e * 3 + t0
    up_done = lambda e: e * 3 + (t0 + 1)
    down_done = lambda e: e * 3 + (t0 + 5)
    silu_done = lambda e: e + (s0 + 1)
    weighted_done = lambda e: e * 2 + (v0 + 1)
    hidden_done = lambda e: e * 2 + (v0 + 2)

    def gate_up(e, parity, turn, first=False):
        pe = nc.tensor
        for n, bank in enumerate(banks[parity]):
            pe.wait_ge(full[parity][n], turn * 16 + 16)
            if not first:
                if n == 0:
                    pe.wait_ge(scalar.sem, silu_done(e - 2))
                else:
                    pe.wait_ge(vector.sem, hidden_done(e - 2))
            for j in range(2):
                for k in range(KT):
                    ins = c.mm(bank[:, j, :], slots[parity][n][:, k, j * P:(j + 1) * P], x1T[:, k, :], k == 0, k == KT - 1)
            ins.then_inc(tensor.sem, 1)
        gate, up = banks[parity]
        gate_at, up_at = (t0 + 1, t0 + 2) if first and parity == 0 else (gate_done(e), up_done(e))
        nc.scalar.wait_ge(tensor.sem, gate_at)
        if not first:
            nc.scalar.wait_ge(vector.sem, hidden_done(e - 2))
        nc.scalar.activation(silu[parity], gate, ACT.Silu).then_inc(scalar.sem, 1)
        weight = s.weight[:, e:e + 1, :] if isinstance(e, int) else s.weight[:, bass.ds(e, 1), :]
        nc.vector.wait_ge(scalar.sem, silu_done(e))
        nc.vector.tensor_tensor(silu[parity], silu[parity], weight.to_broadcast([P, 2, SEQ]),
                                ALU.mult).then_inc(vector.sem, 1)
        nc.vector.wait_ge(tensor.sem, up_at)
        nc.vector.wait_ge(vector.sem, weighted_done(e))
        if not first:
            nc.vector.wait_ge(tensor.sem, down_done(e - 2))
        nc.vector.tensor_tensor(hidden[parity], up, silu[parity], ALU.mult).then_inc(vector.sem, 1)

    def down(e, parity, turn):
        nc.tensor.wait_ge(full[parity][2], turn * 16 + 16)
        nc.tensor.wait_ge(vector.sem, hidden_done(e))
        for t in range(TT):
            for half in range(2):
                for k in range(2):
                    ins = nc.tensor.matmul(out_banks[2 * t + half], hidden[parity][:, k, t * P:(t + 1) * P],
                                           slots[parity][2][:, k, half * 512:(half + 1) * 512], start=False,
                                           stop=True, skip_group_check=True)
        ins.then_inc(tensor.sem, 1)

    def reload(e, parity, parts, done):
        for n in parts:
            nc.sync.wait_ge(tensor.sem, done[n])
            load(n, e + 2, parity)

    for e in range(2):
        for n in range(3):
            load(n, e, e)
    gate_up(0, 0, 0, first=True)
    reload(0, 0, (0, 1), (t0 + 1, t0 + 2))
    gate_up(1, 1, 0, first=True)
    reload(1, 1, (0, 1), (gate_done(1), up_done(1)))
    down(0, 0, 0)
    reload(0, 0, (2,), (0, 0, down_done(0)))

    def step(e, parity, turn_up, turn_down, more_up=True, more_down=True):
        gate_up(e + 1, 1 - parity, turn_up)
        if more_up:
            reload(e + 1, 1 - parity, (0, 1), (gate_done(e + 1), up_done(e + 1)))
        down(e, parity, turn_down)
        if more_down:
            reload(e, parity, (2,), (0, 0, down_done(e)))

    turns = (EXPERTS - 4) // 2
    with nc.Fori(0, turns) as n:
        step(n * 2 + 1, 1, n + 1, n)
        step(n * 2 + 2, 0, n + 1, n + 1)
    last = EXPERTS - 3
    step(last, 1, turns + 1, turns, more_up=False)
    step(last + 1, 0, turns + 1, turns + 1, more_up=False, more_down=False)
    down(last + 2, 1, turns + 1)
    tensor.count, scalar.count, vector.count = t0 + 3 * EXPERTS, s0 + EXPERTS, v0 + 2 * EXPERTS
    for q in (tensor, scalar, vector):
        q.seen = {}
    for t in range(TT):
        for half in range(2):
            m = c.copy(y[:, t, half * 512:(half + 1) * 512], out_banks[2 * t + half], tensor.last)
    return m


def second_block(c, a, x):
    nc = c.nc
    s = State()
    c.mem = Region(c.arena, 0, ARENA)
    second_constants(c, s)
    vectors_2(c, a, s)
    s.merged, s.merged_begun = c.carve(8, SEQ), False
    pieces = second_pieces(a)
    xT = c.hT
    c.vector.wait(c.gpsimd.last)
    done = c.columns_from_rows(xT, x, c.identity, KT, None)
    c.tensor.wait(*done)

    def cols(dst, piece):
        w = c.weights(c.tensor, piece)
        i, src, m = c.product_cols(xT, w, range(KT))
        c.release(m)
        c.read(i, c.copy(dst, src, m, q=c.scalar))

    def branch_gates(gates, branch):
        for n in range(4):
            w = c.weights(c.tensor, pieces["gate"][branch][n])
            i, src, m = c.product_cols(xT, w, range(KT))
            c.release(m)
            for j in range(2):
                f = 8 * branch + 2 * n + j
                d = c.act(gates[:, 2 * n + j, :], src[:, j, :], ACT.Sigmoid, m, bias=s.v["gate_b_2"][:, f:f + 1])
            c.read(i, d)
            yield

    def hand_over():
        c.meet()
        yield

    def rwkv_branch():
        yT = c.carve(4, SEQ)
        yield from rwkv_input(c, a, s, cols, pieces["rwkv"])
        yield from hand_over()
        c.mem.at = s.rwkv_end
        yield from rwkv_scan(c, s, yT)
        yield from hand_over()
        c.mem.at = s.rwkv_end
        gates = c.carve(8, SEQ)
        yield from branch_gates(gates, 0)
        yield from rwkv_output(c, s, yT)
        yield from add_branch(c, s, gates, yT, pieces["up"][0])

    def moba_and_ssm_branches():
        start = c.mem.at
        yT, qkT, v_rows = c.carve(4, SEQ), c.carve(8, SEQ), c.carve(TT, 512)
        for n in range(4):
            cols(qkT[:, 2 * n:2 * n + 2, :], pieces["moba"][n])
            yield
        for n in range(2):
            w = c.weights(c.tensor, pieces["moba"][4 + n])
            i, src, m = c.product_rows(xT, w, range(KT))
            c.release(m)
            c.read(i, c.copy(v_rows[:, :, 256 * n:256 * n + 256], src, m, q=c.scalar))
            yield
        attention = c.mem.at
        for h0 in (0, 4):
            c.mem.at = attention
            c.tensor.wait(c.scalar.last)
            yield from moba(c, s, qkT, v_rows, yT, h0)
        c.mem.at = attention
        gates = c.carve(8, SEQ)
        yield from branch_gates(gates, 1)
        yield from add_branch(c, s, gates, yT, pieces["up"][1])
        yield from hand_over()
        c.mem.at = start
        yT, u = c.carve(4, SEQ), c.carve(4, SEQ)
        for n in range(2):
            cols(u[:, 2 * n:2 * n + 2, :], pieces["ssm"][n])
            yield
        yield from s5(c, a, s, u, yT, pieces["glu"])
        gates = c.carve(8, SEQ)
        yield from branch_gates(gates, 2)
        yield from add_branch(c, s, gates, yT, pieces["up"][2])

    tail = c.mem.rest()
    other = c.mem.rest(SSM_MOBA_FLOATS)
    c.weave((rwkv_branch(), c.mem), (moba_and_ssm_branches(), other))
    c.meet()
    c.mem = tail
    y, small, junk = c.carve(TT, D), c.carve(4), c.carve(D)
    ln = [c.carve(D) for _ in range(4)]
    s.w_router, s.b_router = c.carve(KT, 36), c.carve(36)
    loads = Loads(nc, "last_loads")
    load = lambda dst, src: loads.load(nc.scalar, dst, src)
    for dst, name in zip(ln, ("ln1_w_2", "ln1_b_2", "ln2_w_2", "ln2_b_2")):
        load(dst, a[name].to_broadcast([P, D]))
    load(s.w_router[:, :, 0:4], a["router_group_w_2"].rearrange("a (k p) n -> p (a k) n", p=P))
    load(s.w_router[:, :, 4:36], a["router_expert_w_2"].rearrange("a (k p) n -> p (a k) n", p=P))
    load(s.b_router[:, 0:4], a["router_group_b_2"].to_broadcast([P, 4]))
    load(s.b_router[:, 4:36], a["router_expert_b_2"].to_broadcast([P, 32]))
    for _ in out_rows(c, s.merged, y, pieces["out"]):
        pass
    for t in range(TT):
        m = c.stt(y[:, t, :], x[:, t, :], ALPHA, y[:, t, :], ALU.mult, ALU.add)
    m = layer_norm(c, x, y, ln[0], ln[1], small, junk, m, loads.last)
    x1T = c.hT
    c.tensor.wait(loads.last)
    done = c.columns_from_rows(x1T, x, c.identity, KT, None, m)
    c.tensor.wait(*done)
    s.weight = c.carve(EXPERTS, SEQ)
    route(c, s, x1T)
    experts(c, a, s, x1T, y)
    for t in range(TT):
        m = c.stt(y[:, t, :], x[:, t, :], ALPHA, y[:, t, :], ALU.mult, ALU.add)
    layer_norm(c, x, y, ln[2], ln[3], small, junk, m)


def build(nc, a, out):
    c = Core(nc)
    x = c.keep("x", TT, D)
    c.hT = c.keep("hT", KT, SEQ)
    constants(c)
    loads = Loads(nc, "x_load")
    loads.load(nc.scalar, x, a["x"].rearrange("a (t p) d -> p (a t) d", p=P))
    c.vector.wait(loads.last)
    c.scalar.wait(loads.last)
    first_block(c, a, x)
    second_block(c, a, x)
    s_out = nc.alloc_semaphore("stored")
    c.sync.wait(c.vector.last)
    nc.sync.dma_start(out.rearrange("a (t p) d -> p (a t) d", p=P), x).then_inc(s_out, 16)
    nc.sync.wait_ge(s_out, 16)


INPUTS = [
    'x', 'c', 'positions', 'w_ada', 'b_ada', 'norm_g', 'w_in', 'diff_lambda', 'diff_subln_g',
    'mla_q_norm_g', 'w_uq', 'mla_kv_norm_g', 'w_ukv', 'conv_w', 'conv_b', 'dt_bias', 'a_log', 'd_skip',
    'ssm_norm_g', 'w_out', 'w_up', 'w_down', 'w_in_2', 'rwkv_mu_2', 'rwkv_w0_2', 'rwkv_w2_2',
    'rwkv_a0_2', 'rwkv_a2_2', 'rwkv_g2_2', 'rwkv_k_k_2', 'rwkv_k_a_2', 'rwkv_r_k_2', 'rwkv_ln_w_2',
    'rwkv_ln_b_2', 'ssm_a_re_2', 'ssm_a_im_2', 'ssm_b_re_2', 'ssm_b_im_2', 'ssm_c_re_2', 'ssm_c_im_2',
    'ssm_d_2', 'ssm_log_dt_2', 'ssm_glu_w_2', 'ssm_glu_b_2', 'w_up_rwkv_2', 'w_up_moba_2', 'w_up_ssm_2',
    'gate_b_2', 'w_out_2', 'ln1_w_2', 'ln1_b_2', 'router_group_w_2', 'router_group_b_2',
    'router_expert_w_2', 'router_expert_b_2', 'expert_w_gate_2', 'expert_w_up_2', 'expert_w_down_2',
    'ln2_w_2', 'ln2_b_2'
]


def kernel(**inputs):
    import numpy as _np
    import concourse.bacc as _bacc
    from concourse import mybir as _mybir
    from concourse.bass_utils import run_bass_kernel_spmd as _run

    nc = _bacc.Bacc("TRN2", target_bir_lowering=False, num_devices=1)
    arrays, handles = {}, {}
    for name in INPUTS:
        array = _np.ascontiguousarray(inputs[name])
        arrays[f"in_{name}"] = array
        handles[name] = nc.dram_tensor(f"in_{name}", array.shape, _mybir.dt.from_np(array.dtype),
                                       kind="ExternalInput").ap()
    out = nc.dram_tensor("out", (1, SEQ, D), F32, kind="ExternalOutput").ap()
    build(nc, handles, out)
    result = _run(nc, [arrays], core_ids=[0])
    return result.results[0]["out"]
```

```python
import math

import numpy as np

import concourse.bass as bass
from concourse import mybir
from concourse.alu_op_type import AluOpType as ALU

F32 = mybir.dt.float32
F32R = mybir.dt.float32r
I32 = mybir.dt.int32
ACT = mybir.ActivationFunctionType
AX = mybir.AxisListType.X

P = 128
SEQ = 256
TT = SEQ // P
D = 1024
KT = D // P
DEPTH = 2
FF = 4 * D
SLOT = 2048
RING = 4
EXPERTS, D_EXPERT = 32, 256
TWO_PI = 2 * math.pi
ARENA = 40448
ROUND = 1.5 * 2.0 ** 23


class Queue:

    def __init__(self, nc, engine, name, ordered=True):
        self.engine, self.sem, self.ordered = engine, nc.alloc_semaphore(name), ordered
        self.count, self.own, self.seen = 0, 0, {}

    def wait(self, *marks):
        for mark in marks:
            if mark is not None and self.seen.get(mark[0].name, 0) < mark[1]:
                self.engine.wait_ge(mark[0], mark[1])
                self.seen[mark[0].name] = mark[1]

    def after(self, *marks):
        self.wait(*marks)
        if self.ordered:
            self.wait(self.last)
        return self.engine

    def did(self, instruction):
        instruction.then_inc(self.sem, 1)
        self.count += 1
        self.own = self.count
        return self.last

    @property
    def last(self):
        return (self.sem, self.own) if self.own else None


class Loads:

    def __init__(self, nc, name):
        self.sem, self.count = nc.alloc_semaphore(name), 0

    def load(self, engine, out, in_):
        engine.dma_start(out, in_).then_inc(self.sem, 16)
        self.count += 16

    @property
    def last(self):
        return (self.sem, self.count) if self.count else None


class Region:

    def __init__(self, arena, start, end):
        self.arena, self.at, self.end = arena, start, end

    def carve(self, *shape):
        n = int(np.prod(shape))
        piece = self.arena[:, self.at:self.at + n]
        self.at += n
        assert self.at <= self.end, (self.at, self.end)
        if len(shape) == 2:
            piece = piece.rearrange("p (a b) -> p a b", b=shape[1])
        if len(shape) == 3:
            piece = piece.rearrange("p (a b c) -> p a b c", b=shape[1], c=shape[2])
        return piece

    def rest(self, size=None):
        start = self.at
        if size is None:
            return Region(self.arena, start, self.end)
        self.at += size
        assert self.at <= self.end, (self.at, self.end)
        return Region(self.arena, start, start + size)


class SplitWeights:

    def __init__(self, c, name, pieces, buffers=3):
        self.c, self.pieces = c, list(pieces)
        self.pairs = [c.carve_split(f"{name}{n}", SLOT) for n in range(buffers)]
        self.free, self.given, self.ready = [()] * buffers, 0, []
        for _ in range(buffers - 1):
            self.prepare()

    def prepare(self):
        n = self.given + len(self.ready)
        if n < len(self.pieces):
            view, place = self.pieces[n][0], n % len(self.pairs)
            w = self.c.weights(self.c.scalar, self.pieces[n])
            pair = tuple(view(buffer) for buffer in self.pairs[place])
            m = self.c.split(pair, w, *self.free[place])
            self.c.release(m)
            self.ready.append((pair, m))

    def take(self):
        pair, m = self.ready.pop(0)
        self.given += 1
        self.prepare()
        self.c.tensor.wait(m)
        return pair

    def release(self, mark):
        self.free[(self.given - 1) % len(self.pairs)] = (mark,)


class Core:

    def __init__(self, nc):
        self.nc = nc
        self.tensor = Queue(nc, nc.tensor, "tensor_done", ordered=False)
        self.vector = Queue(nc, nc.vector, "vector_done")
        self.scalar = Queue(nc, nc.scalar, "scalar_done")
        self.gpsimd = Queue(nc, nc.gpsimd, "gpsimd_done")
        self.sync = Queue(nc, nc.sync, "sync_done")
        self.banks = [nc.alloc_psum_tensor(f"bank{i}", [P, 512], F32).ap() for i in range(8)]
        self.bank_free = [[] for _ in self.banks]
        self.bank_next, self.bank_used, self.held = 0, list(range(8)), set()
        self.ring = [nc.alloc_sbuf_tensor(f"weights{i}", [P, SLOT], F32).ap() for i in range(RING)]
        self.ring_full = [nc.alloc_semaphore(f"weights{i}_full") for i in range(RING)]
        self.ring_free, self.ring_count = [()] * RING, 0
        self.arena_start = nc.sbuf_base
        self.arena = nc.alloc_sbuf_tensor("arena", [P, ARENA], F32).ap()
        self.mem = Region(self.arena, 0, ARENA)

    def keep(self, name, *shape, dtype=F32):
        return self.nc.alloc_sbuf_tensor(name, [P, *shape], dtype).ap()

    def carve(self, *shape):
        return self.mem.carve(*shape)

    def carve_split(self, name, *shape):
        pair = []
        for part in ("hi", "lo"):
            self.mem.at += -self.mem.at % 8
            start = self.arena_start + 4 * self.mem.at
            self.carve(*shape)
            pair.append(self.nc.alloc_sbuf_tensor_at(f"{name}_{part}", [P, *shape], F32R, offset=start, align_bytes=32).ap())
        return tuple(pair)

    def bank(self):
        i = self.bank_used[self.bank_next % len(self.bank_used)]
        while i in self.held:
            self.bank_next += 1
            i = self.bank_used[self.bank_next % len(self.bank_used)]
        self.bank_next += 1
        self.tensor.wait(*self.bank_free[i])
        self.bank_free[i] = []
        return i, self.banks[i]

    def read(self, i, *marks):
        self.bank_free[i] += [m for m in marks if m]

    def weights(self, queue, piece):
        (view, source), s = piece, self.ring_count % RING
        self.sync.wait(*self.ring_free[s])
        self.nc.sync.dma_start(view(self.ring[s]), source).then_inc(self.ring_full[s], 16)
        queue.wait((self.ring_full[s], 16 * (self.ring_count // RING + 1)))
        self.ring_count += 1
        return view(self.ring[s])

    def release(self, *readers):
        self.ring_free[(self.ring_count - 1) % RING] = readers

    def split(self, pair, src, *marks):
        hi, lo = pair
        m = self.copy(hi, src, *marks, q=self.scalar)
        return self.tt(lo, src, hi.bitcast(F32), ALU.subtract, m)

    def mm_split(self, out, lhsT, rhs, start=True, stop=True):
        self.mm(out, lhsT[0], rhs[0], start, False)
        self.mm(out, lhsT[0], rhs[1], False, False)
        return self.mm(out, lhsT[1], rhs[0], False, stop)

    def split_cols(self, xT, w, tiles=KT):
        i, bank = self.bank()
        for j in range(2):
            for k in range(tiles):
                ins = self.mm_split(bank[:, j * SEQ:(j + 1) * SEQ], [v[:, k, j * P:(j + 1) * P] for v in w],
                                    [v[:, k, :] for v in xT], k == 0, k == tiles - 1)
        return i, bank[:, :].rearrange("p (j s) -> p j s", s=SEQ), self.tensor.did(ins)

    def meet(self):
        queues = [self.tensor, self.vector, self.scalar, self.gpsimd]
        for q in queues:
            q.wait(*(other.last for other in queues))

    def weave(self, *streams, lead=0):
        queues = (self.tensor, self.vector, self.scalar, self.gpsimd)
        streams, turn = [(steps, region, {q.sem.name: q.count for q in queues}) for steps, region in streams], 0
        while streams:
            for stream in list(streams) if turn >= lead else streams[:1]:
                steps, self.mem, own = stream
                for q in queues:
                    q.own = own[q.sem.name]
                if next(steps, "end") == "end":
                    streams.remove(stream)
                own.update({q.sem.name: q.own for q in queues})
            turn += 1
        for q in queues:
            q.own = q.count

    def mm(self, out, lhsT, rhs, start=True, stop=True):
        return self.nc.tensor.matmul(out, lhsT, rhs, start=start, stop=stop)

    def tt(self, out, a, b, op, *marks, q=None):
        q = q or self.vector
        return q.did(q.after(*marks).tensor_tensor(out, a, b, op))

    def ts(self, out, a, s1, s2, op0, op1, *marks, q=None):
        q = q or self.vector
        if op1 is None:
            return q.did(q.after(*marks).tensor_scalar(out, a, s1, None, op0))
        return q.did(q.after(*marks).tensor_scalar(out, a, s1, s2, op0, op1))

    def stt(self, out, a, s, b, op0, op1, *marks):
        q = self.vector
        return q.did(q.after(*marks).scalar_tensor_tensor(out, a, s, b, op0, op1))

    def copy(self, out, a, *marks, q=None):
        q = q or self.vector
        if q is self.scalar:
            return q.did(q.after(*marks).activation(out, a, ACT.Copy))
        return q.did(q.after(*marks).tensor_copy(out, a))

    def act(self, out, a, func, *marks, **kw):
        q = self.scalar
        return q.did(q.after(*marks).activation(out, a, func, **kw))

    def reduce(self, out, a, op, *marks, negate=None):
        q = self.vector
        return q.did(q.after(*marks).tensor_reduce(out, a, AX, op, negate=negate))

    def recip(self, out, a, *marks):
        q = self.vector
        return q.did(q.after(*marks).reciprocal(out, a))

    def fill(self, out, value, *marks, q=None):
        q = q or self.vector
        return q.did(q.after(*marks).memset(out, value))

    def sumsq(self, out, a, b, junk, *marks):
        q = self.vector
        return q.did(q.after(*marks).tensor_tensor_reduce(out=junk, in0=a, in1=b, scale=1.0, scalar=0.0,
                                                          op0=ALU.mult, op1=ALU.add, accum_out=out))

    def rsqrt(self, out, total, n, eps, *marks):
        m = self.ts(out, total, 1.0 / n, eps, ALU.mult, ALU.add, *marks)
        m = self.act(out, out, ACT.Sqrt, m)
        return self.recip(out, out, m)

    def columns_from_rows(self, out, rows, identity, tiles, evacuate, *marks):
        self.tensor.wait(*marks)
        done = []
        for k0 in range(0, tiles, 2):
            i, bank = self.bank()
            n = min(2, tiles - k0)
            for k in range(k0, k0 + n):
                for t in range(TT):
                    c = ((k - k0) * TT + t) * P
                    ins = self.nc.tensor.transpose(bank[:, c:c + P], rows[:, t, k * P:(k + 1) * P], identity)
            m = self.tensor.did(ins)
            if evacuate is None:
                src = bank[:, 0:n * SEQ].rearrange("p (k s) -> p k s", s=SEQ)
                q = self.scalar if (k0 // 2) % 2 else self.vector
                d = [self.copy(out[:, k0:k0 + n, :], src, m, q=q)]
            else:
                d = [evacuate(k, out[:, k, :], bank[:, (k - k0) * SEQ:(k - k0 + 1) * SEQ], m)
                     for k in range(k0, k0 + n)]
            self.read(i, *d)
            done += d
        return done

    def product_cols(self, xT, w, tiles, width=2):
        i, bank = self.bank()
        for j in range(width):
            for n, k in enumerate(tiles):
                ins = self.mm(bank[:, j * SEQ:(j + 1) * SEQ], w[:, n, j * P:(j + 1) * P], xT[:, k, :],
                              start=(n == 0), stop=(n == len(tiles) - 1))
        return i, bank[:, 0:width * SEQ].rearrange("p (j s) -> p j s", s=SEQ), self.tensor.did(ins)

    def product_rows(self, xT, w, tiles, width=256):
        i, bank = self.bank()
        for t in range(TT):
            for n, k in enumerate(tiles):
                ins = self.mm(bank[:, t * width:(t + 1) * width], xT[:, k, t * P:(t + 1) * P], w[:, n, :],
                              start=(n == 0), stop=(n == len(tiles) - 1))
        return i, bank[:, 0:TT * width].rearrange("p (t n) -> p t n", t=TT), self.tensor.did(ins)

    def sincos(self, sin, cos, x, k, *marks):
        c1 = 6.28125
        c2 = round((TWO_PI - c1) * 2 ** 20) / 2 ** 20
        c3 = TWO_PI - c1 - c2
        m = self.ts(k, x, 1 / TWO_PI, ROUND, ALU.mult, ALU.add, *marks)
        m = self.ts(k, k, -ROUND, None, ALU.add, None)
        for c in (c1, c2, c3):
            m = self.stt(x, k, -c, x, ALU.mult, ALU.add)
        m = self.ts(x, x, 3.1415925, -3.1415925, ALU.min, ALU.max)
        ms = self.act(sin, x, ACT.Sin, m)
        m = self.act(cos, x, ACT.Sin, m, scale=0.5)
        m = self.tt(cos, cos, cos, ALU.mult, m)
        m = self.ts(cos, cos, -2.0, 1.0, ALU.mult, ALU.add)
        return [m, ms]

    def softmax_exp(self, scores, neg_max, total, n, keys, *marks):
        m = self.reduce(neg_max[:, 0:n], scores[:, 0:n, 0:keys], ALU.max, *marks, negate=True)
        for h in range(n):
            m = self.act(scores[:, h, 0:keys], scores[:, h, 0:keys], ACT.Exp, m,
                         bias=neg_max[:, h:h + 1], accum_out=total[:, h:h + 1])
        return self.recip(total[:, 0:n], total[:, 0:n], m)

    def transpose_maps(self, pT, maps, n, t, identity, *marks):
        self.tensor.wait(*marks)
        done = []
        kts = t + 1
        per = 4 // kts
        for h0 in range(0, n, per):
            i, bank = self.bank()
            for h in range(h0, h0 + per):
                for kt in range(kts):
                    c = ((h - h0) * kts + kt) * P
                    ins = self.nc.tensor.transpose(bank[:, c:c + P], maps[:, h, kt * P:(kt + 1) * P], identity)
            m = self.tensor.did(ins)
            src = bank[:, :].rearrange("p (h k s) -> p h k s", h=per, k=kts)
            q = self.scalar if (h0 // per) % 2 else self.vector
            d = self.copy(pT[:, h0:h0 + per, 0:kts, t * P:(t + 1) * P], src, m, q=q)
            self.read(i, d)
            done.append(d)
        return done


def constants(c):
    g = c.gpsimd

    def select(out, cmp, fill, base, pattern, channel):
        return g.did(g.after().affine_select(out=out, in_=out, compare_op=cmp, fill=fill, base=base,
                                             pattern=pattern, channel_multiplier=channel))

    c.identity = c.keep("identity", P)
    c.fill(c.identity, 0.0, q=g)
    select(c.identity, ALU.not_equal, 1.0, 0, [[-1, P]], 1)
    c.ones = c.keep("ones", P)
    c.fill(c.ones, 1.0, q=g)
    c.head_sum = c.keep("head_sum", P)
    c.fill(c.head_sum, 1.0, q=g)
    select(c.head_sum[:, 0:64], ALU.is_ge, 0.0, 63, [[0, 64]], -1)
    select(c.head_sum[:, 64:P], ALU.is_ge, 0.0, -64, [[0, 64]], 1)


def first_constants(c):
    g = c.gpsimd

    def select(out, cmp, fill, base, pattern, channel):
        return g.did(g.after().affine_select(out=out, in_=out, compare_op=cmp, fill=fill, base=base,
                                             pattern=pattern, channel_multiplier=channel))
    c.chunk_mask = c.carve(TT, SEQ)
    c.fill(c.chunk_mask, 0.0, q=g)
    for t in range(TT):
        for half in range(2):
            rows = c.chunk_mask[64 * half:64 * half + 64, t, :]
            select(rows, ALU.is_ge, -1e30, t * P + 64 * half + 63, [[-1, SEQ]], 0)
    c.causal = c.carve(TT, SEQ)
    c.fill(c.causal, 1.0, q=g)
    for t in range(TT):
        select(c.causal[:, t, :], ALU.is_ge, 0.0, -t * P, [[1, SEQ]], -1)


OFF_Q, OFF_K, OFF_V, OFF_CQ, OFF_CKV, OFF_Z, OFF_XBC, OFF_DT = 0, 256, 512, 768, 1024, 1184, 1696, 2464
LORA = 160


def k_tiles(n, width=256):
    return lambda slot: slot[:, 0:n * width].rearrange("p (k n) -> p k n", n=width)


def rope_tables(c, a):
    c.rope_cos, c.rope_sin = c.carve(TT, 16), c.carve(TT, 16)
    pos_i, pos = c.carve(TT).bitcast(I32), c.carve(TT)
    loads = Loads(c.nc, "position_loads")
    freq, angle, turn = c.carve(16), c.carve(TT, 16), c.carve(TT, 16)
    for t in range(TT):
        loads.load(c.nc.scalar, pos_i[:, t:t + 1], a["positions"][0:1, t * P:(t + 1) * P].rearrange("a p -> p a"))
    m = c.copy(pos, pos_i, loads.last)
    for j in range(16):
        f = np.float32(1.0) / np.power(np.float32(10000.0), np.float32(2 * j) / np.float32(32))
        m = c.fill(freq[:, j:j + 1], float(f))
    for t in range(TT):
        m = c.ts(angle[:, t, :], freq, pos[:, t:t + 1], None, ALU.mult, None, m)
    c.sincos(c.rope_sin, c.rope_cos, angle, turn, m)


def rope(c, out, x, t, heads, stride_view, scratch, *marks):
    cos = c.rope_cos[:, t:t + 1, :].to_broadcast([P, heads, 16])
    sin = c.rope_sin[:, t:t + 1, :].to_broadcast([P, heads, 16])
    x1, x2 = x[:, :, 0:16], x[:, :, 16:32]
    m = c.tt(out[:, :, 0:16], x1, cos, ALU.mult, *marks)
    m = c.tt(scratch, x2, sin, ALU.mult)
    m = c.tt(out[:, :, 0:16], out[:, :, 0:16], scratch, ALU.subtract)
    m = c.tt(scratch, x1, sin, ALU.mult)
    m = c.tt(out[:, :, 16:32], x2, cos, ALU.mult)
    return c.tt(out[:, :, 16:32], out[:, :, 16:32], scratch, ALU.add)


def layer_pieces(a, l):
    w = {name: a[name][l].rearrange("(k p) n -> p k n", p=P) for name in ("w_ada", "w_in", "w_out", "w_up", "w_down")}
    col = lambda name, off: (k_tiles(KT), w[name][:, :, off:off + 256])
    pieces = {"ada": [(lambda s: s, w["w_ada"][:, k, g * SLOT:(g + 1) * SLOT]) for g in range(3) for k in range(KT)]}
    pieces["in"] = [col("w_in", off) for off in (OFF_Q, OFF_K, OFF_V, OFF_CQ)]
    pieces["in"].append((k_tiles(KT, LORA), w["w_in"][:, :, OFF_CKV:OFF_CKV + LORA]))
    pieces["in"] += [col("w_in", off + 256 * n) for off, count in ((OFF_Z, 2), (OFF_XBC, 3)) for n in range(count)]
    pieces["out"] = [col("w_out", n * 256) for n in range(4)]
    pieces["up"] = [col("w_up", n * 256) for n in range(FF // 256)]
    pieces["down"] = [(k_tiles(2, D), w["w_down"][:, 2 * n:2 * n + 2, :]) for n in range(FF // 256)]
    return pieces


ATTENTION_FLOATS = 10000

V_NORM0, V_NORM2, V_QN, V_KVN, V_CONV_W, V_CONV_B, V_COND, V_ADA = 0, 8, 16, 18, 19, 43, 49, 57
V_ROWS = V_ADA + 48


def modulation(c, a, l, s, pieces):
    nc = c.nc
    vec, norm, acc = c.carve(P), c.carve(D), [c.carve(SLOT) for _ in range(2)]
    loads, rows = Loads(nc, f"vector_loads{l}"), Loads(nc, f"row_loads{l}")
    q = nc.scalar
    for n0, n, src in ((V_NORM0, 8, a["norm_g"][l, 0:1, :]), (V_NORM2, 8, a["norm_g"][l, 2:3, :]),
                       (V_QN, 2, a["mla_q_norm_g"][l:l + 1]), (V_KVN, 1, a["mla_kv_norm_g"][l:l + 1]),
                       (V_CONV_W, 24, a["conv_w"][l]), (V_CONV_B, 6, a["conv_b"][l:l + 1]), (V_COND, 8, a["c"]),
                       (V_ADA, 48, a["b_ada"][l:l + 1])):
        loads.load(nc.sync, vec[n0:n0 + n, :], src.rearrange("a (r p) -> (a r) p", p=P))
    for dst, off in ((s.gate_m, 2 * D), (s.gate_f, 5 * D)):
        rows.load(q, dst, a["b_ada"][l:l + 1, off:off + D].to_broadcast([P, D]))
    rows.load(q, norm, a["norm_g"][l, 1:2, :].to_broadcast([P, D]))
    c.tensor.wait(loads.last, c.gpsimd.last)
    i, bank = c.bank()
    m = c.tensor.did(nc.tensor.transpose(bank[:, 0:V_ROWS], vec[0:V_ROWS, :], c.identity[0:V_ROWS, 0:V_ROWS]))
    m = c.copy(s.vec, bank[:, 0:V_ROWS], m, loads.last)
    c.read(i, m)
    cond = c.carve(8)
    mc = c.act(cond, s.vec[:, V_COND:V_COND + 8], ACT.Silu, m)
    for g in range(3):
        part = acc[g % 2]
        for k in range(KT):
            w = c.weights(c.vector, pieces[g * KT + k])
            if k == 0:
                m = c.ts(part, w, cond[:, 0:1], None, ALU.mult, None, mc, done if g == 2 else None)
            else:
                m = c.stt(part, w, cond[:, k:k + 1], part, ALU.mult, ALU.add)
            c.release(m)
            yield
        c.tensor.wait(m)
        i, bank = c.bank()
        for n in range(16):
            ins = c.mm(bank[:, n:n + 1], part[:, n * P:(n + 1) * P], c.ones[:, 0:1])
        done = c.tensor.did(ins)
        m = c.tt(s.mod[:, 16 * g:16 * g + 16], bank[:, 0:16], s.vec[:, V_ADA + 16 * g:V_ADA + 16 * g + 16], ALU.add, done)
        c.read(i, m)
        if g == 0:
            c.stt(s.in_scale_m, s.mod[:, 8:16], 1.0, s.vec[:, V_NORM0:V_NORM0 + 8], ALU.add, ALU.mult)
            continue
        if g == 2:
            c.stt(s.in_scale_f, s.mod[:, 32:40], 1.0, s.vec[:, V_NORM2:V_NORM2 + 8], ALU.add, ALU.mult)
        gate, off = ((s.gate_m, 0), (s.gate_f, D))[g - 1]
        for h in range(2):
            i, bank = c.bank()
            m = done = c.tensor.did(c.mm(bank, c.ones, part[:, off + h * 512:off + (h + 1) * 512]))
            half = gate[:, h * 512:(h + 1) * 512]
            m = c.tt(half, bank, half, ALU.add, m, rows.last)
            c.read(i, m)
            m = c.tt(half, half, norm[:, h * 512:(h + 1) * 512], ALU.mult)
        if g == 1:
            c.scalar.wait(m)
            rows.load(q, norm, a["norm_g"][l, 3:4, :].to_broadcast([P, D]))
        yield


def normed_rows(c, x, work, small):
    for t in range(TT):
        m = c.sumsq(small[:, t:t + 1], x[:, t, :], x[:, t, :], work[:, t, :])
    m = c.rsqrt(small[:, 0:TT], small[:, 0:TT], D, 1e-6, m)
    for t in range(TT):
        m = c.act(work[:, t, :], x[:, t, :], ACT.Copy, m, scale=small[:, t:t + 1])
    return m


def modulated_cols(c, hT, work, scale, shift, *marks):
    def evacuate(k, out, src, mark):
        if (k // 2) % 2:
            return c.act(out, src, ACT.Identity, mark, scale=scale[:, k:k + 1], bias=shift[:, k:k + 1])
        return c.ts(out, src, scale[:, k:k + 1], shift[:, k:k + 1], ALU.mult, ALU.add, mark)
    return c.columns_from_rows(hT, work, c.identity, KT, evacuate, *marks, c.vector.last)


def projections(c, s, loads, pieces):
    hT, pieces = s.hT, iter(pieces)

    def cols(dst, width=2):
        w = c.weights(c.tensor, next(pieces))
        i, src, m = c.product_cols(hT, w, range(KT), width)
        c.release(m)
        c.read(i, c.copy(dst, src, m, q=c.scalar))

    def rows(dst, width=256):
        w = c.weights(c.tensor, next(pieces))
        i, src, m = c.product_rows(hT, w, range(KT), width)
        c.release(m)
        c.read(i, c.copy(dst, src, m))

    cols(s.qT)
    yield
    cols(s.kT)
    yield
    for dst in (s.vq[:, :, 0:256], s.vq[:, :, 256:512]):
        rows(dst)
        yield
    rows(s.lora, LORA)
    yield
    for dst in (s.z[:, :, 0:256], s.z[:, :, 256:512]):
        rows(dst)
        yield
    for j in range(3):
        cols(s.xbc[:, 2 * j:2 * j + 2, 3:3 + SEQ])
        yield
    c.tensor.wait(loads.last)
    i, bank = c.bank()
    for t in range(TT):
        for k in range(KT):
            ins = c.mm(bank[:, t * 8:t * 8 + 8], hT[:, k, t * P:(t + 1) * P], s.w_dt[:, k, :], k == 0, k == KT - 1)
    m = c.tensor.did(ins)
    c.read(i, c.copy(s.dt, bank[:, 0:16].rearrange("p (t h) -> p t h", t=TT), m))


def diff_attention(c, s, loads, y):
    nc, lam = c.nc, s.lam
    for j in range(2):
        m = c.sumsq(lam[:, j:j + 1], s.lp[:, 2 * j, :], s.lp[:, 2 * j + 1, :], s.lp_work, loads.last)
    m = c.act(lam[:, 2:4], lam[:, 0:2], ACT.Exp, m)
    m = c.stt(lam[:, 4:5], lam[:, 2:3], s.lambda_init, lam[:, 3:4], ALU.add, ALU.subtract, m)
    m = c.ts(lam[:, 4:5], lam[:, 4:5], -1.0, None, ALU.mult, None)
    scores, total, negmax = c.carve(8, SEQ), c.carve(8), c.carve(8)
    pT, work = c.carve(4, 2, SEQ), c.carve(256)
    pv_done = None
    for t in range(TT):
        keys = P * (t + 1)
        c.tensor.wait(c.scalar.last)
        for r in range(4):
            i, bank = c.bank()
            for e in range(2):
                ins = c.mm(bank[:, e * SEQ:e * SEQ + keys], s.qT[32 * r:32 * r + 32, e, t * P:(t + 1) * P],
                           s.kT[32 * r:32 * r + 32, e, 0:keys])
            m = c.tensor.did(ins)
            src = bank[:, :].rearrange("p (e k) -> p e k", e=2)[:, :, 0:keys]
            mask = c.chunk_mask[:, t:t + 1, 0:keys].to_broadcast([P, 2, keys])
            both = scores[:, :, :].rearrange("p (e r) k -> p e r k", e=2)[:, :, r, 0:keys]
            m = c.stt(both, src, 32 ** -0.5, mask, ALU.mult, ALU.add, m, pv_done)
            c.read(i, m)
            if r % 2:
                yield
        m = c.softmax_exp(scores, negmax, total, 8, keys, m)
        yield
        pair = total[:, :].rearrange("p (h e) -> p h e", e=2)
        m = c.ts(pair[:, :, 1], pair[:, :, 1], lam[:, 4:5], None, ALU.mult, None)
        sc = scores[:, :, 0:keys]
        m = c.tt(sc, sc, total[:, 0:8].unsqueeze(2).to_broadcast([P, 8, keys]), ALU.mult)
        two = scores[:, :, :].rearrange("p (h e) k -> p h e k", e=2)
        m = c.tt(two[:, :, 0, 0:keys], two[:, :, 0, 0:keys], two[:, :, 1, 0:keys], ALU.add)
        yield
        done = c.transpose_maps(pT, two[:, :, 0, :], 4, t, c.identity, m)
        pv_done = c.tensor.last
        yield
        c.tensor.wait(*done, c.vector.last)
        i, bank = c.bank()
        for h in range(4):
            for kt in range(t + 1):
                ins = c.mm(bank[:, h * 64:(h + 1) * 64], pT[:, h, kt, t * P:(t + 1) * P],
                           s.vq[:, kt, h * 64:(h + 1) * 64], kt == 0, kt == t)
        m = c.tensor.did(ins)
        yt = y[:, t, 0:256]
        m = c.copy(yt, bank[:, 0:256], m)
        c.read(i, m)
        m = c.tt(work, yt, yt, ALU.mult, m)
        m = c.reduce(total[:, 0:4], work[:, :].rearrange("p (h e) -> p h e", h=4), ALU.add, m)
        yield
        m = c.rsqrt(total[:, 0:4], total[:, 0:4], 64, 1e-5, m)
        yh = yt.rearrange("p (h e) -> p h e", h=4)
        m = c.tt(yh, yh, total[:, 0:4].unsqueeze(2).to_broadcast([P, 4, 64]), ALU.mult, m)
        m = c.tt(yh, yh, s.subln.unsqueeze(1).to_broadcast([P, 4, 64]), ALU.mult, m)
        m = c.ts(yt, yt, 1.0 - s.lambda_init, None, ALU.mult, None)
        yield


def latent_attention(c, s, yT):
    cq, lora = s.vq, s.lora
    small, work = c.carve(8), c.carve(TT, 384)
    for t in range(TT):
        m = c.sumsq(small[:, t:t + 1], cq[:, t, 256:512], cq[:, t, 256:512], work[:, t, 0:256])
        m = c.sumsq(small[:, 2 + t:3 + t], lora[:, t, 0:128], lora[:, t, 0:128], work[:, t, 0:128])
    c.rsqrt(small[:, 0:2], small[:, 0:2], 256, 1e-6)
    m = c.rsqrt(small[:, 2:4], small[:, 2:4], 128, 1e-6)
    latT = c.carve(3, SEQ)
    for t in range(TT):
        c.ts(work[:, t, 0:256], cq[:, t, 256:512], small[:, t:t + 1], None, ALU.mult, None)
        m = c.ts(work[:, t, 256:384], lora[:, t, 0:128], small[:, 2 + t:3 + t], None, ALU.mult, None)
    yield
    done = c.columns_from_rows(latT, work, c.identity, 3,
                               lambda k, out, src, mark: c.ts(out, src, s.vec[:, V_QN + k:V_QN + k + 1], None,
                                                              ALU.mult, None, mark), m)
    q_rows, k_rows, v_rows = c.carve(TT, 4, 96), c.carve(TT, 4, 96), c.carve(TT, 256)
    qraw, kvraw, half = c.carve(384), c.carve(512), c.carve(4, 16)
    c.tensor.wait(*done)
    for t in range(TT):
        i, bank = c.bank()
        for k in range(2):
            ins = c.mm(bank[:, 0:384], latT[:, k, t * P:(t + 1) * P], s.w_uq[:, k, :], k == 0, k == 1)
        m = c.tensor.did(ins)
        m = c.copy(qraw, bank[:, 0:384], m)
        c.read(i, m)
        qh = qraw[:, :].rearrange("p (h e) -> p h e", h=4)
        c.copy(q_rows[:, t, :, 0:64], qh[:, :, 0:64])
        rope(c, q_rows[:, t, :, 64:96], qh[:, :, 64:96], t, 4, None, half)
        i, bank = c.bank()
        m = c.tensor.did(c.mm(bank, latT[:, 2, t * P:(t + 1) * P], s.w_ukv))
        m = c.copy(kvraw, bank, m)
        c.read(i, m)
        kh = kvraw[:, :].rearrange("p (h e) -> p h e", h=4)
        c.copy(k_rows[:, t, :, 0:64], kh[:, :, 0:64])
        c.copy(v_rows[:, t, :].rearrange("p (h e) -> p h e", h=4), kh[:, :, 64:128])
        kr = lora[:, t:t + 1, 128:160]
        rope(c, k_rows[:, t, 0:1, 64:96], kr, t, 1, None, half[:, 0:1, :])
        m = c.copy(k_rows[:, t, 1:4, 64:96], k_rows[:, t, 0:1, 64:96].to_broadcast([P, 3, 32]))
        yield
    qT, kT = c.carve(4, SEQ), c.carve(4, SEQ)
    c.tensor.wait(m)
    done = []
    for src, dst in ((q_rows, qT), (k_rows, kT)):
        for h in range(0, 4, 2):
            i, bank = c.bank()
            for e in range(2):
                for t in range(TT):
                    n = (e * TT + t) * P
                    ins = c.nc.tensor.transpose(bank[0:96, n:n + P], src[:, t, h + e, :], c.identity)
            m = c.tensor.did(ins)
            d = c.copy(dst[0:96, h:h + 2, :], bank[0:96, :].rearrange("p (h s) -> p h s", h=2), m, q=c.scalar)
            c.read(i, d)
            done.append(d)
        yield
    scores, total, negmax = c.carve(4, SEQ), c.carve(4), c.carve(4)
    pT = c.carve(4, 2, SEQ)
    c.tensor.wait(*done)
    pv_done = None
    for t in range(TT):
        keys = P * (t + 1)
        for h in range(0, 4, 2):
            i, bank = c.bank()
            for e in range(2):
                ins = c.mm(bank[:, e * SEQ:e * SEQ + keys], qT[0:96, h + e, t * P:(t + 1) * P], kT[0:96, h + e, 0:keys])
            m = c.tensor.did(ins)
            src = bank[:, :].rearrange("p (e k) -> p e k", e=2)[:, :, 0:keys]
            mask = c.chunk_mask[:, t:t + 1, 0:keys].to_broadcast([P, 2, keys])
            m = c.stt(scores[:, h:h + 2, 0:keys], src, 96 ** -0.5, mask, ALU.mult, ALU.add, m, pv_done)
            c.read(i, m)
        yield
        m = c.softmax_exp(scores, negmax, total, 4, keys, m)
        yield
        sc = scores[:, :, 0:keys]
        m = c.tt(sc, sc, total[:, 0:4].unsqueeze(2).to_broadcast([P, 4, keys]), ALU.mult, m)
        done = c.transpose_maps(pT, scores, 4, t, c.identity, m)
        pv_done = c.tensor.last
        yield
        c.tensor.wait(*done)
    c.tensor.wait(*heads_out(c, yT, 2, pT, v_rows, 4))


def heads_out(c, yT, tile0, pT, v_rows, heads):
    done = []
    for h0 in range(0, heads, 4):
        i, bank = c.bank()
        for h in range(h0, h0 + 4):
            r, col = 64 * (h % 2), ((h - h0) // 2) * SEQ
            for t in range(TT):
                for kt in range(t + 1):
                    ins = c.mm(bank[r:r + 64, col + t * P:col + (t + 1) * P], v_rows[:, kt, h * 64:(h + 1) * 64],
                               pT[:, h, kt, t * P:(t + 1) * P], kt == 0, kt == t)
        m = c.tensor.did(ins)
        d = c.copy(yT[:, tile0 + h0 // 2:tile0 + h0 // 2 + 2, :], bank[:, :].rearrange("p (k s) -> p k s", k=2), m)
        c.read(i, d)
        done.append(d)
    return done


def log1p_positive(c, out, e, z, zz, *marks):
    m = c.ts(z, e, 2.0, None, ALU.add, None, *marks)
    m = c.recip(z, z)
    m = c.tt(z, z, e, ALU.mult)
    m = c.tt(zz, z, z, ALU.mult)
    m = c.ts(out, zz, 1.0 / 15, 1.0 / 13, ALU.mult, ALU.add)
    for n in (11, 9, 7, 5, 3, 1):
        m = c.tt(out, out, zz, ALU.mult)
        m = c.ts(out, out, 1.0 / n, None, ALU.add, None)
    m = c.tt(out, out, z, ALU.mult)
    return c.ts(out, out, 2.0, None, ALU.mult, None)


def state_space(c, s, loads, y):
    conv = c.carve(6, SEQ)
    for r in range(6):
        w = lambda j: s.vec[:, V_CONV_W + 6 * j + r:V_CONV_W + 6 * j + r + 1]
        m = c.ts(conv[:, r, :], s.xbc[:, r, 0:SEQ], w(0), None, ALU.mult, None, c.scalar.last, c.gpsimd.last)
        for j in range(1, 4):
            m = c.stt(conv[:, r, :], s.xbc[:, r, j:j + SEQ], w(j), conv[:, r, :], ALU.mult, ALU.add)
        ms = c.act(conv[:, r, :], conv[:, r, :], ACT.Silu, m, bias=s.vec[:, V_CONV_B + r:V_CONV_B + r + 1])
        if r % 2:
            yield
    xs = c.carve(TT, 512)
    dt, da, e, z, zz, n = (c.carve(TT, 8) for _ in range(6))
    bias = s.dt_bias.unsqueeze(1).to_broadcast([P, TT, 8])
    m = c.tt(dt, s.dt, bias, ALU.add, loads.last)
    m = c.ts(n, dt, -1.0, None, ALU.mult, None)
    m = c.tt(n, dt, n, ALU.min)
    m = c.act(e, n, ACT.Exp, m)
    m = log1p_positive(c, da, e, z, zz, m)
    m = c.stt(dt, dt, 0.0, da, ALU.max, ALU.add)
    yield
    neg_a = c.carve(8)
    ma = c.act(neg_a, s.a_log, ACT.Exp, loads.last)
    m = c.stt(da, dt, -1.0, neg_a.unsqueeze(1).to_broadcast([P, TT, 8]), ALU.mult, ALU.mult, ma)
    wide = c.carve(TT, 8, P)
    m = c.copy(wide, da.unsqueeze(3).to_broadcast([P, TT, 8, P]), m)
    c.tensor.wait(m, c.gpsimd.last)
    i, bank = c.bank()
    for t in range(TT):
        for u in range(t + 1):
            ins = c.mm(bank[:, t * 8:t * 8 + 8], c.causal[:, u, t * P:(t + 1) * P], da[:, u, :], u == 0, u == t)
    m = c.tensor.did(ins)
    sum_col = c.carve(TT, 8)
    m = c.copy(sum_col, bank[:, 0:16].rearrange("p (t h) -> p t h", t=TT), m)
    c.read(i, m)
    yield
    bc = c.carve(TT * 2, SEQ)
    c.tensor.wait(ms)
    for g in range(2):
        i, bank = c.bank()
        for t in range(TT):
            ins = c.mm(bank[:, t * SEQ:(t + 1) * SEQ], conv[64 * g:64 * g + 64, 4, t * P:(t + 1) * P],
                       conv[64 * g:64 * g + 64, 5, :])
        m = c.tensor.did(ins)
        m = c.tt(bc[:, :, :].rearrange("p (t g) s -> p t g s", g=2)[:, :, g, :],
                 bank[:, :].rearrange("p (t s) -> p t s", t=TT), c.causal, ALU.mult, m)
        c.read(i, m)
    yield
    for t in range(TT):
        i, bank = c.bank()
        for k in range(4):
            ins = c.nc.tensor.transpose(bank[:, k * P:(k + 1) * P], conv[:, k, t * P:(t + 1) * P], c.identity)
        m = c.tensor.did(ins)
        c.read(i, c.copy(xs[:, t, :], bank, m, q=c.scalar))
    xd = c.carve(TT, 512)
    for t in range(TT):
        m = c.tt(xd[:, t, :].rearrange("p (h e) -> p h e", h=8), xs[:, t, :].rearrange("p (h e) -> p h e", h=8),
                 dt[:, t, :].unsqueeze(2).to_broadcast([P, 8, 64]), ALU.mult, c.scalar.last)
    yield
    mix = [c.carve(TT, SEQ) for _ in range(2)]
    outs = [c.bank() for _ in range(TT)]
    c.held.update(i for i, _ in outs)
    mixed = [None] * 2

    def apply(h):
        c.tensor.wait(mixed[h % 2])
        for t in range(TT):
            for u in range(t + 1):
                ins = c.mm(outs[t][1][:, h * 64:(h + 1) * 64], mix[h % 2][:, u, t * P:(t + 1) * P],
                           xd[:, u, h * 64:(h + 1) * 64], u == 0, u == t)
        return c.tensor.did(ins)
    applied = [None] * 2
    for h in range(8):
        i, bank = c.bank()
        for u in range(TT):
            ins = c.mm(bank[:, 0:SEQ], wide[:, u, h, :], c.causal[:, u, :], u == 0, u == 1)
        m = c.tensor.did(ins)
        part = mix[h % 2]
        for t in range(TT):
            m1 = c.ts(part[:, t, :], bank[:, 0:SEQ], sum_col[:, t, h:h + 1], 0.0, ALU.subtract, ALU.min, m, applied[h % 2])
        c.read(i, m1)
        m = c.act(part, part, ACT.Exp, m1)
        if h:
            applied[(h - 1) % 2] = apply(h - 1)
        mixed[h % 2] = c.tt(part, part, bc[:, :, :].rearrange("p (t g) s -> p t g s", g=2)[:, :, h // 4, :], ALU.mult, m)
        yield
    m_all = apply(7)
    work = c.carve(512)
    small = c.carve(2)
    for t in range(TT):
        (i, bank), m = outs[t], m_all
        out = y[:, t, 512:1024]
        m0 = c.tt(work[:, :].rearrange("p (h e) -> p h e", h=8), xs[:, t, :].rearrange("p (h e) -> p h e", h=8),
                  s.d_skip.unsqueeze(2).to_broadcast([P, 8, 64]), ALU.mult)
        m = c.tt(out, bank, work, ALU.add, m)
        c.read(i, m)
        c.held.discard(i)
        yield
        mz = c.act(s.z[:, t, :], s.z[:, t, :], ACT.Silu, m0)
        m = c.tt(out, out, s.z[:, t, :], ALU.mult, mz)
        m = c.tt(work, out, out, ALU.mult)
        m = c.reduce(small, work[:, :].rearrange("p (g e) -> p g e", g=2), ALU.add)
        m = c.rsqrt(small, small, 256, 1e-6, m)
        og = out.rearrange("p (g e) -> p g e", g=2)
        m = c.tt(og, og, small.unsqueeze(2).to_broadcast([P, 2, 256]), ALU.mult, m)
        m = c.tt(out, out, s.ssm_norm, ALU.mult)
        yield


def add_gated(c, x, y, gate, small, junk, *marks):
    for t in range(TT):
        m = c.sumsq(small[:, t:t + 1], y[:, t, :], y[:, t, :], junk, *marks)
    m = c.rsqrt(small[:, 0:TT], small[:, 0:TT], D, 1e-6, m)
    for t in range(TT):
        m = c.stt(y[:, t, :], y[:, t, :], small[:, t:t + 1], gate, ALU.mult, ALU.mult, m)
        m = c.tt(x[:, t, :], x[:, t, :], y[:, t, :], ALU.add)
    return m


class State:
    pass


def mixer_loads(c, a, l, s):
    loads = Loads(c.nc, f"mixer_loads{l}")
    load = lambda dst, src: loads.load(c.nc.scalar, dst, src)
    s.w_dt, s.w_uq, s.w_ukv = c.carve(KT, 8), c.carve(2, 384), c.carve(512)
    s.lp, s.lp_work, s.subln = c.carve(4, 32), c.carve(32), c.carve(64)
    load(s.w_dt, a["w_in"][l, :, OFF_DT:OFF_DT + 8].rearrange("(k p) n -> p k n", p=P))
    load(s.w_uq, a["w_uq"][l].rearrange("(k p) n -> p k n", p=P))
    load(s.w_ukv, a["w_ukv"][l])
    load(s.lp, a["diff_lambda"][l:l + 1].to_broadcast([P, 4, 32]))
    load(s.subln, a["diff_subln_g"][l:l + 1].to_broadcast([P, 64]))
    s.d_skip, s.dt_bias, s.a_log, s.ssm_norm = c.carve(8), c.carve(8), c.carve(8), c.carve(512)
    for dst, name in ((s.d_skip, "d_skip"), (s.dt_bias, "dt_bias"), (s.a_log, "a_log"), (s.ssm_norm, "ssm_norm_g")):
        load(dst, a[name][l:l + 1].to_broadcast([P, dst.shape[1]]))
    return loads


def mixer(c, a, l, s, x, pieces, ada, spare, normed):
    work, small, junk = c.carve(TT, D), c.carve(4), c.carve(D)
    loads = mixer_loads(c, a, l, s)
    s.lam = c.carve(5)
    s.qT, s.kT = c.carve(2, SEQ), c.carve(2, SEQ)
    s.vq, s.lora, s.z = c.carve(TT, 512), c.carve(TT, LORA), c.carve(TT, 512)
    s.xbc, s.dt = c.carve(6, 3 + SEQ), c.carve(TT, 8)
    c.fill(s.xbc[:, :, 0:3], 0.0, q=c.gpsimd)
    m = normed_rows(c, x, work, small) if normed is None else normed
    done = modulated_cols(c, s.hT, work, s.in_scale_m, s.mod[:, 0:8], m)
    c.tensor.wait(*done)
    here = c.mem
    c.weave((projections(c, s, loads, pieces["in"]), here), *ada)
    c.meet()
    y, yT = work, s.hT
    latent_mem, ssm_mem = here.rest(ATTENTION_FLOATS), here.rest()

    def diff():
        yield from diff_attention(c, s, loads, y)
        c.tensor.wait(c.vector.last)
        c.columns_from_rows(yT[:, 0:2, :], y[:, :, 0:256], c.identity, 2, None)

    c.weave((state_space(c, s, loads, y), ssm_mem), (diff(), spare), (latent_attention(c, s, yT), latent_mem))
    c.tensor.wait(c.vector.last)
    done = c.columns_from_rows(yT[:, 4:8, :], y[:, :, 512:1024], c.identity, 4, None)
    c.tensor.wait(*done, c.scalar.last, c.vector.last)
    c.vector.wait(c.tensor.last)
    c.scalar.wait(c.tensor.last)
    for _ in out_rows(c, s.hT, y, pieces["out"]):
        pass
    add_gated(c, x, y, s.gate_m, small, junk)


def mlp(c, l, s, x, pieces, ada):
    work, small, junk = c.carve(TT, D), c.carve(4), c.carve(D)
    m = normed_rows(c, x, work, small)
    done = modulated_cols(c, s.hT, work, s.in_scale_f, s.mod[:, 24:32], m)
    h_pair = c.carve_split(f"mlp_in{l}", KT, SEQ)
    hidden = [c.carve_split(f"hidden{l}_{n}", 2, SEQ) for n in range(2)]
    raw = c.carve(2, SEQ)
    order = [pieces["up"][0]]
    for n, down in enumerate(pieces["down"]):
        order += pieces["up"][n + 1:n + 2] + [down]
    c.scalar.wait(*done)
    c.vector.wait(*done)
    m = c.split(h_pair, s.hT)
    stream = SplitWeights(c, f"mlp_weights{l}_", order)
    c.tensor.wait(m)
    here = c.mem
    ready, read = [None] * 2, [None] * 2

    def up(n):
        i, src, m = c.split_cols(h_pair, stream.take())
        stream.release(m)
        m = c.act(raw, src, ACT.Relu, m, c.vector.last)
        c.read(i, m)
        m = c.act(raw, raw, ACT.Square, m)
        ready[n % 2] = c.split(hidden[n % 2], raw, m, read[n % 2])

    def steps():
        outs = [c.bank() for _ in range(4)]
        c.held.update(i for i, _ in outs)
        up(0)
        yield
        last = len(pieces["down"]) - 1
        for n in range(last + 1):
            if n < last:
                up(n + 1)
                yield
            w = stream.take()
            c.tensor.wait(ready[n % 2])
            for t in range(TT):
                for half in range(2):
                    for k in range(2):
                        ins = c.mm_split(outs[2 * t + half][1], [v[:, k, t * P:(t + 1) * P] for v in hidden[n % 2]],
                                         [v[:, k, half * 512:(half + 1) * 512] for v in w],
                                         n == 0 and k == 0, n == last and k == 1)
            m = read[n % 2] = c.tensor.did(ins)
            stream.release(m)
            yield
        for n, (i, bank) in enumerate(outs):
            t, half = n // 2, n % 2
            c.read(i, c.copy(work[:, t, half * 512:(half + 1) * 512], bank, m, q=(c.vector, c.scalar)[half]))
            c.held.discard(i)
        c.vector.wait(c.scalar.last)

    c.weave((steps(), here), *ada)
    add_gated(c, x, work, s.gate_f, small, junk)


def first_block(c, a, x):
    first_constants(c)
    rope_tables(c, a)
    layers = []
    for l in range(DEPTH):
        s = State()
        s.hT, s.lambda_init = c.hT, 0.8 - 0.6 * math.exp(-0.3 * l)
        s.vec, s.mod = c.carve(V_ROWS), c.carve(48)
        s.in_scale_m, s.in_scale_f, s.gate_m, s.gate_f = c.carve(8), c.carve(8), c.carve(D), c.carve(D)
        layers.append(s)
    ada_floats = P + D + 2 * SLOT + 8
    ada_mem = c.mem.rest(ada_floats)
    free = c.mem
    c.mem = free.rest()
    normed = normed_rows(c, x, c.carve(TT, D), c.carve(4))
    steps = modulation(c, a, 0, layers[0], layer_pieces(a, 0)["ada"])
    c.mem = ada_mem
    for _ in range(KT + 1):
        next(steps)
    left = [(steps, ada_mem)]
    for l, s in enumerate(layers):
        ada_again = Region(c.arena, ada_mem.end - ada_floats, ada_mem.end)
        pieces = layer_pieces(a, l)
        c.mem = free.rest()
        mixer(c, a, l, s, x, pieces, left, Region(c.arena, ada_again.at, ada_again.end), normed)
        normed = None
        c.meet()
        left, beside = [], []
        if l + 1 < DEPTH:
            steps = modulation(c, a, l + 1, layers[l + 1], layer_pieces(a, l + 1)["ada"])
            left = [(steps, ada_again)]
            beside = [(every_other(steps, 2 * (KT + 1)), ada_again)]
        c.mem = free.rest()
        mlp(c, l, s, x, pieces, beside)
        c.meet()


def every_other(steps, count):
    for _ in range(count):
        next(steps)
        yield
        yield


def out_rows(c, inT, out, pieces):
    each = len(pieces) // 4
    for n in range(4):
        (i0, bank0), (i1, bank1) = c.bank(), c.bank()
        for p in range(each):
            w = c.weights(c.tensor, pieces[n * each + p])
            for t, bank in enumerate((bank0, bank1)):
                for k in range(KT):
                    ins = c.mm(bank[:, 0:256], inT[:, p * KT + k, t * P:(t + 1) * P], w[:, k, :],
                               p == 0 and k == 0, p == each - 1 and k == KT - 1)
            m = c.tensor.did(ins)
            c.release(m)
            if each > 1:
                c.held.update((i0, i1))
                yield
                c.held.difference_update((i0, i1))
        c.read(i0, c.copy(out[:, 0, n * 256:(n + 1) * 256], bank0[:, 0:256], m))
        c.read(i1, c.copy(out[:, 1, n * 256:(n + 1) * 256], bank1[:, 0:256], m, q=c.scalar))
    c.vector.wait(c.scalar.last)


C = 32
N_CHUNK = SEQ // C
OFF_MOBA, OFF_SSM, OFF_GATE = 1792, 3328, 3840
HEADS = 8
ALPHA = 2.0 ** 0.25
SSM_MOBA_FLOATS = 9400
VECTORS_2 = [("rwkv_mu_2", 14), ("rwkv_w0_2", 4), ("rwkv_a0_2", 4), ("rwkv_k_k_2", 4), ("rwkv_k_a_2", 4),
             ("rwkv_r_k_2", 4), ("rwkv_ln_w_2", 4), ("rwkv_ln_b_2", 4), ("ssm_d_2", 4), ("ssm_glu_b_2", 8),
             ("gate_b_2", 24), ("ssm_a_re_2", 16), ("ssm_a_im_2", 16), ("ssm_log_dt_2", 16)]


def second_pieces(a):
    w_in = a["w_in_2"].rearrange("a (k p) n -> p (a k) n", p=P)
    col = lambda off: (k_tiles(KT), w_in[:, :, off:off + 256])
    half = lambda w, n: (k_tiles(4, 512), a[w].rearrange("a (k p) n -> p (a k) n", p=P)[:, :, n * 512:(n + 1) * 512])
    gate = lambda branch: [col(OFF_GATE + D * branch + 256 * n) for n in range(4)]
    up = lambda name: [half(name, n) for n in range(2)]
    pieces = {"rwkv": [col(256 * n) for n in range(7)], "moba": [col(OFF_MOBA + 256 * n) for n in range(6)],
              "ssm": [col(OFF_SSM + 256 * n) for n in range(2)], "gate": [gate(branch) for branch in range(3)],
              "up": [up("w_up_rwkv_2"), up("w_up_moba_2"), up("w_up_ssm_2")], "glu": up("ssm_glu_w_2")}
    w_out = a["w_out_2"].rearrange("a (k p) n -> p (a k) n", p=P)
    pieces["out"] = [(k_tiles(KT), w_out[:, :, n * 256:(n + 1) * 256]) for n in range(4)]
    return pieces


def second_constants(c, s):
    g = c.gpsimd

    def select(out, cmp, fill, base, pattern, channel):
        return g.did(g.after().affine_select(out=out, in_=out, compare_op=cmp, fill=fill, base=base,
                                             pattern=pattern, channel_multiplier=channel))
    s.distance = c.carve(TT, SEQ)
    for t in range(TT):
        g.did(g.after().iota(s.distance[:, t, :], pattern=[[-1, SEQ]], base=t * P, channel_multiplier=1,
                             allow_small_or_imprecise_dtypes=True))
        select(s.distance[:, t, :], ALU.is_ge, 1e34, t * P, [[-1, SEQ]], 1)
    s.pair = c.carve(5, P)
    c.fill(s.pair, 1.0, q=g)
    for kind, block in ((0, C), (1, C), (2, C), (3, 16), (4, 16)):
        for b in range(P // block):
            part = s.pair[:, kind, b * block:(b + 1) * block]
            if kind in (0, 3):
                select(part, ALU.is_gt, 0.0, b * block, [[1, block]], -1)
                select(part, ALU.is_ge, 0.0, -b * block, [[0, block]], 1)
            elif kind == 1:
                select(part, ALU.is_ge, 0.0, b * block, [[1, block]], -1)
                select(part, ALU.is_ge, 0.0, -b * block, [[0, block]], 1)
            else:
                select(part, ALU.is_gt, 0.0, -b * block, [[-1, block]], 1)
                select(part, ALU.is_ge, 0.0, (b + 1) * block - 1, [[0, block]], -1)
    s.chunk_start = c.carve(4 * SEQ)
    c.fill(s.chunk_start, 1.0, q=g)
    c.fill(s.chunk_start[:, :].rearrange("p (n c) -> p n c", c=C)[:, :, 0:1], 0.0, q=g)
    s.time = c.carve(SEQ)
    g.did(g.after().iota(s.time, pattern=[[1, SEQ]], base=0, channel_multiplier=0,
                         allow_small_or_imprecise_dtypes=True))
    number, s.group_odd = c.carve(1).bitcast(I32), c.carve(2)
    m = g.did(g.after().iota(number, pattern=[[0, 1]], base=0, channel_multiplier=1))
    m = c.ts(number, number, 4, 1, ALU.arith_shift_right, ALU.bitwise_and, m)
    m = c.copy(s.group_odd[:, 1:2], number, m)
    c.ts(s.group_odd[:, 0:1], s.group_odd[:, 1:2], -1.0, 1.0, ALU.mult, ALU.add)


def vectors_2(c, a, s):
    s.columns, s.log_dt, s.v = c.carve(P), c.carve(16), {}
    rows, each = c.carve(P), c.carve(16, 2)
    loads = Loads(c.nc, "vector_loads_2")
    loads.load(c.nc.scalar, each, a["ssm_log_dt_2"].rearrange("a (i e) -> a i e", e=2).to_broadcast([P, 16, 2]))
    n0 = 0
    for name, n in VECTORS_2:
        if name == "ssm_log_dt_2":
            continue
        flat = a[name]
        if name == "rwkv_r_k_2":
            flat = flat.rearrange("a h e -> a (h e)")
        elif name in ("ssm_a_re_2", "ssm_a_im_2"):
            flat = flat.rearrange("a g e -> a (g e)")
        flat = flat.rearrange("a (r p) -> (a r) p", p=P)
        loads.load(c.nc.scalar, rows[n0:n0 + n, :], flat)
        s.v[name] = s.columns[:, n0:n0 + n]
        n0 += n
    c.tensor.wait(loads.last)
    i, bank = c.bank()
    m = c.tensor.did(c.nc.tensor.transpose(bank[:, 0:n0], rows[0:n0, :], c.identity[0:n0, 0:n0]))
    c.read(i, c.copy(s.columns[:, 0:n0], bank[:, 0:n0], m))
    for e in range(2):
        c.copy(s.log_dt[64 * e:64 * e + 64, :], each[64 * e:64 * e + 64, :, e], loads.last)


def rwkv_input(c, a, s, project, pieces):
    col = lambda name, k: s.v[name][:, k:k + 1]
    s.rwkv_gate, s.bonus = c.carve(4, SEQ), c.carve(4, SEQ)
    s.AR = c.carve(4, TT, 2 * P)
    s.b, s.k, s.bend, s.kend, s.chunk_decay = (c.carve(4, SEQ), c.carve(4, SEQ), c.carve(4, SEQ), c.carve(4, SEQ),
                                               c.carve(4, N_CHUNK))
    s.v_cols = c.carve(4, SEQ)
    s.rwkv_end = c.mem.at
    s.lora_w, s.g2 = c.carve(512), c.carve(512)
    z = c.carve(14, SEQ + 1)
    loads = Loads(c.nc, "rwkv_loads")
    loads.load(c.nc.scalar, s.lora_w[0:64, :], a["rwkv_w2_2"][0, :, :])
    loads.load(c.nc.scalar, s.lora_w[64:P, :], a["rwkv_a2_2"][0, :, :])
    loads.load(c.nc.scalar, s.g2, a["rwkv_g2_2"][0, :, :])
    c.fill(z[:, :, 0:1], 0.0, q=c.gpsimd)
    for n in range(7):
        project(z[:, 2 * n:2 * n + 2, 1:SEQ + 1], pieces[n])
        yield
    r, k_, low, gate_in, tmp = c.carve(4, SEQ), c.carve(4, SEQ), c.carve(SEQ), c.carve(SEQ), c.carve(SEQ)
    v = s.v_cols
    shifted = [part[:, n, :] for part in (r, k_, v) for n in range(4)] + [low, gate_in]
    for k in range(14):
        m = c.tt(tmp, z[:, k, 0:SEQ], z[:, k, 1:SEQ + 1], ALU.subtract, c.scalar.last, c.gpsimd.last)
        m = c.stt(shifted[k], tmp, col("rwkv_mu_2", k), z[:, k, 1:SEQ + 1], ALU.mult, ALU.add)
        if k % 4 == 3:
            yield
    m = c.act(low[0:64, :], low[0:64, :], ACT.Tanh, m)
    m = c.act(gate_in, gate_in, ACT.Sigmoid, m)
    c.tensor.wait(m, c.vector.last, loads.last)
    logw, icl = c.carve(4, SEQ), c.carve(4, SEQ)
    for k in range(4):
        for out, r0, bias in ((logw, 0, "rwkv_w0_2"), (icl, 64, "rwkv_a0_2")):
            i, bank = c.bank()
            m = c.tensor.did(c.mm(bank[:, 0:SEQ], s.lora_w[r0:r0 + 64, k * P:(k + 1) * P], low[r0:r0 + 64, :]))
            c.read(i, c.act(out[:, k, :], bank[:, 0:SEQ], ACT.Sigmoid, m, bias=col(bias, k)))
        i, bank = c.bank()
        m = c.tensor.did(c.mm(bank[:, 0:SEQ], s.g2[:, k * P:(k + 1) * P], gate_in))
        c.read(i, c.copy(s.rwkv_gate[:, k, :], bank[:, 0:SEQ], m, q=c.scalar))
        yield
    c.ts(logw, logw, -math.exp(-0.5), None, ALU.mult, None, c.scalar.last)
    kk, work, ka = c.carve(4, SEQ), c.carve(4, SEQ), c.carve(4, SEQ)
    for k in range(4):
        m = c.ts(kk[:, k, :], k_[:, k, :], col("rwkv_k_k_2", k), None, ALU.mult, None)
    m = c.tt(work, kk, kk, ALU.mult)
    c.tensor.wait(m)
    for k in range(0, 4, 2):
        i, bank = c.bank()
        m = c.tensor.did(c.mm(bank, c.head_sum, work[:, k:k + 2, :].rearrange("p k s -> p (k s)")))
        m = c.ts(ka[:, k:k + 2, :], bank[:, :].rearrange("p (k s) -> p k s", k=2), 1e-24, None, ALU.max, None, m)
        c.read(i, m)
    yield
    m = c.act(ka, ka, ACT.Sqrt, m)
    m = c.recip(ka, ka, m)
    yield
    m = c.tt(kk, kk, ka, ALU.mult)
    for k in range(4):
        m = c.ts(ka[:, k, :], icl[:, k, :], -1.0, col("rwkv_k_a_2", k), ALU.add, ALU.mult)
    m = c.stt(k_, ka, 1.0, k_, ALU.add, ALU.mult)
    for k in range(4):
        m = c.stt(work[:, k, :], r[:, k, :], col("rwkv_r_k_2", k), k_[:, k, :], ALU.mult, ALU.mult, c.tensor.last)
    c.tensor.wait(m)
    for k in range(0, 4, 2):
        i, bank = c.bank()
        m = c.tensor.did(c.mm(bank, c.head_sum, work[:, k:k + 2, :].rearrange("p k s -> p (k s)")))
        m = c.tt(s.bonus[:, k:k + 2, :], bank[:, :].rearrange("p (k s) -> p k s", k=2), v[:, k:k + 2, :], ALU.mult, m)
        c.read(i, m)
    yield
    run = c.carve(4, SEQ)
    flat = lambda t: t.rearrange("p k s -> p (k s)")
    v1 = c.vector
    m = v1.did(v1.after().tensor_tensor_scan(flat(run), s.chunk_start, flat(logw), 0.0, ALU.mult, ALU.add))
    part = lambda n: s.AR[:, :, :, n * P:(n + 1) * P].rearrange("p k t s -> p (k t) s")
    tiled = lambda t: t.rearrange("p k (t s) -> p (k t) s", t=TT)
    m = c.tt(work, run, logw, ALU.subtract, c.tensor.last)
    m = c.act(work, work, ACT.Exp, m)
    yield
    m = c.stt(part(0), tiled(kk), -1.0, tiled(work), ALU.mult, ALU.mult, m)
    m = c.act(work, run, ACT.Exp, m)
    yield
    m = c.tt(part(1), tiled(r), tiled(work), ALU.mult, m)
    chunks = lambda t: t.rearrange("p k (n c) -> p (k n) c", c=C)
    m = c.copy(s.chunk_decay[:, :, :].rearrange("p k n -> p (k n)"), chunks(work)[:, :, C - 1])
    m = c.act(work, run, ACT.Exp, m, scale=-1.0)
    yield
    c.tt(kk, kk, icl, ALU.mult)
    m = c.tt(s.b, kk, work, ALU.mult, m)
    m = c.tt(s.k, k_, work, ALU.mult)
    m = c.tt(chunks(work), chunks(run)[:, :, C - 1:C].to_broadcast([P, 4 * N_CHUNK, C]), chunks(run), ALU.subtract)
    m = c.act(work, work, ACT.Exp, m)
    yield
    m = c.tt(s.bend, kk, work, ALU.mult, m)
    m = c.tt(s.kend, k_, work, ALU.mult)


def rwkv_scan(c, s, yT):
    nc, I = c.nc, c.identity
    eight = c.scalar, c.vector
    state = c.carve(4, 64)
    m = c.fill(state, 0.0)
    for t in range(TT):
        rows = {}
        inner = c.mem.at
        W = c.carve(HEADS, P)
        for n, name in enumerate(("a", "bend", "kend", "v")):
            src = {"bend": s.bend, "kend": s.kend, "v": s.v_cols}.get(name)
            c.tensor.wait(c.vector.last)
            i, bank = c.bank()
            for k in range(4):
                part = s.AR[:, k, t, 0:P] if name == "a" else src[:, k, t * P:(t + 1) * P]
                ins = nc.tensor.transpose(bank[:, k * P:(k + 1) * P], part, I)
            m = c.tensor.did(ins)
            heads = bank[:, :].rearrange("p (h e) -> p h e", h=HEADS)
            rows[name] = W[:, :, 0:64] if name == "a" else c.carve(HEADS, 64)
            c.read(i, c.copy(rows[name], heads, m, q=eight[n % 2]))
            yield
        G, N, PP = c.carve(HEADS, 4 * P), c.carve(HEADS, P), c.carve(HEADS, P)
        N1, P2, N2 = c.carve(HEADS, P), c.carve(HEADS, P), c.carve(HEADS, P)
        Z = c.carve(HEADS, P)
        for h in range(HEADS):
            k, r = h // 2, 64 * (h % 2)
            hs = slice(r, r + 64)
            tok = slice(t * P, (t + 1) * P)
            i, bank = c.bank()
            c.mm(bank[:, 0:2 * P], s.b[hs, k, tok], s.AR[hs, k, t, :])
            m = c.tensor.did(c.mm(bank[:, 2 * P:4 * P], s.k[hs, k, tok], s.AR[hs, k, t, :]))
            m = c.tt(G[:, h, :].rearrange("p (a b s) -> p a (b s)", a=2, b=2),
                     bank[:, :].rearrange("p (a s) -> p a s", a=2),
                     s.pair[:, 0:2, :].rearrange("p b s -> p (b s)").unsqueeze(1).to_broadcast([P, 2, 2 * P]),
                     ALU.mult, m)
            c.read(i, m)
            i, bank = c.bank()
            m = c.tensor.did(c.mm(bank[:, 0:P], s.AR[hs, k, t, 0:P], s.b[hs, k, tok]))
            m = c.tt(N1[:, h, :], bank[:, 0:P], s.pair[:, 2, :], ALU.mult, m)
            c.read(i, m)
            if h % 2:
                yield
        bc8 = lambda kind: s.pair[:, kind:kind + 1, :].to_broadcast([P, HEADS, P])
        m = c.tt(PP, G[:, :, 0:P], bc8(3), ALU.mult)
        m = c.tt(N, N1, bc8(4), ALU.mult)
        m = c.tt(Z, PP, I.unsqueeze(1).to_broadcast([P, HEADS, P]), ALU.add)
        m = c.tt(N1, N1, N, ALU.subtract)
        yield

        def per_head(out, left, right, combine=None, marks=()):
            c.tensor.wait(c.vector.last, c.scalar.last, *marks)
            done = []
            for h0 in range(0, HEADS, 4):
                i, bank = c.bank()
                for h in range(h0, h0 + 4):
                    ins = c.mm(bank[:, (h - h0) * P:(h - h0 + 1) * P], left[:, h, :], right[:, h, :])
                m = c.tensor.did(ins)
                src = bank[:, :].rearrange("p (h s) -> p h s", h=4)
                if combine is None:
                    d = c.copy(out[:, h0:h0 + 4, :], src, m, q=c.scalar)
                else:
                    d = c.tt(out[:, h0:h0 + 4, :], src, combine[:, h0:h0 + 4, :], ALU.add, m)
                c.read(i, d)
                done.append(d)
            return done
        p, n, p_next, n_next = PP, N, P2, N2
        for level in range(3):
            per_head(n_next, p, n)
            yield
            if level < 2:
                per_head(p_next, n, p)
            per_head(Z, n_next, Z, Z)
            yield
            p, n, p_next, n_next = p_next, n_next, p, n
        X, M = P2, N2
        c.tensor.wait(c.vector.last)
        for h0 in range(0, HEADS, 4):
            i, bank = c.bank()
            for h in range(h0, h0 + 4):
                ins = nc.tensor.transpose(bank[:, (h - h0) * P:(h - h0 + 1) * P], Z[:, h, :], I)
            m = c.tensor.did(ins)
            c.read(i, c.copy(X[:, h0:h0 + 4, :], bank[:, :].rearrange("p (h s) -> p h s", h=4), m, q=c.scalar))
        yield
        per_head(M, N1, Z)
        yield
        per_head(Z, X, M, Z)
        yield
        AK = G[:, :, 2 * P:3 * P]
        c.tensor.wait(c.vector.last)
        i, bank = c.bank()
        for h in range(HEADS):
            ins = c.mm(bank[:, h * 64:(h + 1) * 64], AK[:, h, :], rows["v"][:, h, :])
        m = c.tensor.did(ins)
        c.read(i, c.copy(W[:, :, 64:P], bank[:, :].rearrange("p (h e) -> p h e", h=HEADS), m))
        yield
        G12 = PP
        per_head(G12, Z, W)
        yield
        c.tensor.wait(c.scalar.last, c.vector.last)
        R2, Y0 = N1[:, 4:8, :], P2[:, 4:8, :]
        i, bank = c.bank()
        for h in range(HEADS):
            o = bank[64 * (h % 2):64 * (h % 2) + 64, (h // 2) * P:(h // 2 + 1) * P]
            ins = c.mm(o, G12[:, h, 0:64], G[:, h, P:2 * P])
        m = c.tensor.did(ins)
        m = c.tt(R2, bank[:, :].rearrange("p (k s) -> p k s", k=4), s.AR[:, :, t, P:2 * P], ALU.add, m)
        c.read(i, m)
        i, bank = c.bank()
        for h in range(HEADS):
            o = bank[64 * (h % 2):64 * (h % 2) + 64, (h // 2) * P:(h // 2 + 1) * P]
            c.mm(o, G12[:, h, 64:P], G[:, h, P:2 * P], True, False)
            ins = c.mm(o, rows["v"][:, h, :], G[:, h, 3 * P:4 * P], False, True)
        m = c.tensor.did(ins)
        c.read(i, c.copy(Y0, bank[:, :].rearrange("p (k s) -> p k s", k=4), m))
        yield
        n_here = P // C
        gain, states = c.carve(n_here, 4 * 64), c.carve(n_here, 4 * 64)
        step = N1, P2, N2, Z
        for n in range(n_here):
            ts_ = slice(n * C, (n + 1) * C)
            decay = s.chunk_decay[:, :, t * n_here + n]
            m = c.tt(step[n][:, 0:4, :], I.unsqueeze(1).to_broadcast([P, 4, P]),
                     decay.unsqueeze(2).to_broadcast([P, 4, P]), ALU.mult, c.tensor.last)
            i, bank = c.bank()
            for h in range(HEADS):
                r, k = 64 * (h % 2), h // 2
                ins = c.mm(bank[r:r + 64, k * P + r:k * P + r + 64], G12[ts_, h, 0:64], rows["bend"][ts_, h, :])
            m = c.tensor.did(ins)
            for r in (0, 64):
                d = step[n][r:r + 64, 0:4, r:r + 64]
                b = bank[r:r + 64, :].rearrange("p (k s) -> p k s", k=4)[:, :, r:r + 64]
                m1 = c.tt(d, b, d, ALU.add, m)
            c.read(i, m1)
            i, bank = c.bank()
            for h in range(HEADS):
                r, k = 64 * (h % 2), h // 2
                o = bank[r:r + 64, k * 64:(k + 1) * 64]
                c.mm(o, rows["bend"][ts_, h, :], G12[ts_, h, 64:P], True, False)
                ins = c.mm(o, rows["kend"][ts_, h, :], rows["v"][ts_, h, :], False, True)
            m = c.tensor.did(ins)
            c.read(i, c.copy(gain[:, n, :], bank[:, 0:256], m, q=c.scalar))
            yield
        current = state[:, :, :].rearrange("p k e -> p (k e)")
        for n in range(n_here):
            m = c.copy(states[:, n, :], current, c.scalar.last)
            c.tensor.wait(m)
            i, bank = c.bank()
            for k in range(4):
                ins = c.mm(bank[:, k * 64:(k + 1) * 64], step[n][:, k, :], states[:, n, k * 64:(k + 1) * 64])
            m = c.tensor.did(ins)
            m = c.tt(current, bank[:, 0:256], gain[:, n, :], ALU.add, m)
            c.read(i, m)
            yield
        pair_banks = [c.bank() for _ in range(2)]
        for n in range(n_here):
            for h in range(HEADS):
                r, k = 64 * (h % 2), h // 2
                o = pair_banks[h % 2][1][r:r + 64, k * P + n * C:k * P + (n + 1) * C]
                ins = c.mm(o, states[r:r + 64, n, k * 64:(k + 1) * 64], R2[r:r + 64, k, n * C:(n + 1) * C])
        m = c.tensor.did(ins)
        for e, (i, bank) in enumerate(pair_banks):
            r = 64 * e
            c.read(i, c.tt(yT[r:r + 64, :, t * P:(t + 1) * P], bank[r:r + 64, :].rearrange("p (k s) -> p k s", k=4),
                           Y0[r:r + 64, :, :], ALU.add, m))
        c.mem.at = inner
        yield
        c.vector.wait(c.tensor.last)
        c.scalar.wait(c.tensor.last, c.vector.last)


def rwkv_output(c, s, yT):
    col = lambda name, k: s.v[name][:, k:k + 1]
    work = c.carve(4, SEQ)

    def head_mean(src, out, sub):
        c.tensor.wait(c.vector.last)
        for k in range(0, 4, 2):
            i, bank = c.bank()
            m = c.tensor.did(c.mm(bank, c.head_sum, src[:, k:k + 2, :].rearrange("p k s -> p (k s)")))
            b = bank[:, :].rearrange("p (k s) -> p k s", k=2)
            if sub is not None:
                m = c.stt(out[:, k:k + 2, :], b, -1.0 / 64, sub[:, k:k + 2, :], ALU.mult, ALU.add, m)
            else:
                m = c.ts(out[:, k:k + 2, :], b, 1.0 / 64, 64e-5, ALU.mult, ALU.add, m)
            c.read(i, m)
        return m
    head_mean(yT, yT, yT)
    yield
    c.tt(work, yT, yT, ALU.mult)
    m = head_mean(work, work, None)
    yield
    m = c.act(work, work, ACT.Sqrt, m)
    m = c.recip(work, work, m)
    yield
    c.tt(yT, yT, work, ALU.mult)
    for k in range(4):
        m = c.ts(yT[:, k, :], yT[:, k, :], col("rwkv_ln_w_2", k), col("rwkv_ln_b_2", k), ALU.mult, ALU.add)
    c.tt(yT, yT, s.bonus, ALU.add)
    c.tt(yT, yT, s.rwkv_gate, ALU.mult)


def add_branch(c, s, gates, yT, pieces):
    tmp = c.carve(2, SEQ)
    c.tensor.wait(c.vector.last, c.scalar.last)
    first, s.merged_begun = not s.merged_begun, True
    for half in range(2):
        w = c.weights(c.tensor, pieces[half])
        products = [c.product_cols(yT, w[:, :, k * P:(k + 2) * P], range(4)) for k in (0, 2)]
        c.release(products[1][2])
        for k, (i, src, m) in zip((0, 2), products):
            f = 4 * half + k
            g, total = gates[:, f:f + 2, :], s.merged[:, f:f + 2, :]
            if first:
                d = s.merged_done = c.tt(total, src, g, ALU.mult, m)
            else:
                d = c.tt(tmp, src, g, ALU.mult, m)
                s.merged_done = c.tt(total, total, tmp, ALU.add, d, s.merged_done)
            c.read(i, d)
        yield


def moba(c, s, qkT, v_rows, yT, h0):
    n_heads = 4
    scores, total, negmax = c.carve(n_heads, SEQ), c.carve(n_heads), c.carve(n_heads)
    pT = c.carve(n_heads, 2, SEQ)
    pv_done = None
    for t in range(TT):
        keys = P * (t + 1)
        k = h0 // 2
        for e in range(2):
            i, bank = c.bank()
            hs = slice(64 * e, 64 * e + 64)
            for j in range(2):
                ins = c.mm(bank[:, j * SEQ:j * SEQ + keys], qkT[hs, k + j, t * P:(t + 1) * P], qkT[hs, 4 + k + j, 0:keys])
            m = c.tensor.did(ins)
            for j in range(2):
                h = 2 * (k + j) + e
                part = scores[:, h - h0, 0:keys]
                m1 = c.ts(part, s.distance[:, t, 0:keys], -2.0 ** -(h + 1), None, ALU.mult, None, m, pv_done)
                m1 = c.stt(part, bank[:, j * SEQ:j * SEQ + keys], 0.125, part, ALU.mult, ALU.add)
            c.read(i, m1)
        yield
        m = c.softmax_exp(scores, negmax, total, n_heads, keys, m1)
        yield
        sc = scores[:, :, 0:keys]
        m = c.tt(sc, sc, total[:, 0:n_heads].unsqueeze(2).to_broadcast([P, n_heads, keys]), ALU.mult, m)
        done = c.transpose_maps(pT, scores, n_heads, t, c.identity, m)
        pv_done = c.tensor.last
        yield
        c.tensor.wait(*done)
    heads_out(c, yT, h0 // 2, pT, v_rows[:, :, h0 * 64:], n_heads)
    yield
    c.vector.wait(c.tensor.last)
    c.scalar.wait(c.tensor.last)


def s5(c, a, s, u, yT, glu_pieces):
    nc = c.nc
    G16 = 16
    dt, mag, th, turn, sn, cs = (c.carve(G16) for _ in range(6))
    lr, li, den, cr, ci, t1 = (c.carve(G16) for _ in range(6))
    bT, cT = [c.carve(4, P) for _ in range(2)], [c.carve(4, P) for _ in range(2)]
    later = c.mem.at
    b_re, b_im, c_re, c_im = c.carve(16, 16), c.carve(16, 16), c.carve(4, 64), c.carve(4, 64)
    loads = Loads(nc, "ssm_loads")
    for dst, name in ((b_re, "ssm_b_re_2"), (b_im, "ssm_b_im_2")):
        loads.load(nc.scalar, dst, a[name].rearrange("a (i e) q h -> (a e q) i h", e=2))
    for dst, name in ((c_re, "ssm_c_re_2"), (c_im, "ssm_c_im_2")):
        loads.load(nc.scalar, dst, a[name].rearrange("a (k g) h q -> (a g h) k q", g=8))
    re, im = s.v["ssm_a_re_2"], s.v["ssm_a_im_2"]
    m = c.act(dt, s.log_dt, ACT.Exp, c.vector.last)
    m = c.tt(mag, re, dt, ALU.mult, m)
    m = c.act(mag, mag, ACT.Exp, m)
    m = c.tt(th, im, dt, ALU.mult, m)
    m = c.sincos(sn, cs, th, turn, m)
    yield
    c.vector.wait(c.scalar.last, loads.last, c.gpsimd.last)
    c.tt(lr, mag, cs, ALU.mult)
    c.tt(li, mag, sn, ALU.mult)
    c.ts(lr, lr, -1.0, None, ALU.add, None)
    c.tt(den, re, re, ALU.mult)
    c.tt(t1, im, im, ALU.mult)
    c.tt(den, den, t1, ALU.add)
    c.recip(den, den)
    c.tt(cr, lr, re, ALU.mult)
    c.tt(t1, li, im, ALU.mult)
    c.tt(cr, cr, t1, ALU.add)
    c.tt(cr, cr, den, ALU.mult)
    c.tt(ci, li, re, ALU.mult)
    c.tt(t1, lr, im, ALU.mult)
    c.tt(ci, ci, t1, ALU.subtract)
    c.tt(ci, ci, den, ALU.mult)
    bb = [c.carve(G16, 32) for _ in range(2)]
    t2 = c.carve(G16, 16)
    for part in bb:
        c.fill(part, 0.0)
    for e in range(2):
        hs = slice(64 * e, 64 * e + 64)
        n = slice(16 * e, 16 * e + 16)
        crb, cib = (x[hs, :].unsqueeze(2).to_broadcast([64, G16, 16]) for x in (cr, ci))
        bre, bim = b_re[hs, :, :], b_im[hs, :, :]
        c.tt(bb[0][hs, :, n], crb, bre, ALU.mult)
        c.tt(t2[hs, :, :], cib, bim, ALU.mult)
        c.tt(bb[0][hs, :, n], bb[0][hs, :, n], t2[hs, :, :], ALU.subtract)
        c.tt(bb[1][hs, :, n], crb, bim, ALU.mult)
        c.tt(t2[hs, :, :], cib, bre, ALU.mult)
        c.tt(bb[1][hs, :, n], bb[1][hs, :, n], t2[hs, :, :], ALU.add)
    cc = [c.carve(4, P) for _ in range(2)]
    for dst, src, sign in ((cc[0], c_re, 1.0), (cc[1], c_im, -1.0)):
        for e in range(2):
            m = c.ts(dst[:, :, 64 * e:64 * e + 64], src, s.group_odd[:, e:e + 1], sign, ALU.mult, ALU.mult)
    yield
    c.tensor.wait(m)
    done = []
    for src, dst in ((bb[0], bT[0]), (bb[1], bT[1]), (cc[0], cT[0]), (cc[1], cT[1])):
        flat = src.rearrange("p a b -> p (a b)")
        i, bank = c.bank()
        for k in range(4):
            ins = nc.tensor.transpose(bank[:, k * P:(k + 1) * P], flat[:, k * P:(k + 1) * P], c.identity)
        m = c.tensor.did(ins)
        d = c.copy(dst, bank[:, :].rearrange("p (k s) -> p k s", k=4), m, q=c.scalar)
        c.read(i, d)
        done.append(d)
    c.tensor.wait(*done)
    yield
    c.vector.wait(c.tensor.last)
    c.scalar.wait(c.tensor.last, c.vector.last)
    c.mem.at = later
    cos, sin, turns, angle, br, bi, gr, gi = (c.carve(2, SEQ) for _ in range(8))
    c.ts(th, th, 1 / TWO_PI, None, ALU.mult, None)
    for part in range(8):
        k, i0, r0 = part // 2, 2 * part, 64 * (part % 2)
        for j in range(2):
            m = c.ts(angle[:, j, :], s.time, th[:, i0 + j:i0 + j + 1], None, ALU.mult, None, c.scalar.last)
        m = c.ts(turns, angle, ROUND, -ROUND, ALU.add, ALU.add, m)
        m = c.tt(angle, angle, turns, ALU.subtract, m)
        m = c.act(sin, angle, ACT.Sin, m, scale=6.283185)
        m = c.act(cos, angle, ACT.Sin, m, scale=3.1415925)
        m = c.act(cos, cos, ACT.Square, m)
        m = c.act(cos, cos, ACT.Identity, m, scale=-2.0, bias=c.ones[:, 0:1])
        yield
        c.vector.wait(c.scalar.last)
        for j in range(2):
            i, bank = c.bank()
            ch = slice(r0 + 32 * j, r0 + 32 * j + 32)
            c.mm(bank[:, 0:SEQ], bT[0][ch, k, :], u[ch, k, :])
            m = c.tensor.did(c.mm(bank[:, SEQ:2 * SEQ], bT[1][ch, k, :], u[ch, k, :]))
            c.tt(br[:, j, :], bank[:, 0:SEQ], cos[:, j, :], ALU.mult, m, c.tensor.last)
            c.tt(gi[:, j, :], bank[:, 0:SEQ], sin[:, j, :], ALU.mult)
            c.tt(bi[:, j, :], bank[:, SEQ:2 * SEQ], cos[:, j, :], ALU.mult)
            c.read(i, c.tt(gr[:, j, :], bank[:, SEQ:2 * SEQ], sin[:, j, :], ALU.mult))
        c.tt(br, br, gr, ALU.add)
        c.tt(bi, bi, gi, ALU.subtract)
        yield
        v = c.vector
        for j in range(2):
            keep = mag[:, i0 + j:i0 + j + 1].to_broadcast([P, SEQ])
            for src, dst in ((br, gr), (bi, gi)):
                m = v.did(v.after().tensor_tensor_scan(dst[:, j, :], keep, src[:, j, :], 0.0, ALU.mult, ALU.add))
        yield
        c.tt(br, cos, gr, ALU.mult)
        c.tt(bi, sin, gr, ALU.mult)
        c.tt(gr, sin, gi, ALU.mult)
        c.tt(gi, cos, gi, ALU.mult)
        c.tt(br, br, gr, ALU.subtract)
        m = c.tt(bi, bi, gi, ALU.add)
        c.tensor.wait(m)
        i, bank = c.bank()
        for j in range(2):
            ch = slice(r0 + 32 * j, r0 + 32 * j + 32)
            c.mm(bank[ch, 0:SEQ], cT[0][:, k, ch], br[:, j, :], True, False)
            ins = c.mm(bank[ch, 0:SEQ], cT[1][:, k, ch], bi[:, j, :], False, True)
        m = c.tensor.did(ins)
        ch = slice(r0, r0 + 64)
        m = c.stt(yT[ch, k, :], u[ch, k, :], s.v["ssm_d_2"][ch, k:k + 1], bank[ch, 0:SEQ], ALU.mult, ALU.add, m)
        c.read(i, m)
    m = c.act(yT, yT, ACT.Gelu_apprx_tanh, m)
    c.tensor.wait(m)
    c.mem.at = later
    glu = c.carve(4, SEQ), c.carve(4, SEQ)
    for half in range(2):
        w = c.weights(c.tensor, glu_pieces[half])
        products = [c.product_cols(yT, w[:, :, k * P:(k + 2) * P], range(4)) for k in (0, 2)]
        c.release(products[1][2])
        for k, (i, src, m) in zip((0, 2), products):
            for j in range(2):
                bias = s.v["ssm_glu_b_2"][:, 4 * half + k + j:4 * half + k + j + 1]
                d = c.act(glu[half][:, k + j, :], src[:, j, :], ACT.Sigmoid if half else ACT.Identity, m, bias=bias)
            c.read(i, d)
        yield
    c.tt(yT, glu[0], glu[1], ALU.mult, d, c.tensor.last)


def layer_norm(c, out, x, w, b, small, junk, *marks):
    for t in range(TT):
        m = c.reduce(small[:, t:t + 1], x[:, t, :], ALU.add, *marks)
        m = c.ts(small[:, t:t + 1], small[:, t:t + 1], 1.0 / D, None, ALU.mult, None)
        m = c.ts(x[:, t, :], x[:, t, :], small[:, t:t + 1], None, ALU.subtract, None)
        m = c.sumsq(small[:, 2 + t:3 + t], x[:, t, :], x[:, t, :], junk)
    m = c.rsqrt(small[:, 2:4], small[:, 2:4], D, 1e-5, m)
    for t in range(TT):
        m = c.stt(x[:, t, :], x[:, t, :], small[:, 2 + t:3 + t], w, ALU.mult, ALU.mult, m)
        m = c.tt(out[:, t, :], x[:, t, :], b, ALU.add, m)
    return m


def route(c, s, x1T):
    nc = c.nc
    i, bank = c.bank()
    for t in range(TT):
        for k in range(KT):
            ins = c.mm(bank[:, t * 36:t * 36 + 36], x1T[:, k, t * P:(t + 1) * P], s.w_router[:, k, :], k == 0, k == KT - 1)
    m = c.tensor.did(ins)
    logits = c.carve(TT, 36)
    m = c.tt(logits, bank[:, 0:72].rearrange("p (t n) -> p t n", t=TT), s.b_router.unsqueeze(1).to_broadcast([P, TT, 36]),
             ALU.add, m)
    c.read(i, m)
    top, pick, work, hot = c.carve(TT), c.carve(TT), c.carve(TT, 32), [c.carve(TT, 32) for _ in range(2)]
    group, p_group, exps = c.carve(TT, 4), c.carve(TT), c.carve(TT, 4)
    wide = lambda t, n: t.unsqueeze(2).to_broadcast([P, TT, n])

    def first_of(out, values, best, n):
        index = s.time[:, 0:n].unsqueeze(1).to_broadcast([P, TT, n])
        w = work[:, :, 0:n]
        c.tt(w, values, wide(best, n), ALU.is_lt)
        c.stt(w, w, 1000.0, index, ALU.mult, ALU.add)
        c.reduce(pick, w, ALU.min)
        return c.tt(out, index, wide(pick, n), ALU.is_equal)
    g = logits[:, :, 0:4]
    c.reduce(top, g, ALU.max)
    first_of(group, g, top, 4)
    m = c.tt(exps, g, wide(top, 4), ALU.subtract)
    m = c.act(exps, exps, ACT.Exp, m)
    m = c.reduce(p_group, exps, ALU.add, m)
    c.recip(p_group, p_group)
    e = c.carve(TT, 32)
    outside = c.carve(TT, 4)
    c.ts(outside, group, -1.0, 3e38, ALU.add, ALU.mult)
    for t in range(TT):
        inside = group[:, t, :].unsqueeze(2).to_broadcast([P, 4, 8])
        ev, lv = (v.rearrange("p (g n) -> p g n", g=4) for v in (e[:, t, :], logits[:, t, 4:36]))
        c.tt(ev, lv, inside, ALU.mult)
        c.tt(ev, ev, outside[:, t, :].unsqueeze(2).to_broadcast([P, 4, 8]), ALU.add)
    second = c.carve(TT)
    c.reduce(top, e, ALU.max)
    first_of(hot[0], e, top, 32)
    c.stt(e, hot[0], -3.3e38, e, ALU.mult, ALU.add)
    c.ts(e, e, -3.3e38, None, ALU.max, None)
    c.reduce(second, e, ALU.max)
    first_of(hot[1], e, second, 32)
    m = c.tt(second, second, top, ALU.subtract)
    m = c.act(second, second, ACT.Exp, m)
    c.ts(top, second, 1.0, None, ALU.add, None, m)
    c.recip(top, top)
    c.tt(top, top, p_group, ALU.mult)
    c.tt(second, second, top, ALU.mult)
    c.tt(hot[0], hot[0], wide(top, 32), ALU.mult)
    c.tt(hot[1], hot[1], wide(second, 32), ALU.mult)
    m = c.tt(hot[0], hot[0], hot[1], ALU.add)
    c.tensor.wait(m)
    i, bank = c.bank()
    for t in range(TT):
        ins = nc.tensor.transpose(bank[0:32, t * P:(t + 1) * P], hot[0][:, t, :], c.identity)
    m = c.tensor.did(ins)
    wT = c.carve(SEQ)
    m = c.copy(wT[0:32, :], bank[0:32, 0:SEQ], m)
    c.read(i, m)
    spread = s.weight
    some = c.carve(8, SEQ)
    for e0 in range(0, EXPERTS, 8):
        m = c.tt(some[0:32], wT[0:32].unsqueeze(1).to_broadcast([32, 8, SEQ]),
                 c.identity[0:32, e0:e0 + 8].unsqueeze(2).to_broadcast([32, 8, SEQ]), ALU.mult, c.tensor.last)
        c.tensor.wait(m)
        for n in range(0, 8, 2):
            i, bank = c.bank()
            m = c.tensor.did(c.mm(bank, c.ones[0:32, :], some[0:32, n:n + 2, :].rearrange("p a s -> p (a s)")))
            c.read(i, c.copy(spread[:, e0 + n:e0 + n + 2, :], bank[:, :].rearrange("p (a s) -> p a s", a=2), m, q=c.scalar))


EXPERT_STEP = {"tensor": ("gate", "up", "down"),
               "scalar": ("up_hi", "down_hi", "silu", "gate_hi", "hidden_hi"),
               "vector": ("up_lo", "down_lo", "weighted", "gate_lo", "hidden", "hidden_lo")}


class Experts:

    def __init__(self, c, a):
        self.c, nc = c, c.nc
        self.sources = {kind: a[f"expert_w_{kind}_2"].rearrange("a e (k p) n -> (a e) p k n", p=P)
                        for kind in ("gate", "up", "down")}
        down = c.carve(2, SLOT)
        self.raw = {"gate": [k_tiles(KT)(c.ring[e]) for e in range(2)],
                    "up": [k_tiles(KT)(c.ring[2 + e]) for e in range(2)],
                    "down": [k_tiles(2, D)(down[:, e, :]) for e in range(2)]}
        self.full = {kind: [nc.alloc_semaphore(f"{kind}_full{e}") for e in range(2)] for kind in self.raw}
        c.sync.wait(*(mark for readers in c.ring_free for mark in readers))
        for kind, e in (("gate", 0), ("up", 0), ("gate", 1), ("down", 0), ("up", 1), ("down", 1)):
            self.load(kind, e, e)

    def load(self, kind, e, parity):
        source = self.sources[kind]
        source = source[e] if isinstance(e, int) else source[bass.ds(e, 1)].rearrange("a p k n -> p (a k) n")
        self.c.nc.sync.dma_start(self.raw[kind][parity], source).then_inc(self.full[kind][parity], 16)

    def at(self, queue, name, s):
        names = EXPERT_STEP[queue]
        place = names.index(name)
        skipped = sum(1 for other in self.skipped[queue] if other < (s, place)) if isinstance(s, int) else 0
        base = self.base[queue] + place + 1 - skipped
        return self.queues[queue].sem, s * len(names) + base

    def did(self, instruction, queue):
        instruction.then_inc(self.queues[queue].sem, 1)

    def split(self, kind, n, parity, ahead, known):
        s, e, act, dve = n * 2 + parity, (parity + ahead) % 2, self.c.nc.scalar, self.c.nc.vector
        if known is not None and known + ahead >= EXPERTS:
            for queue, part in (("scalar", "_hi"), ("vector", "_lo")):
                self.skipped[queue].append((known, EXPERT_STEP[queue].index(kind + part)))
            return
        (hi, lo), raw = self.pairs[kind], self.raw[kind][e]
        act.wait_ge(self.full[kind][e], (n + (parity + ahead) // 2) * 16 + 16)
        if known != -1:
            act.wait_ge(*self.at("tensor", kind, s - 1 if kind in ("up", "down") else s))
        elif ahead == 2:
            act.wait_ge(*self.at("tensor", kind, s))
        self.did(act.activation(hi, raw, ACT.Copy), "scalar")
        place = {"gate": "up", "up": "down"}[kind] if known == -1 and ahead == 1 else kind
        dve.wait_ge(*self.at("scalar", place + "_hi", s))
        self.did(dve.tensor_tensor(lo, raw, hi.bitcast(F32), ALU.subtract), "vector")
        if known is None or known + ahead + 2 < EXPERTS:
            self.c.nc.sync.wait_ge(*self.at("vector", place + "_lo", s))
            self.load(kind, s + (ahead + 2), e)

    def step(self, n, parity, known=None):
        nc, s, at = self.c.nc, n * 2 + parity, self.at
        pe, act, dve, e = nc.tensor, nc.scalar, nc.vector, 1 - parity
        exists = known is None or known + 1 < EXPERTS
        gate_bank, up_bank = (bank.rearrange("p (j s) -> p j s", s=SEQ) for bank in self.c.banks[4:6])
        hidden, raw, silu = self.hidden[e], self.hidden_raw, self.silu
        if known == -1:
            self.split("gate", n, parity, 1, known)
            self.split("up", n, parity, 1, known)
        else:
            self.split("up", n, parity, 1, known)
            self.split("down", n, parity, 0, known)
        if exists:
            for bank, kind in ((gate_bank, "gate"), (up_bank, "up")):
                if known == -1:
                    pe.wait_ge(*at("vector", {"gate": "up_lo", "up": "down_lo"}[kind], s))
                elif kind == "gate":
                    pe.wait_ge(*at("vector", "gate_lo", s - 1))
                    pe.wait_ge(*at("scalar", "silu", s - 1))
                else:
                    pe.wait_ge(*at("vector", "up_lo", s))
                    pe.wait_ge(*at("vector", "hidden", s - 1))
                for j in range(2):
                    for k in range(KT):
                        ins = self.c.mm_split(bank[:, j, :], [v[:, k, j * P:(j + 1) * P] for v in self.pairs[kind]],
                                              [v[:, k, :] for v in self.x_pair], k == 0, k == KT - 1)
                self.did(ins, "tensor")
            weight = self.weight[:, known + 1:known + 2, :] if known is not None else self.weight[:, bass.ds(s + 1, 1), :]
            act.wait_ge(*at("tensor", "gate", s))
            if known != -1:
                act.wait_ge(*at("vector", "hidden", s - 1))
            self.did(act.activation(silu, gate_bank, ACT.Silu), "scalar")
            dve.wait_ge(*at("scalar", "silu", s))
            self.did(dve.tensor_tensor(silu, silu, weight.to_broadcast([P, 2, SEQ]), ALU.mult), "vector")
            self.split("gate", n, parity, 2, known)
            dve.wait_ge(*at("tensor", "up", s))
            dve.wait_ge(*at("vector", "weighted", s))
            self.did(dve.tensor_tensor(raw, up_bank, silu, ALU.mult), "vector")
            act.wait_ge(*at("vector", "hidden", s))
            if known != -1:
                act.wait_ge(*at("tensor", "down", s - 1))
            self.did(act.activation(hidden[0], raw, ACT.Copy), "scalar")
            dve.wait_ge(*at("scalar", "hidden_hi", s))
            self.did(dve.tensor_tensor(hidden[1], raw, hidden[0].bitcast(F32), ALU.subtract), "vector")
        if known == -1:
            return
        pe.wait_ge(*at("vector", "down_lo", s))
        pe.wait_ge(*at("vector", "hidden_lo", s - 1))
        for t in range(TT):
            for half in range(2):
                for k in range(2):
                    out = self.c.banks[2 * t + half]
                    (h_hi, h_lo), (w_hi, w_lo) = self.hidden[parity], self.pairs["down"]
                    for h, w in ((h_hi, w_hi), (h_hi, w_lo), (h_lo, w_hi)):
                        ins = nc.tensor.matmul(out, h[:, k, t * P:(t + 1) * P], w[:, k, half * 512:(half + 1) * 512],
                                               start=False, stop=True, skip_group_check=True)
        self.did(ins, "tensor")

    def run(self, x1T, weight, y, done_with):
        c, nc = self.c, self.c.nc
        self.weight, rest = weight, c.mem
        c.mem = done_with
        self.x_pair, self.silu, zero = c.carve_split("x1", KT, SEQ), c.carve(2, SEQ), c.carve(P)
        c.mem = rest
        self.pairs = {kind: tuple((k_tiles(2, D) if kind == "down" else k_tiles(KT))(v)
                                  for v in c.carve_split(f"expert_{kind}", SLOT)) for kind in ("gate", "up", "down")}
        self.hidden = [c.carve_split(f"expert_hidden{e}", 2, SEQ) for e in range(2)]
        self.hidden_raw = c.carve(2, SEQ)
        c.meet()
        m = c.split(self.x_pair, x1T)
        m = c.fill(zero, 0.0, m)
        c.tensor.wait(m)
        self.queues = {"tensor": c.tensor, "scalar": c.scalar, "vector": c.vector}
        self.skipped = {name: [] for name in self.queues}
        self.base = {name: q.count + len(EXPERT_STEP[name]) for name, q in self.queues.items()}
        self.step(-1, 1, -1)
        for bank in c.banks[0:4]:
            ins = c.mm(bank, zero, weight[:, 0:2, :].rearrange("p a s -> p (a s)"))
        self.did(ins, "tensor")
        turns = (EXPERTS - 4) // 2
        with nc.Fori(0, turns) as n:
            self.step(n, 0)
            self.step(n, 1)
        for s in range(2 * turns, EXPERTS):
            self.step(s // 2, s % 2, s)
        self.skipped["tensor"] = [(EXPERTS - 1, place) for place in (0, 1)]
        c.tensor.count = self.at("tensor", "down", EXPERTS - 1)[1]
        c.scalar.count = self.at("scalar", "down_hi", EXPERTS - 1)[1]
        c.vector.count = self.at("vector", "down_lo", EXPERTS - 1)[1]
        for q in self.queues.values():
            q.own, q.seen = q.count, {}
        for n, bank in enumerate(c.banks[0:4]):
            t, half = n // 2, n % 2
            m = c.copy(y[:, t, half * 512:(half + 1) * 512], bank, c.tensor.last, q=(c.vector, c.scalar)[half])
        c.vector.wait(c.scalar.last)


def second_block(c, a, x):
    nc = c.nc
    s = State()
    c.mem = Region(c.arena, 0, ARENA)
    xT = c.hT
    done = c.columns_from_rows(xT, x, c.identity, KT, None)
    c.tensor.wait(*done)
    second_constants(c, s)
    vectors_2(c, a, s)
    s.merged, s.merged_begun = c.carve(8, SEQ), False
    pieces = second_pieces(a)
    c.vector.wait(c.gpsimd.last)

    def cols(dst, piece):
        w = c.weights(c.tensor, piece)
        i, src, m = c.product_cols(xT, w, range(KT))
        c.release(m)
        c.read(i, c.copy(dst, src, m, q=c.scalar))

    def branch_gates(gates, branch):
        for n in range(4):
            w = c.weights(c.tensor, pieces["gate"][branch][n])
            i, src, m = c.product_cols(xT, w, range(KT))
            c.release(m)
            for j in range(2):
                f = 8 * branch + 2 * n + j
                d = c.act(gates[:, 2 * n + j, :], src[:, j, :], ACT.Sigmoid, m, bias=s.v["gate_b_2"][:, f:f + 1])
            c.read(i, d)
            yield

    def hand_over():
        c.meet()
        yield

    def rwkv_branch():
        yT = c.carve(4, SEQ)
        yield from rwkv_input(c, a, s, cols, pieces["rwkv"])
        yield from hand_over()
        c.mem.at = s.rwkv_end
        yield from rwkv_scan(c, s, yT)
        yield from hand_over()
        c.mem.at = s.rwkv_end
        gates = c.carve(8, SEQ)
        yield from branch_gates(gates, 0)
        yield from rwkv_output(c, s, yT)
        yield from add_branch(c, s, gates, yT, pieces["up"][0])

    def moba_and_ssm_branches():
        start = c.mem.at
        yT, qkT, v_rows = c.carve(4, SEQ), c.carve(8, SEQ), c.carve(TT, 512)
        for n in range(4):
            cols(qkT[:, 2 * n:2 * n + 2, :], pieces["moba"][n])
            yield
        for n in range(2):
            w = c.weights(c.tensor, pieces["moba"][4 + n])
            i, src, m = c.product_rows(xT, w, range(KT))
            c.release(m)
            c.read(i, c.copy(v_rows[:, :, 256 * n:256 * n + 256], src, m, q=c.scalar))
            yield
        attention = c.mem.at
        for h0 in (0, 4):
            c.mem.at = attention
            c.tensor.wait(c.scalar.last)
            yield from moba(c, s, qkT, v_rows, yT, h0)
        c.mem.at = attention
        gates = c.carve(8, SEQ)
        yield from branch_gates(gates, 1)
        yield from add_branch(c, s, gates, yT, pieces["up"][1])
        yield from hand_over()
        c.mem.at = start
        yT, u = c.carve(4, SEQ), c.carve(4, SEQ)
        for n in range(2):
            cols(u[:, 2 * n:2 * n + 2, :], pieces["ssm"][n])
            yield
        yield from s5(c, a, s, u, yT, pieces["glu"])
        gates = c.carve(8, SEQ)
        yield from branch_gates(gates, 2)
        yield from add_branch(c, s, gates, yT, pieces["up"][2])

    tail, tail_start = c.mem.rest(), c.mem.at
    other = c.mem.rest(SSM_MOBA_FLOATS)
    c.weave((rwkv_branch(), c.mem), (moba_and_ssm_branches(), other), lead=7)
    c.meet()
    c.mem = tail
    y, small, junk = c.carve(TT, D), c.carve(4), c.carve(D)
    ln = [c.carve(D) for _ in range(4)]
    s.w_router, s.b_router = c.carve(KT, 36), c.carve(36)
    loads = Loads(nc, "last_loads")
    load = lambda dst, src: loads.load(nc.scalar, dst, src)
    for dst, name in zip(ln, ("ln1_w_2", "ln1_b_2", "ln2_w_2", "ln2_b_2")):
        load(dst, a[name].to_broadcast([P, D]))
    load(s.w_router[:, :, 0:4], a["router_group_w_2"].rearrange("a (k p) n -> p (a k) n", p=P))
    load(s.w_router[:, :, 4:36], a["router_expert_w_2"].rearrange("a (k p) n -> p (a k) n", p=P))
    load(s.b_router[:, 0:4], a["router_group_b_2"].to_broadcast([P, 4]))
    load(s.b_router[:, 4:36], a["router_expert_b_2"].to_broadcast([P, 32]))
    for _ in out_rows(c, s.merged, y, pieces["out"]):
        pass
    moe = Experts(c, a)
    for t in range(TT):
        m = c.stt(y[:, t, :], x[:, t, :], ALPHA, y[:, t, :], ALU.mult, ALU.add)
    m = layer_norm(c, x, y, ln[0], ln[1], small, junk, m, loads.last)
    x1T = c.hT
    c.tensor.wait(loads.last)
    done = c.columns_from_rows(x1T, x, c.identity, KT, None, m)
    c.tensor.wait(*done)
    s.weight = c.carve(EXPERTS, SEQ)
    after_weights = c.mem.at
    route(c, s, x1T)
    c.mem.at = after_weights
    moe.run(x1T, s.weight, y, Region(c.arena, 0, tail_start))
    for t in range(TT):
        m = c.stt(y[:, t, :], x[:, t, :], ALPHA, y[:, t, :], ALU.mult, ALU.add)
    layer_norm(c, x, y, ln[2], ln[3], small, junk, m)


def build(nc, a, out):
    c = Core(nc)
    x = c.keep("x", TT, D)
    c.hT = c.keep("hT", KT, SEQ)
    constants(c)
    c.tensor.wait(c.gpsimd.last)
    loads = Loads(nc, "x_load")
    loads.load(nc.sync, x, a["x"].rearrange("a (t p) d -> p (a t) d", p=P))
    c.vector.wait(loads.last)
    c.scalar.wait(loads.last)
    first_block(c, a, x)
    second_block(c, a, x)
    s_out = nc.alloc_semaphore("stored")
    c.sync.wait(c.vector.last)
    nc.sync.dma_start(out.rearrange("a (t p) d -> p (a t) d", p=P), x).then_inc(s_out, 16)
    nc.sync.wait_ge(s_out, 16)


INPUTS = [
    'x', 'c', 'positions', 'w_ada', 'b_ada', 'norm_g', 'w_in', 'diff_lambda', 'diff_subln_g',
    'mla_q_norm_g', 'w_uq', 'mla_kv_norm_g', 'w_ukv', 'conv_w', 'conv_b', 'dt_bias', 'a_log', 'd_skip',
    'ssm_norm_g', 'w_out', 'w_up', 'w_down', 'w_in_2', 'rwkv_mu_2', 'rwkv_w0_2', 'rwkv_w2_2',
    'rwkv_a0_2', 'rwkv_a2_2', 'rwkv_g2_2', 'rwkv_k_k_2', 'rwkv_k_a_2', 'rwkv_r_k_2', 'rwkv_ln_w_2',
    'rwkv_ln_b_2', 'ssm_a_re_2', 'ssm_a_im_2', 'ssm_b_re_2', 'ssm_b_im_2', 'ssm_c_re_2', 'ssm_c_im_2',
    'ssm_d_2', 'ssm_log_dt_2', 'ssm_glu_w_2', 'ssm_glu_b_2', 'w_up_rwkv_2', 'w_up_moba_2', 'w_up_ssm_2',
    'gate_b_2', 'w_out_2', 'ln1_w_2', 'ln1_b_2', 'router_group_w_2', 'router_group_b_2',
    'router_expert_w_2', 'router_expert_b_2', 'expert_w_gate_2', 'expert_w_up_2', 'expert_w_down_2',
    'ln2_w_2', 'ln2_b_2'
]


def kernel(**inputs):
    import numpy as _np
    import concourse.bacc as _bacc
    from concourse import mybir as _mybir
    from concourse.bass_utils import run_bass_kernel_spmd as _run

    nc = _bacc.Bacc("TRN2", target_bir_lowering=False, num_devices=1)
    arrays, handles = {}, {}
    for name in INPUTS:
        array = _np.ascontiguousarray(inputs[name])
        arrays[f"in_{name}"] = array
        handles[name] = nc.dram_tensor(f"in_{name}", array.shape, _mybir.dt.from_np(array.dtype),
                                       kind="ExternalInput").ap()
    out = nc.dram_tensor("out", (1, SEQ, D), F32, kind="ExternalOutput").ap()
    build(nc, handles, out)
    result = _run(nc, [arrays], core_ids=[0])
    return result.results[0]["out"]
```
